# Optimizing a Trainium2 kernel written in Bass

```python
import jax, jax.numpy as jnp
from jax import lax
import numpy as np

D_MODEL = 1024
BATCH = 1
SEQ = 256
DEPTH = 2

GRID_W = 64
NA_HEADS = 8
NA_HEAD_DIM = 64
NA_WIN_R = 8
NA_WIN_C = 16
NA_W = NA_HEADS * NA_HEAD_DIM
MLA_HEADS = 4
MLA_Q_RANK = 384
MLA_KV_RANK = 256
MLA_NOPE = 128
MLA_ROPE = 64
MLA_V = 128
MLA_QK = MLA_NOPE + MLA_ROPE
MLA_W = MLA_HEADS * MLA_V
GQA_HEADS = 8
GQA_KV_HEADS = 2
GQA_HEAD_DIM = 64
GQA_WINDOW = 128
GQA_Q_W = GQA_HEADS * GQA_HEAD_DIM
GQA_KV_W = GQA_KV_HEADS * GQA_HEAD_DIM
BLOCK = 128
N_BRANCH = 3
D_FF = 2816
CONV_W = 3
ROPE_THETA = 10000.0
EPS = 1e-6
NEG_INF = -1e30
IN_SPLITS = (3 * NA_W, MLA_Q_RANK, MLA_KV_RANK, MLA_ROPE, GQA_Q_W, 2 * GQA_KV_W, N_BRANCH * D_MODEL)
IN_W = 3 * NA_W + MLA_Q_RANK + MLA_KV_RANK + MLA_ROPE + GQA_Q_W + 2 * GQA_KV_W + N_BRANCH * D_MODEL


def rmsnorm(x, g):
    xf = x.astype(jnp.float32)
    y = xf * lax.rsqrt(jnp.mean(xf * xf, axis=-1, keepdims=True) + EPS)
    return (y * g.astype(jnp.float32)).astype(x.dtype)

def rope_tables(seq, dim):
    inv = 1.0 / (ROPE_THETA ** (jnp.arange(0, dim, 2, dtype=jnp.float32) / dim))
    ang = jnp.arange(seq, dtype=jnp.float32)[:, None] * inv[None, :]
    return jnp.cos(ang), jnp.sin(ang)

def apply_rope(x, cos, sin):
    x1, x2 = jnp.split(x, 2, axis=-1)
    c = cos[None, :, None, :].astype(x.dtype)
    s = sin[None, :, None, :].astype(x.dtype)
    return jnp.concatenate([x1 * c - x2 * s, x1 * s + x2 * c], axis=-1)

def neighbourhood_attention(q, k, v, rpb):
    B, S, H, hd = q.shape
    rows = S // GRID_W
    win_r = min(NA_WIN_R, rows)
    qg = q.reshape(B, rows, GRID_W, H, hd)
    kg = k.reshape(B, rows, GRID_W, H, hd)
    vg = v.reshape(B, rows, GRID_W, H, hd)
    col_q = jnp.arange(GRID_W)
    col_start = jnp.clip(col_q - NA_WIN_C // 2, 0, GRID_W - NA_WIN_C)
    col_idx = col_start[:, None] + jnp.arange(NA_WIN_C)[None, :]
    col_bias_idx = col_idx - col_q[:, None] + (NA_WIN_C - 1)
    scale = hd ** -0.5

    def one_row(r):
        r_start = jnp.clip(r - NA_WIN_R // 2, 0, rows - win_r)
        q_r = lax.dynamic_index_in_dim(qg, r, axis=1, keepdims=False)
        k_rows = lax.dynamic_slice_in_dim(kg, r_start, win_r, axis=1)
        v_rows = lax.dynamic_slice_in_dim(vg, r_start, win_r, axis=1)
        k_win = k_rows[:, :, col_idx]
        v_win = v_rows[:, :, col_idx]
        s = jnp.einsum('bqhd,brqchd->bhqrc', q_r, k_win,
                       preferred_element_type=jnp.float32) * scale
        row_bias_idx = r_start + jnp.arange(win_r) - r + (NA_WIN_R - 1)
        bias = rpb[:, row_bias_idx[None, :, None], col_bias_idx[:, None, :]]
        s = s + bias[None].astype(jnp.float32)
        p = jax.nn.softmax(s.reshape(B, H, GRID_W, win_r * NA_WIN_C), axis=-1)
        p = p.reshape(B, H, GRID_W, win_r, NA_WIN_C).astype(v.dtype)
        return jnp.einsum('bhqrc,brqchd->bqhd', p, v_win)

    out = lax.map(one_row, jnp.arange(rows))
    return out.transpose(1, 0, 2, 3, 4).reshape(B, S, H * hd)

def mla_attention(c_q, c_kv, k_rope, g_qa, g_kva, w_uq, w_ukv, cos, sin):
    B, S, _ = c_q.shape
    H = MLA_HEADS
    q = (rmsnorm(c_q, g_qa) @ w_uq).reshape(B, S, H, MLA_QK)
    q_nope = q[..., :MLA_NOPE]
    q_pe = apply_rope(q[..., MLA_NOPE:], cos, sin)
    kv = (rmsnorm(c_kv, g_kva) @ w_ukv).reshape(B, S, H, MLA_NOPE + MLA_V)
    k_nope = kv[..., :MLA_NOPE]
    v = kv[..., MLA_NOPE:]
    k_pe = apply_rope(k_rope[:, :, None, :], cos, sin)[:, :, 0, :]
    scale = MLA_QK ** -0.5
    nb = S // BLOCK
    qn_b = q_nope.reshape(B, nb, BLOCK, H, MLA_NOPE).transpose(1, 0, 2, 3, 4)
    qp_b = q_pe.reshape(B, nb, BLOCK, H, MLA_ROPE).transpose(1, 0, 2, 3, 4)

    def one_block(args):
        qn, qp = args
        s = (jnp.einsum('bqhd,bkhd->bhqk', qn, k_nope, preferred_element_type=jnp.float32)
             + jnp.einsum('bqhr,bkr->bhqk', qp, k_pe, preferred_element_type=jnp.float32)) * scale
        p = jax.nn.softmax(s, axis=-1).astype(v.dtype)
        return jnp.einsum('bhqk,bkhd->bqhd', p, v)

    o = lax.map(one_block, (qn_b, qp_b))
    return o.transpose(1, 0, 2, 3, 4).reshape(B, S, H * MLA_V)

def window_gqa_sink(q, k, v, sink, cos, sin):
    B, S, H, hd = q.shape
    KVH = k.shape[2]
    G = H // KVH
    q = apply_rope(q, cos, sin)
    k = apply_rope(k, cos, sin)
    nb = S // BLOCK
    qb = q.reshape(B, nb, BLOCK, KVH, G, hd)
    pad = ((0, 0), (BLOCK, BLOCK), (0, 0), (0, 0))
    kp = jnp.pad(k, pad).reshape(B, nb + 2, BLOCK, KVH, hd)
    vp = jnp.pad(v, pad).reshape(B, nb + 2, BLOCK, KVH, hd)
    kw = jnp.concatenate([kp[:, :-2], kp[:, 1:-1], kp[:, 2:]], axis=2)
    vw = jnp.concatenate([vp[:, :-2], vp[:, 1:-1], vp[:, 2:]], axis=2)
    scale = hd ** -0.5
    s = jnp.einsum('bnqkgd,bnjkd->bnkgqj', qb, kw,
                   preferred_element_type=jnp.float32) * scale
    blk = jnp.arange(nb)
    qpos = blk[:, None] * BLOCK + jnp.arange(BLOCK)[None, :]
    kpos = (blk[:, None] - 1) * BLOCK + jnp.arange(3 * BLOCK)[None, :]
    valid = ((kpos[:, None, :] >= 0) & (kpos[:, None, :] < S)
             & (jnp.abs(qpos[:, :, None] - kpos[:, None, :]) <= GQA_WINDOW))
    s = jnp.where(valid[None, :, None, None], s, NEG_INF)
    sink_b = jnp.broadcast_to(sink.astype(jnp.float32).reshape(KVH, G)[None, None, :, :, None, None],
                              s.shape[:-1] + (1,))
    p = jax.nn.softmax(jnp.concatenate([s, sink_b], axis=-1), axis=-1)[..., :-1]
    o = jnp.einsum('bnkgqj,bnjkd->bnqkgd', p.astype(v.dtype), vw)
    return o.reshape(B, S, H * hd)

def gated_parallel_mixer(h, w_in, b_gate, na_rpb, mla_qa_g, mla_kva_g, mla_w_uq, mla_w_ukv,
                         gqa_sink, w_br_na, w_br_mla, w_br_gqa, w_out, cos_mla, sin_mla, cos_gqa, sin_gqa):
    B, S, _ = h.shape
    z = h @ w_in
    offs = np.cumsum(IN_SPLITS)[:-1].tolist()
    z_na, c_q, c_kv, k_rope, z_gq, z_gkv, z_gate = jnp.split(z, offs, axis=-1)
    na_qkv = z_na.reshape(B, S, 3, NA_HEADS, NA_HEAD_DIM)
    y_na = neighbourhood_attention(na_qkv[:, :, 0], na_qkv[:, :, 1], na_qkv[:, :, 2], na_rpb)
    y_mla = mla_attention(c_q, c_kv, k_rope, mla_qa_g, mla_kva_g, mla_w_uq, mla_w_ukv, cos_mla, sin_mla)
    gkv = z_gkv.reshape(B, S, 2, GQA_KV_HEADS, GQA_HEAD_DIM)
    y_gqa = window_gqa_sink(z_gq.reshape(B, S, GQA_HEADS, GQA_HEAD_DIM), gkv[:, :, 0], gkv[:, :, 1],
                            gqa_sink, cos_gqa, sin_gqa)
    gates = jax.nn.sigmoid(z_gate + b_gate).reshape(B, S, N_BRANCH, D_MODEL)
    merged = (gates[:, :, 0] * (y_na @ w_br_na)
              + gates[:, :, 1] * (y_mla @ w_br_mla)
              + gates[:, :, 2] * (y_gqa @ w_br_gqa))
    return merged @ w_out

def conv_ffn(h, w_up, conv_w, conv_b, w_down):
    u = h @ w_up
    C = u.shape[-1]
    u = lax.conv_general_dilated(u, conv_w[:, None, :].astype(u.dtype), window_strides=(1,),
                                 padding=((CONV_W // 2, CONV_W // 2),),
                                 dimension_numbers=('NWC', 'WIO', 'NWC'),
                                 feature_group_count=C) + conv_b
    a, g = jnp.split(u, 2, axis=-1)
    return (jax.nn.gelu(g) * a) @ w_down

def first_inputs(seed: int = 0) -> dict:
    key = jax.random.key(seed)
    ks = jax.random.split(key, 24)
    f32 = jnp.float32

    def nrm(k, shape, scale):
        return jax.random.normal(k, shape, f32) * scale

    L = DEPTH
    return {
        "x": nrm(ks[0], (BATCH, SEQ, D_MODEL), 1.0),
        "norm1_g": 1.0 + nrm(ks[1], (L, D_MODEL), 0.05),
        "w_in": nrm(ks[2], (L, D_MODEL, IN_W), D_MODEL ** -0.5),
        "b_gate": nrm(ks[3], (L, N_BRANCH * D_MODEL), 0.02),
        "na_rpb": nrm(ks[4], (L, NA_HEADS, 2 * NA_WIN_R - 1, 2 * NA_WIN_C - 1), 0.1),
        "mla_qa_g": 1.0 + nrm(ks[5], (L, MLA_Q_RANK), 0.05),
        "mla_kva_g": 1.0 + nrm(ks[6], (L, MLA_KV_RANK), 0.05),
        "mla_w_uq": nrm(ks[7], (L, MLA_Q_RANK, MLA_HEADS * MLA_QK), MLA_Q_RANK ** -0.5),
        "mla_w_ukv": nrm(ks[8], (L, MLA_KV_RANK, MLA_HEADS * (MLA_NOPE + MLA_V)), MLA_KV_RANK ** -0.5),
        "gqa_sink": nrm(ks[9], (L, GQA_HEADS), 0.5),
        "w_br_na": nrm(ks[10], (L, NA_W, D_MODEL), NA_W ** -0.5),
        "w_br_mla": nrm(ks[11], (L, MLA_W, D_MODEL), MLA_W ** -0.5),
        "w_br_gqa": nrm(ks[12], (L, GQA_Q_W, D_MODEL), GQA_Q_W ** -0.5),
        "w_out": nrm(ks[13], (L, D_MODEL, D_MODEL), D_MODEL ** -0.5),
        "norm2_g": 1.0 + nrm(ks[14], (L, D_MODEL), 0.05),
        "w_up": nrm(ks[15], (L, D_MODEL, 2 * D_FF), D_MODEL ** -0.5),
        "conv_w": nrm(ks[16], (L, CONV_W, 2 * D_FF), CONV_W ** -0.5),
        "conv_b": nrm(ks[17], (L, 2 * D_FF), 0.02),
        "w_down": nrm(ks[18], (L, D_FF, D_MODEL), D_FF ** -0.5),
        "final_g": 1.0 + nrm(ks[19], (D_MODEL,), 0.05),
    }

def first_block(x, norm1_g, w_in, b_gate, na_rpb, mla_qa_g, mla_kva_g, mla_w_uq, mla_w_ukv,
              gqa_sink, w_br_na, w_br_mla, w_br_gqa, w_out, norm2_g, w_up, conv_w, conv_b,
              w_down, final_g):
    S = x.shape[1]
    cos_mla, sin_mla = rope_tables(S, MLA_ROPE)
    cos_gqa, sin_gqa = rope_tables(S, GQA_HEAD_DIM)
    for l in range(DEPTH):
        h = rmsnorm(x, norm1_g[l])
        x = x + gated_parallel_mixer(h, w_in[l], b_gate[l], na_rpb[l], mla_qa_g[l], mla_kva_g[l],
                                     mla_w_uq[l], mla_w_ukv[l], gqa_sink[l], w_br_na[l], w_br_mla[l],
                                     w_br_gqa[l], w_out[l], cos_mla, sin_mla, cos_gqa, sin_gqa)
        h = rmsnorm(x, norm2_g[l])
        x = x + conv_ffn(h, w_up[l], conv_w[l], conv_b[l], w_down[l])
    return rmsnorm(x, final_g)


CTX_LEN = 256
HEAD_DIM = 64
ATTN_DIM = D_MODEL // 2
N_Q_HEADS = ATTN_DIM // HEAD_DIM
N_KV_HEADS = N_Q_HEADS // 4
Q_PER_KV = N_Q_HEADS // N_KV_HEADS
KV_DIM = N_KV_HEADS * HEAD_DIM
GMLP_DIM = D_MODEL - ATTN_DIM
GMLP_GROUP_DIM = 128
N_GMLP_GROUPS = GMLP_DIM // GMLP_GROUP_DIM
CHUNK = 128
MIX_DIM = ATTN_DIM + GMLP_DIM
IN_DIM = ATTN_DIM + 2 * KV_DIM + 2 * GMLP_DIM
FF_DIM = 4 * D_MODEL
Q_BLOCK = 128
N_MOD = 6


def rmsnorm_2(x, g):
    xf = x.astype(jnp.float32)
    y = xf * lax.rsqrt(jnp.mean(xf * xf, axis=-1, keepdims=True) + EPS)
    return (y * g.astype(jnp.float32)).astype(x.dtype)

def group_layernorm(v, g):
    vf = v.astype(jnp.float32)
    mu = jnp.mean(vf, axis=-1, keepdims=True)
    var = jnp.mean(jnp.square(vf - mu), axis=-1, keepdims=True)
    return ((vf - mu) * lax.rsqrt(var + EPS) * g.astype(jnp.float32)).astype(v.dtype)

def modulation(cond, w_mod, b_mod):
    m = jax.nn.silu(cond) @ w_mod + b_mod
    return m.reshape(m.shape[:-1] + (N_MOD, D_MODEL))

def modulate(h, shift, scale):
    return h * (1 + scale) + shift

def axial_rope_tables(n_lat):
    rows = n_lat // GRID_W
    row = jnp.repeat(jnp.arange(rows, dtype=jnp.float32), GRID_W)
    col = jnp.tile(jnp.arange(GRID_W, dtype=jnp.float32), rows)
    n_freq = HEAD_DIM // 4
    inv_freq = ROPE_THETA ** (-jnp.arange(n_freq, dtype=jnp.float32) / n_freq)
    ang = jnp.stack([row[:, None] * inv_freq, col[:, None] * inv_freq], axis=1)
    return jnp.cos(ang), jnp.sin(ang)

def apply_rope_2(x, cos, sin):
    xf = x.astype(jnp.float32).reshape(x.shape[:-1] + (2, 2, HEAD_DIM // 4))
    x1, x2 = xf[..., 0, :], xf[..., 1, :]
    out = jnp.stack([x1 * cos - x2 * sin, x2 * cos + x1 * sin], axis=-2)
    return out.reshape(x.shape).astype(x.dtype)

def q_heads(q):
    b, n, _ = q.shape
    return q.reshape(b, n, N_KV_HEADS, Q_PER_KV, HEAD_DIM).transpose(0, 2, 3, 1, 4)

def kv_heads(k):
    b, n, _ = k.shape
    return k.reshape(b, n, N_KV_HEADS, HEAD_DIM).transpose(0, 2, 1, 3)

def gqa_blocks(q, k, v):
    b, kvh, g, n, dh = q.shape
    nb = n // Q_BLOCK
    qb = jnp.moveaxis(q.reshape(b, kvh, g, nb, Q_BLOCK, dh), 3, 0)

    def one_block(qblk):
        s = jnp.einsum('bkgqd,bkmd->bkgqm', qblk, k).astype(jnp.float32)
        p = jax.nn.softmax(s, axis=-1).astype(v.dtype)
        return jnp.einsum('bkgqm,bkmd->bkgqd', p, v)

    o = lax.map(one_block, qb)
    o = jnp.moveaxis(o, 0, 3).reshape(b, kvh, g, n, dh)
    return o.transpose(0, 3, 1, 2, 4).reshape(b, n, ATTN_DIM)

def chunk_gmlp(u, vg, w_s, b_s, g_norm):
    b, n, _ = u.shape
    u = jax.nn.gelu(u)
    vg = group_layernorm(jax.nn.gelu(vg).reshape(b, n, N_GMLP_GROUPS, GMLP_GROUP_DIM),
                         g_norm.reshape(N_GMLP_GROUPS, GMLP_GROUP_DIM))
    vc = vg.reshape(b, n // CHUNK, CHUNK, N_GMLP_GROUPS, GMLP_GROUP_DIM)
    mixed = jnp.einsum('gpq,bnqgc->bnpgc', w_s, vc) + b_s.T[None, None, :, :, None]
    return u * mixed.reshape(b, n, GMLP_DIM)

def sqrelu_mlp(h, w1, w2):
    return jnp.square(jax.nn.relu(h @ w1)) @ w2

def second_inputs(seed: int = 0) -> dict:
    key = jax.random.key(seed)
    ks = jax.random.split(key, 17)
    f32 = jnp.float32
    nrm = lambda k, shape, s: (jax.random.normal(k, shape, f32) * s)
    gain = lambda k, shape: 1.0 + 0.02 * jax.random.normal(k, shape, f32)
    return {
        "x": nrm(ks[0], (BATCH, SEQ, D_MODEL), 1.0),
        "c": nrm(ks[1], (BATCH, D_MODEL), 1.0),
        "ctx": nrm(ks[2], (BATCH, CTX_LEN, D_MODEL), 1.0),
        "c_ctx": nrm(ks[3], (D_MODEL,), 1.0),
        "w_mod": nrm(ks[4], (DEPTH, D_MODEL, N_MOD * D_MODEL), D_MODEL ** -0.5),
        "b_mod": nrm(ks[5], (DEPTH, N_MOD * D_MODEL), 0.02),
        "norm1_g": gain(ks[6], (DEPTH, D_MODEL)),
        "w_in": nrm(ks[7], (DEPTH, D_MODEL, IN_DIM), D_MODEL ** -0.5),
        "q_norm_g": gain(ks[8], (DEPTH, HEAD_DIM)),
        "k_norm_g": gain(ks[9], (DEPTH, HEAD_DIM)),
        "gmlp_norm_g": gain(ks[10], (DEPTH, GMLP_DIM)),
        "w_spatial": nrm(ks[11], (DEPTH, N_GMLP_GROUPS, CHUNK, CHUNK), CHUNK ** -0.5),
        "b_spatial": gain(ks[12], (DEPTH, N_GMLP_GROUPS, CHUNK)),
        "w_out": nrm(ks[13], (DEPTH, MIX_DIM, D_MODEL), MIX_DIM ** -0.5),
        "norm2_g": gain(ks[14], (DEPTH, D_MODEL)),
        "w_ff1": nrm(ks[15], (DEPTH, D_MODEL, FF_DIM), D_MODEL ** -0.5),
        "w_ff2": nrm(ks[16], (DEPTH, FF_DIM, D_MODEL), FF_DIM ** -0.5),
    }

def second_block(x, c, ctx, c_ctx, w_mod, b_mod, norm1_g, w_in, q_norm_g, k_norm_g, gmlp_norm_g,
              w_spatial, b_spatial, w_out, norm2_g, w_ff1, w_ff2):
    n_lat = x.shape[1]
    cos, sin = axial_rope_tables(n_lat)
    q_scale = HEAD_DIM ** -0.5
    kv_lo, kv_hi = ATTN_DIM, ATTN_DIM + 2 * KV_DIM
    x_lat, x_ctx = x, ctx
    for l in range(DEPTH):
        last = l == DEPTH - 1
        m_lat = modulation(c, w_mod[l], b_mod[l])
        m_ctx = modulation(c_ctx, w_mod[l], b_mod[l])
        sh1, sc1, ga1, sh2, sc2, ga2 = [m_lat[:, i, None, :] for i in range(N_MOD)]
        csh1, csc1, cga1, csh2, csc2, cga2 = [m_ctx[None, i, None, :] for i in range(N_MOD)]

        h_lat = modulate(rmsnorm_2(x_lat, norm1_g[l]), sh1, sc1)
        h_ctx = modulate(rmsnorm_2(x_ctx, norm1_g[l]), csh1, csc1)
        z_lat = h_lat @ w_in[l]
        q_l = z_lat[..., :ATTN_DIM]
        k_l = z_lat[..., kv_lo:kv_lo + KV_DIM]
        v_l = z_lat[..., kv_lo + KV_DIM:kv_hi]
        u_l = z_lat[..., kv_hi:kv_hi + GMLP_DIM]
        g_l = z_lat[..., kv_hi + GMLP_DIM:]
        if last:
            z_ctx = h_ctx @ w_in[l][:, kv_lo:kv_hi]
            k_c, v_c = z_ctx[..., :KV_DIM], z_ctx[..., KV_DIM:]
        else:
            z_ctx = h_ctx @ w_in[l]
            q_c = z_ctx[..., :ATTN_DIM]
            k_c = z_ctx[..., kv_lo:kv_lo + KV_DIM]
            v_c = z_ctx[..., kv_lo + KV_DIM:kv_hi]
            u_c = z_ctx[..., kv_hi:kv_hi + GMLP_DIM]
            g_c = z_ctx[..., kv_hi + GMLP_DIM:]

        qh_l = apply_rope_2(rmsnorm_2(q_heads(q_l), q_norm_g[l]), cos, sin) * q_scale
        kh_l = apply_rope_2(rmsnorm_2(kv_heads(k_l), k_norm_g[l]), cos, sin)
        kh_c = rmsnorm_2(kv_heads(k_c), k_norm_g[l])
        vh_c = kv_heads(v_c)
        k_all = jnp.concatenate([kh_c, kh_l], axis=2)
        v_all = jnp.concatenate([vh_c, kv_heads(v_l)], axis=2)
        attn_lat = gqa_blocks(qh_l, k_all, v_all)
        gm_lat = chunk_gmlp(u_l, g_l, w_spatial[l], b_spatial[l], gmlp_norm_g[l])
        x_lat = x_lat + ga1 * (jnp.concatenate([attn_lat, gm_lat], axis=-1) @ w_out[l])
        x_lat = x_lat + ga2 * sqrelu_mlp(modulate(rmsnorm_2(x_lat, norm2_g[l]), sh2, sc2),
                                         w_ff1[l], w_ff2[l])

        if not last:
            qh_c = rmsnorm_2(q_heads(q_c), q_norm_g[l]) * q_scale
            attn_ctx = gqa_blocks(qh_c, kh_c, vh_c)
            gm_ctx = chunk_gmlp(u_c, g_c, w_spatial[l], b_spatial[l], gmlp_norm_g[l])
            x_ctx = x_ctx + cga1 * (jnp.concatenate([attn_ctx, gm_ctx], axis=-1) @ w_out[l])
            x_ctx = x_ctx + cga2 * sqrelu_mlp(modulate(rmsnorm_2(x_ctx, norm2_g[l]), csh2, csc2),
                                              w_ff1[l], w_ff2[l])
    return x_lat


def setup_inputs(seed=0):
    out = dict(first_inputs(seed))
    for name, value in second_inputs(seed + 1).items():
        if name != "x":
            out[name + "_2"] = value
    return out


def reference(
    x, norm1_g, w_in, b_gate, na_rpb, mla_qa_g, mla_kva_g, mla_w_uq, mla_w_ukv, gqa_sink,
    w_br_na, w_br_mla, w_br_gqa, w_out, norm2_g, w_up, conv_w, conv_b, w_down, final_g, c_2,
    ctx_2, c_ctx_2, w_mod_2, b_mod_2, norm1_g_2, w_in_2, q_norm_g_2, k_norm_g_2, gmlp_norm_g_2,
    w_spatial_2, b_spatial_2, w_out_2, norm2_g_2, w_ff1_2, w_ff2_2,
):
    x = first_block(
        x, norm1_g, w_in, b_gate, na_rpb, mla_qa_g, mla_kva_g, mla_w_uq, mla_w_ukv, gqa_sink,
        w_br_na, w_br_mla, w_br_gqa, w_out, norm2_g, w_up, conv_w, conv_b, w_down, final_g,
    )
    return second_block(
        x, c_2, ctx_2, c_ctx_2, w_mod_2, b_mod_2, norm1_g_2, w_in_2, q_norm_g_2, k_norm_g_2,
        gmlp_norm_g_2, w_spatial_2, b_spatial_2, w_out_2, norm2_g_2, w_ff1_2, w_ff2_2,
    )


_drawn_inputs = setup_inputs


def setup_inputs(seed=0):
    import zlib

    import numpy as np

    out = dict(_drawn_inputs(seed))
    spreads = {}
    factors = {'norm1_g': 2.704,
     'b_gate': 8.0,
     'na_rpb': 3.493,
     'mla_qa_g': 8.0,
     'mla_kva_g': 6.903,
     'gqa_sink': 8.0,
     'norm1_g_2': 4.273,
     'q_norm_g_2': 8.0,
     'k_norm_g_2': 8.0,
     'gmlp_norm_g_2': 6.998,
     'b_spatial_2': 7.148,
     'norm2_g_2': 2.85}
    for name, (base, spread) in spreads.items():
        noise = np.random.default_rng([zlib.crc32(name.encode()), seed]).standard_normal(out[name].shape)
        drawn = base * np.exp(spread * noise) if base else spread * noise
        out[name] = __import__('jax').numpy.asarray(drawn.astype(out[name].dtype))
    for name, factor in factors.items():
        out[name] = (out[name] * factor).astype(out[name].dtype)
    return out
```

```python
import math
from contextlib import ExitStack

import numpy as np

import concourse.bass as bass
from concourse import mybir

P = 128
D = 1024
S = 256
L = 2
KT = D // P
NB = S // P
EPS = 1e-6
NEG = -1e30
THETA = 10000.0
GRID = 64

NA_HEADS, HD = 8, 64
NA_ROWS = S // GRID
WIN_R, WIN_C = 8, 16
MLA_HEADS, Q_RANK, KV_RANK, NOPE, ROPE, VD = 4, 384, 256, 128, 64, 128
QT, KVT = Q_RANK // P, KV_RANK // P
MLA_SCALE = (NOPE + ROPE) ** -0.5
HD_SCALE = HD ** -0.5
GQA_WINDOW = 128
FF = 2816
FT = FF // P
FF2 = 4096
FT2 = FF2 // P
N_MOD = 6
MT = N_MOD * KT
GELU = "Gelu_apprx_tanh"

C_ID, C_ONE, C_ROT1, C_ROT2, C_HEAD = 0, 128, 256, 384, 512
C_COS1, C_SIN1, C_COS2, C_SIN2 = 640, 896, 1152, 1408
C_WIN, C_NA, C_INV, C_PICK = 1664, 2176, 2432, 2436
N_CONST = C_PICK + 2
V_G1, V_BG, V_QA, V_KVA, V_SINK = 0, 8, 32, 35, 37
N_VA = 45
V_G2, V_W0, V_CB = 0, 8, 8 + 3 * 2 * FT
N_VB = V_CB + 2 * FT
U_G1, U_G2, U_QG, U_KG, U_GG = 0, 8, 16, 17, 18
N_U = 22


def number(order):
    count, out = {}, {}
    for name, place, times in order:
        out[name] = (place, count.get(place, 0))
        count[place] = count.get(place, 0) + times
    return out, count


UNITS1 = [("na", h) for h in range(NA_HEADS)] + [("gqa", j) for j in range(8)] + [("mla", h) for h in range(MLA_HEADS)]
NU1 = len(UNITS1)


def fills_1():
    names = ["cq01", "cq2gk", "ckv", "gv", "kr", "q0", "q1", "ms_q", "ms_kv", "k0", "k1", "Rgk", "bc_q", "bc_kv",
             "v0", "v1", "gq0", "gq1", "mqn0", "mqn1", "mqr", "Rgq0", "Rgq1", "mkn0", "mkn1", "Rmqr", "mv0", "mv1"]
    order = [("ms1", 7, 1), ("bc1", 6, 1)]
    order += [(n, i % 8, 1) for i, n in enumerate(names)]
    for i in range(NU1):
        order += [(("S", i), (0, 1, 2)[i % 3], 1), (("T", i), (3, 4)[i % 2], 1)]
        if i % 2 == 0:
            order += [(("Y", i // 2), (5, 6)[(i // 2) % 2], 1)]
    order += [(("gate", b), b, 3) for b in range(4)]
    order += [(("br", b, f), 4 + f % 4, 1) for b in range(3) for f in range(4)]
    order += [(("out", f), f, 1) for f in range(4)]
    order += [("ms2", 4, 1), ("bc2", 5, 1)]
    order += [(("up", j), (6, 7)[j], FT // 2) for j in range(2)]
    order += [("mod", 3, N_MOD * D // 512), ("pick", 2, N_MOD * D // 512)]
    order += [(("down", j), j, KT // 2) for j in range(2)]
    return number(order)


def slabs_1():
    order = [("w_cq", 0, 1), ("w_ckv", 1, 1), ("w_q", 2, 1), ("w_k", 3, 1), ("w_v", 4, 1), ("w_gq", 0, 1),
             ("w_uq", 1, 1), ("w_ukv", 2, 1)]
    order += [(("gate", j), 3 + j, 3) for j in range(2)]
    order += [(("br", b), b, 1) for b in range(3)]
    order += [(("out", j), 3 + j, 1) for j in range(2)]
    order += [(("up", j), j, FT // 2) for j in range(2)]
    order += [(("down", j), 2 + j, KT // 2) for j in range(2)]
    order += [("mod", 4, N_MOD * D // 512)]
    return number(order)


START = 1
FILL1, BANK1 = fills_1()
SLAB1, SLOT1 = slabs_1()

VEC_STEPS = 4 + 4 + 2 + 2 * NU1 + 8 + 4

LAST1 = {"w_cq": "cq2gk", "w_ckv": "kr", "w_q": "q1", "w_k": "k1", "w_v": "v1", "w_gq": "gq1", "w_uq": "mqr",
         "w_ukv": "mv1"}
LAST1.update({("br", b): ("br", b, 3) for b in range(3)})
LAST1.update({("out", j): ("out", 2 * j + 1) for j in range(2)})


UNITS2 = [[("ctx", j // 2, j % 2, 0) for j in range(8)], []]
for _l in range(L):
    UNITS2[_l] = UNITS2[_l] + [("lat", j // 4, j % 2, (j % 4) // 2) for j in range(16)]
Y2 = [[(j // 2, j % 2 == 0, j % 2 == 1) for j in range(8)] + [(4 + j // 4, j % 4 == 0, j % 4 == 3) for j in range(16)],
      [(j // 4, j % 4 == 0, j % 4 == 3) for j in range(16)]]


def fills_2():
    order = [("ms_f", 7, 1), ("bc_f", 6, 1)]
    for l in range(L):
        names = [("ms", 0), ("bc", 0)] + [("q", m) for m in range(4)] + [("k",), ("v",)]
        names += [("hm", m) for m in range(5)] + [("vg", d) for d in range(0 if l == 0 else NB, 2 * NB)]
        names += [("rot", m) for m in range(3)] + [("u", m) for m in range(4)]
        order += [((l, *n), i % 8, 1) for i, n in enumerate(names)]
        for i in range(len(UNITS2[l])):
            order += [((l, "S", i), (0, 1, 2)[i % 3], 1), ((l, "T", i), (3, 4)[i % 2], 1)]
        order += [((l, "Y", y), (5, 6)[y % 2], 1) for y in range(Y2[l][-1][0] + 1)]
        order += [((l, "sp", g), 7, 1) for g in range(4)]
        order += [((l, "out", m), m, 1) for m in range(KT)]
        order += [((l, "ms", 1), 0, 1), ((l, "bc", 1), 1, 1)]
        order += [((l, "f1", m), m, 4) for m in range(8)]
        order += [((l, "f2", j), j, KT // 2) for j in range(2)]
    return number(order)


def slabs_2():
    order = []
    for l in range(L):
        order += [((l, "q"), 0, 1), ((l, "kv"), 1, 1), ((l, "vg"), 2, 1), ((l, "u"), 3, 1),
                  ((l, "out", 0), 4, 1), ((l, "out", 1), 0, 1)]
        order += [((l, "f1", j), 1 + j, 4) for j in range(2)]
        order += [((l, "f2", j), 3 + j, 4) for j in range(2)]
    return number(order)


FILL2, _ = fills_2()
SLAB2, _ = slabs_2()
LAST2, LOOPED2 = {}, {}
for _l in range(L):
    LAST2.update({(_l, "q"): (_l, "q", 3), (_l, "kv"): (_l, "v"), (_l, "vg"): (_l, "vg", 3), (_l, "u"): (_l, "u", 3),
                  (_l, "out", 0): (_l, "out", 3), (_l, "out", 1): (_l, "out", 7)})
    LAST2.update({(_l, "f1", j): (_l, "f1", 4 * j + 3) for j in range(2)})
    LAST2.update({(_l, "f2", j): (_l, "f2", j) for j in range(2)})
    LOOPED2.update({(_l, "f1", m): 4 for m in range(8)})
    LOOPED2.update({(_l, "f2", j): 4 for j in range(2)})
FREED_AT_END1 = {0: 6, 1: 7, 2: 0, 3: 1, 4: 3}
DIAGS2 = {(0, 0): 8 * L + 2, (0, 1): 8 * L + 6, (1, 0): 8 * L + 10, (1, 1): 8 * L + 14}
MODDED2 = {(0, 0): 0, (0, 1): 2 * KT - 1, (1, 0): 2 * (2 * KT - 1), (1, 1): 3 * (2 * KT - 1)}


class Steps:

    def __init__(self, eng, sem, base=0):
        self.eng, self.sem, self.base, self.n = eng, sem, base, 0

    def done(self, instruction):
        instruction.then_inc(self.sem, 1)
        self.n += 1
        self.eng.wait_ge(self.sem, self.base + self.n)


def build(nc, a, out):
    f32 = mybir.dt.float32
    ALU = mybir.AluOpType
    ACT = mybir.ActivationFunctionType
    AX = mybir.AxisListType
    gelu_fn = ACT.Gelu_apprx_tanh

    with ExitStack() as ctx:
        def sb(name, n):
            return ctx.enter_context(nc.sbuf_tensor(name, [P, n], f32))

        def sem(name):
            return ctx.enter_context(nc.semaphore(name))

        X = sb("X", 2 * KT * S)
        H = sb("H", 2 * KT * S)
        ring = sb("ring", 5 * 4096)
        arena = sb("arena", 16384)
        biasb = sb("biasb", 4096)
        con = sb("con", N_CONST)
        vA = sb("vA", N_VA)
        vB = sb("vB", N_VB)
        derived = sb("derived", 40)
        small = sb("small", 128)
        diag = sb("diag", 4 * P)
        mod = sb("mod", L * MT * 2)
        csil = sb("csil", 2 * KT)

        def tiles(t, at, n, w=S):
            return t[:, at:at + n * w].rearrange("p (n w) -> p n w", w=w)

        def slot(s, n=4096):
            return ring[:, s * 4096:s * 4096 + n]

        xc, xl = tiles(X, 0, KT), tiles(X, KT * S, KT)
        hl = tiles(H, KT * S, KT)
        ident, ones = con[:, C_ID:C_ID + P], con[:, C_ONE:C_ONE + P]
        rot1, rot2, headones = con[:, C_ROT1:C_ROT1 + P], con[:, C_ROT2:C_ROT2 + P], con[:, C_HEAD:C_HEAD + P]
        cos1, sin1 = con[:, C_COS1:C_COS1 + S], con[:, C_SIN1:C_SIN1 + S]
        cos2, sin2 = con[:, C_COS2:C_COS2 + S], con[:, C_SIN2:C_SIN2 + S]
        winmask = con[:, C_WIN:C_WIN + 2 * S]
        namask = con[:, C_NA:C_NA + S]
        pick = con[:, C_PICK:C_PICK + 2]
        inv_d, inv_q, inv_kv, eps_c = (con[:, C_INV + i:C_INV + i + 1] for i in range(4))

        q_s, k_s = tiles(arena, 0, 4), tiles(arena, 1024, 4)
        v_s = tiles(arena, 2048, NB, 512)
        gq_s = tiles(arena, 3072, 4)
        gkr_s = tiles(arena, 4096, 2)
        gv_s = tiles(arena, 4608, NB, P)
        cq_s, ckv_s = tiles(arena, 4864, QT), tiles(arena, 5632, KVT)
        mq_s, mqr_s, mk_s = tiles(arena, 6144, 4), tiles(arena, 7168, 2), tiles(arena, 8192, 4)
        mv_s = tiles(arena, 9216, NB, 512)
        y_s = [tiles(arena, 10240 + 1024 * b, 4) for b in range(3)]
        tmp_s = [arena[:, 13312 + 512 * i:13824 + 512 * i] for i in range(2)]
        pt_s = [arena[:, 14336 + 512 * i:14848 + 512 * i] for i in range(2)]
        gate_s = tiles(arena, 0, 3 * KT)
        act_s = tiles(arena, 0, FT)
        conv_s = [tiles(arena, 8192 + 512 * j, 2) for j in range(2)]
        gelu_s = [arena[:, 9216 + 256 * j:9472 + 256 * j] for j in range(2)]
        mod_parts = arena[:, 10240:10752]
        csil_wide = tiles(arena, 15360, KT, 32)
        sq = tiles(X, 0, KT)
        prob_s = [H[:, 512 * i:512 * i + 512] for i in range(4)]
        merged = tiles(H, 0, KT)
        bias_s = tiles(biasb, 0, NA_HEADS, 512)

        psum = ctx.enter_context(nc.psum_tensor("psum", [P, 8, 512], f32))

        full = [sem(f"full{b}") for b in range(8)]
        drained = [sem(f"drained{b}") for b in range(8)]
        loaded = [sem(f"loaded{s}") for s in range(5)]
        const_in, x_in, va_in, vb_in, bias_in = sem("const_in"), sem("x_in"), sem("va_in"), sem("vb_in"), sem("bias_in")
        cond_in = sem("cond_in")
        squared = sem("squared")
        summed = sem("summed")
        diags = sem("diags")
        normed = sem("normed")
        lat_squared = sem("lat_squared")
        roped = sem("roped")
        biased = sem("biased")
        negmax = sem("negmax")
        exped = sem("exped")
        prob = sem("prob")
        half_bias = sem("half_bias")
        merged_in = sem("merged_in")
        tapped = sem("tapped")
        gelued = sem("gelued")
        acted = [sem(f"acted{j}") for j in range(2)]
        cond_exp, cond = sem("cond_exp"), sem("cond")
        vec_step, act_step, conv_step = sem("vec_step"), sem("act_step"), sem("conv_step")
        stored = sem("stored")

        fg_in, mod_in = sem("fg_in"), sem("mod_in")
        uvec = sb("uvec", L * N_U + KT)

        def at1(l, name, i=0):
            b, n = FILL1[name]
            return b, START + l * BANK1[b] + n + i

        def bank(b):
            return psum[:, b, :]

        X2, H2 = (t[:, :].rearrange("p (c t w) -> p c t w", c=2, w=S) for t in (X, H))
        sq2 = biasb[:, :].rearrange("p (c t w) -> p c t w", c=2, w=S)
        q2, k2 = tiles(arena, 0, 4, 2 * S), arena[:, 2048:2560]
        v2 = tiles(arena, 2560, 2 * NB, P)
        u2 = tiles(arena, 3072, 4, 2 * S)
        vg2 = tiles(arena, 5120, 2 * NB, 512)
        root2 = [arena[:, 7168 + 512 * i:7680 + 512 * i] for i in range(5)]
        hsq2 = [arena[:, 9728 + 512 * i:10240 + 512 * i] for i in range(5)]
        prob2 = [arena[:, 7168 + 512 * i:7680 + 512 * i] for i in range(4)]
        pt2 = [arena[:, 9216 + 512 * i:9728 + 512 * i] for i in range(2)]
        tmp2 = [arena[:, 12288 + 512 * i:12800 + 512 * i] for i in range(2)]
        ws2, bs2 = tiles(arena, 13824, 4, P), tiles(arena, 14336, 4, P)
        stats = sb("stats", 16 * 6)
        aggr = sb("aggr", 16 * 2)

        ws_in, ctx_in = sem("ws_in"), sem("ctx_in")
        modded = sem("modded")
        shifted = sem("shifted")
        headed = sem("headed")
        spread_v = sem("spread_v")
        levelled_stats = sem("levelled_stats")
        gated2 = sem("gated2")
        levelled = sem("levelled")
        acted2 = sem("acted2")

        def parts(l, both=False):
            return (0, 1) if l == 0 or both else (1,)

        def at2(name, i=0):
            b, n = FILL2[name]
            return b, START + L * BANK1[b] + n + i

        def modulation(l, which, t, part):
            return mod[:, l * 2 * MT + (which * KT + t) * 2 + part:l * 2 * MT + (which * KT + t) * 2 + part + 1]

        def gain(l, norm, t, part):
            c = (2 * l + norm) * 16 + 2 * t + part
            return gains2[:, c:c + 1]

        gains2 = sb("gains2", 64)
        uv = [uvec[:, KT + N_U * l:KT + N_U * (l + 1)] for l in range(L)]

        def stack2_sync(sp):
            occupant = {}

            def freed(s):
                if s in occupant:
                    b, n = at2(LAST2[occupant[s]])
                    sp.wait_ge(full[b], n + LOOPED2.get(LAST2[occupant[s]], 1))
                else:
                    b = FREED_AT_END1[s]
                    sp.wait_ge(full[b], START + L * BANK1[b])

            def load(name, src, n=4096):
                s, used = SLAB2[name]
                if name[1] not in ("f1", "f2"):
                    freed(s)
                    occupant[s] = name
                sp.dma_start(slot(s, n), src).then_inc(loaded[s], 16)

            load((0, "q"), a["w2_q"][0])
            load((0, "kv"), a["w2_kv"][0], 2048)
            b, n = at2("ms_f")
            sp.wait_ge(full[b], n + 1)
            sp.dma_start(X[:, 0:KT * S], a["ctxT"]).then_inc(ctx_in, 16)
            for l in range(L):
                if l == 1:
                    load((l, "q"), a["w2_q"][l])
                    load((l, "kv"), a["w2_kv"][l], 2048)
                    b, n = at2((0, "f2", 1))
                    sp.wait_ge(full[b], n + KT // 2)
                sp.dma_start(arena[:, 13824:14848], a["spatial"][l]).then_inc(ws_in, 16)
                load((l, "vg"), a["w2_vg"][l])
                load((l, "u"), a["w2_u"][l])
                for j in range(2):
                    load((l, "out", j), a["w2_out"][l, j])
                for stage, src in (("f1", a["w2_ff1"]), ("f2", a["w2_ff2"])):
                    with sp.Fori(0, 4) as i:
                        for j in range(2):
                            s, _u = SLAB2[(l, stage, j)]
                            freed(s)
                            b, n = at2(LAST2[(l, stage, j)], i)
                            sp.wait_ge(full[b], n)
                            load((l, stage, j), src[l, 2 * i + j])
                    for j in range(2):
                        occupant[SLAB2[(l, stage, j)][0]] = (l, stage, j)
            for j in range(2):
                b, n = at2((1, "f2", j))
                sp.wait_ge(drained[b], n + KT // 2)
            sp.dma_start(out, X[:, KT * S:2 * KT * S]).then_inc(stored, 16)
            sp.wait_ge(stored, 16)

        def stack2_tensor(pe):
            def claim(name, i=0):
                b, n = at2(name, i)
                pe.wait_ge(drained[b], n)
                return bank(b), full[b]

            def taken(*names):
                last = {}
                for name in names:
                    b, n = at2(name)
                    last[b] = max(last.get(b, 0), n + LOOPED2.get(name, 1))
                for b, n in last.items():
                    pe.wait_ge(drained[b], n)

            def slab(name, width, nk=KT, i=0):
                s, used = SLAB2[name]
                pe.wait_ge(loaded[s], 16 * (L * SLOT1[s] + used + i + 1))
                return slot(s, nk * width).rearrange("p (k c) -> p k c", c=width)

            def mean_squares(l, norm):
                o, sig = claim((l, "ms", norm))
                pe.wait_ge(summed, (2 * L + 2 * l + norm + 2) * (KT - 1))
                for c in parts(l, norm == 0):
                    for tb in range(NB):
                        mm = pe.matmul(o[:, c * NB + tb:c * NB + tb + 1], sq2[:, c, 0, tb * P:(tb + 1) * P], inv_d,
                                       start=True, stop=True)
                mm.then_inc(sig, 1)

            def spread_factors(l, norm):
                o, sig = claim((l, "bc", norm))
                pe.wait_ge(diags, DIAGS2[l, norm] + NB * len(parts(l, norm == 0)))
                for c in parts(l, norm == 0):
                    for tb in range(NB):
                        d = c * NB + tb
                        mm = pe.matmul(o[:, d * P:(d + 1) * P], ones, diag[:, d * P:(d + 1) * P], start=True, stop=True)
                mm.then_inc(sig, 1)

            def cols(l, both=False):
                return (slice(0, 2), 2 * S) if l == 0 or both else (slice(1, 2), S)

            for l in range(L):
                mean_squares(l, 0)
                spread_factors(l, 0)
                now, w = cols(l)
                shift0 = KT * 2 * l
                sl = slab((l, "q"), 512)
                for m in range(4):
                    o, sig = claim((l, "q", m))
                    for k in range(KT):
                        if m == 0:
                            pe.wait_ge(shifted, shift0 + k + 1)
                        mm = pe.matmul(o[:, 0:w], sl[:, k, m * P:(m + 1) * P], H2[:, now, k, :],
                                       start=(k == 0), stop=(k == KT - 1))
                    mm.then_inc(sig, 1)
                sl = slab((l, "kv"), 256)
                o, sig = claim((l, "k"))
                for k in range(KT):
                    mm = pe.matmul(o, sl[:, k, 0:P], H2[:, :, k, :], start=(k == 0), stop=(k == KT - 1))
                mm.then_inc(sig, 1)
                o, sig = claim((l, "v"))
                for c in range(2):
                    for tb in range(NB):
                        for k in range(KT):
                            mm = pe.matmul(o[:, (c * NB + tb) * P:(c * NB + tb + 1) * P],
                                           H2[:, c, k, tb * P:(tb + 1) * P], sl[:, k, P:2 * P],
                                           start=(k == 0), stop=(k == KT - 1))
                mm.then_inc(sig, 1)
                for m in range(5):
                    taken((l, "k") if m == 0 else (l, "q", m - 1))
                    o, sig = claim((l, "hm", m))
                    n = 2 * S if m == 0 else w
                    pe.matmul(o[:, 0:n], headones, hsq2[m][:, 0:n], start=True, stop=True).then_inc(sig, 1)
                sl = slab((l, "vg"), 512)
                for c in parts(l):
                    for tb in range(NB):
                        o, sig = claim((l, "vg", c * NB + tb))
                        for k in range(KT):
                            mm = pe.matmul(o, H2[:, c, k, tb * P:(tb + 1) * P], sl[:, k, :],
                                           start=(k == 0), stop=(k == KT - 1))
                        mm.then_inc(sig, 1)
                for m in range(3):
                    o, sig = claim((l, "rot", m))
                    pe.wait_ge(headed, 5 * l + (1, 3, 5)[m])
                    if m == 0:
                        mm = pe.matmul(o[:, 0:S], rot2, k2[:, S:2 * S], start=True, stop=True)
                    else:
                        mm = pe.matmul(o, rot2, q2[:, 2 * m - 2:2 * m, S:2 * S], start=True, stop=True)
                    mm.then_inc(sig, 1)
                sl = slab((l, "u"), 512)
                for m in range(4):
                    o, sig = claim((l, "u", m))
                    for k in range(KT):
                        mm = pe.matmul(o[:, 0:w], sl[:, k, m * P:(m + 1) * P], H2[:, now, k, :],
                                       start=(k == 0), stop=(k == KT - 1))
                    mm.then_inc(sig, 1)
                units = UNITS2[l]
                base = L * NU1 + (len(UNITS2[0]) if l else 0)
                for i in range(len(units) + 3):
                    if i == 0:
                        taken((l, "v"))
                        pe.wait_ge(roped, START + 4 * L + 3 * (l + 1))
                    if i < len(units):
                        kind, t, s, qb = units[i]
                        half = slice(64 * s, 64 * s + 64)
                        o, sig = claim((l, "S", i))
                        if kind == "ctx":
                            for n in range(NB):
                                mm = pe.matmul(o[:, n * S:(n + 1) * S], q2[half, t, n * P:(n + 1) * P], k2[half, 0:S],
                                               start=True, stop=True)
                        else:
                            mm = pe.matmul(o, q2[half, t, S + qb * P:S + (qb + 1) * P], k2[half, :],
                                           start=True, stop=True)
                        mm.then_inc(sig, 1)
                    if 3 <= i < 7:
                        g = i - 3
                        pe.wait_ge(levelled, (l + 1) * 4 if l == 0 else 4 + 2)
                        pe.wait_ge(ws_in, 16 * (l + 1))
                        o, sig = claim((l, "sp", g))
                        for c in parts(l):
                            for tb in range(NB):
                                d = c * NB + tb
                                mm = pe.matmul(o[:, d * P:(d + 1) * P], vg2[:, d, g * P:(g + 1) * P], ws2[:, g, :],
                                               start=True, stop=True)
                        mm.then_inc(sig, 1)
                    if 0 <= i - 2 < len(units):
                        u = i - 2
                        kind, t, s, qb = units[u]
                        o, sig = claim((l, "T", u))
                        pe.wait_ge(prob, base + u + 1)
                        for kt in range(4):
                            if kind == "ctx":
                                src, dst = (kt % 2) * S + (kt // 2) * P, (kt // 2) * S + (kt % 2) * P
                            else:
                                src = dst = kt * P
                            mm = pe.transpose(o[:, dst:dst + P], prob2[u % 4][:, src:src + P], ident)
                        mm.then_inc(sig, 1)
                    if 0 <= i - 3 < len(units):
                        u = i - 3
                        kind, t, s, qb = units[u]
                        half = slice(64 * s, 64 * s + 64)
                        y, first, last = Y2[l][u]
                        b, n = at2((l, "Y", y))
                        if first:
                            pe.wait_ge(drained[b], n)
                        taken((l, "T", u))
                        if kind == "ctx":
                            for kt in range(NB):
                                mm = pe.matmul(psum[half, b, 0:S], v2[:, kt, half], pt2[u % 2][:, kt * S:(kt + 1) * S],
                                               start=(kt == 0), stop=(kt == NB - 1))
                        else:
                            for kt in range(2 * NB):
                                mm = pe.matmul(psum[half, b, qb * P:(qb + 1) * P], v2[:, kt, half],
                                               pt2[u % 2][:, kt * P:(kt + 1) * P], start=(kt == 0), stop=(kt == 3))
                        if last:
                            mm.then_inc(full[b], 1)
                taken(*((l, "Y", y) for y in range(Y2[l][-1][0] + 1)))
                pe.wait_ge(gated2, 4 * (l + 1))
                for j in range(2):
                    sl = slab((l, "out", j), 512)
                    for m in range(4):
                        o, sig = claim((l, "out", 4 * j + m))
                        for k in range(KT):
                            mm = pe.matmul(o[:, 0:w], sl[:, k, m * P:(m + 1) * P], H2[:, now, k, :],
                                           start=(k == 0), stop=(k == KT - 1))
                        mm.then_inc(sig, 1)
                mean_squares(l, 1)
                spread_factors(l, 1)
                with pe.Fori(0, 4) as i:
                    for j in range(2):
                        sl = slab((l, "f1", j), 512, KT, i)
                        pe.wait_ge(shifted, shift0 + 2 * KT)
                        for m in range(4):
                            o, sig = claim((l, "f1", 4 * j + m), i)
                            for k in range(KT):
                                mm = pe.matmul(o[:, 0:w], sl[:, k, m * P:(m + 1) * P], H2[:, now, k, :],
                                               start=(k == 0), stop=(k == KT - 1))
                            mm.then_inc(sig, 1)
                act2 = tiles(arena, 0, FT2, w)
                with pe.Fori(0, 4) as i:
                    for j in range(2):
                        sl = slab((l, "f2", j), P, FT2, i)
                        o, sig = claim((l, "f2", j), i)
                        pe.wait_ge(acted2, FT2 * (l + 1))
                        for k in range(FT2):
                            mm = pe.matmul(o[:, 0:w], sl[:, k, :], act2[:, k, :], start=(k == 0), stop=(k == FT2 - 1))
                        mm.then_inc(sig, 1)

        def stack2_scalar(act):
            def wait_full(name, i=0):
                b, n = at2(name, i)
                act.wait_ge(full[b], n + 1)
                return bank(b), drained[b]

            def shift(l, norm):
                now = parts(l, norm == 0)
                for t in range(KT):
                    if t < KT - 1:
                        act.wait_ge(modded, MODDED2[l, norm] + len(now) * (t + 1))
                    else:
                        b, n = at2((l, "bc", norm))
                        act.wait_ge(drained[b], n + 1)
                    for c in now:
                        e = act.activation(H2[:, c, t, :], H2[:, c, t, :], ACT.Identity,
                                           bias=modulation(l, 3 * norm, t, c))
                    e.then_inc(shifted, 1)

            def root_of(l, norm):
                o, sig = wait_full((l, "ms", norm))
                c0 = 0 if len(parts(l, norm == 0)) == 2 else NB
                act.activation(small[:, c0:4], o[:, c0:4], ACT.Sqrt, bias=eps_c).then_inc(sig, 1)

            b, n = at2("bc_f")
            act.wait_ge(drained[b], n + 1)
            act.wait_ge(ctx_in, 16)
            for t in range(KT):
                act.activation(sq2[:, :, t, :], X2[:, :, t, :], ACT.Square).then_inc(squared, 1)
            for l in range(L):
                now = slice(0, 2) if l == 0 else slice(1, 2)
                w = 2 * S if l == 0 else S
                root_of(l, 0)
                shift(l, 0)
                for m in range(4):
                    o, sig = wait_full((l, "q", m))
                    act.activation(q2[:, m, 2 * S - w:2 * S], o[:, 0:w], ACT.Copy)
                    act.activation(hsq2[m + 1][:, 0:w], o[:, 0:w], ACT.Square).then_inc(sig, 1)
                o, sig = wait_full((l, "k"))
                act.activation(k2, o, ACT.Copy)
                act.activation(hsq2[0], o, ACT.Square).then_inc(sig, 1)
                for m in range(5):
                    o, sig = wait_full((l, "hm", m))
                    n = 2 * S if m == 0 else w
                    act.activation(root2[m][:, 0:n], o[:, 0:n], ACT.Sqrt, bias=eps_c).then_inc(sig, 1)
                for c in parts(l):
                    for tb in range(NB):
                        o, sig = wait_full((l, "vg", c * NB + tb))
                        act.activation(vg2[:, c * NB + tb, :], o, gelu_fn).then_inc(sig, 1)
                for m in range(4):
                    o, sig = wait_full((l, "u", m))
                    act.activation(u2[:, m, 2 * S - w:2 * S], o[:, 0:w], gelu_fn).then_inc(sig, 1)
                act.wait_ge(levelled_stats, l + 1)
                g0 = 4 * NB * (2 - len(parts(l)))
                var = aggr[:, :].rearrange("p (g two) -> p g two", two=2)[:, g0:16, 1]
                act.activation(var, var, ACT.Sqrt, bias=eps_c).then_inc(spread_v, 1)
                units = UNITS2[l]
                base = L * NU1 + (len(UNITS2[0]) if l else 0)
                for i in range(len(units) + 3):
                    if i < len(units):
                        kind, t, s, qb = units[i]
                        b, n = at2((l, "S", i))
                        c = 16 + 8 * (i % 4)
                        act.wait_ge(negmax, base + i + 1)
                        for n in range(NB if kind == "ctx" else 1):
                            qs = slice(n * S, (n + 1) * S) if kind == "ctx" else slice(0, 2 * S)
                            e = act.activation(prob2[i % 4][:, qs], bank(b)[:, qs], ACT.Exp, scale=HD_SCALE,
                                               bias=small[:, c + n:c + n + 1], accum_out=small[:, c + 2 + n:c + 3 + n])
                        e.then_inc(drained[b], 1)
                    if 0 <= i - 2 < len(units):
                        o, sig = wait_full((l, "T", i - 2))
                        act.activation(pt2[i % 2], o, ACT.Copy).then_inc(sig, 1)
                    if 0 <= i - 3 < len(units) and Y2[l][i - 3][2]:
                        kind, t, s, qb = units[i - 3]
                        o, sig = wait_full((l, "Y", Y2[l][i - 3][0]))
                        act.activation(H2[:, 0 if kind == "ctx" else 1, t, :], o[:, 0:S], ACT.Copy).then_inc(sig, 1)
                for m in range(KT):
                    b, n = at2((l, "out", m))
                    act.wait_ge(drained[b], n + 1)
                    act.activation(sq2[:, now, m, :], X2[:, now, m, :], ACT.Square).then_inc(squared, 1)
                root_of(l, 1)
                shift(l, 1)
                act2 = tiles(arena, 0, FT2, w)
                with act.Fori(0, 4) as i:
                    for m in range(8):
                        o, sig = wait_full((l, "f1", m), i)
                        act.nop()
                        act.activation(act2[:, bass.ds(8 * i + m, 1), :], o[:, 0:w].unsqueeze(1),
                                       ACT.Relu).then_inc(sig, 1)
                if l < L - 1:
                    with act.Fori(0, 4) as i:
                        for j in range(2):
                            b, n = at2((l, "f2", j), i)
                            act.wait_ge(drained[b], n + 1)
                            act.nop()
                            for c in range(2):
                                e = act.activation(sq2[:, c, bass.ds(2 * i + j, 1), :], X2[:, c, bass.ds(2 * i + j, 1), :],
                                                   ACT.Square)
                            e.then_inc(squared, 1)

        def stack2_gpsimd(pool, add_squares):
            def add(l, norm):
                now = slice(0, 2) if norm == 0 or l == 0 else slice(1, 2)
                n = 2 * l + norm
                add_squares(2 * L + n + 1, lambda t: sq2[:, now, t, :], lambda t: 12 * L + 8 + 8 * n + t + 1)

            for l in range(L):
                add(l, 0)
                add(l, 1)
                w = 2 * S if l == 0 else S
                act2 = tiles(arena, 0, FT2, w)
                with pool.Fori(0, 4) as i:
                    for m in range(8):
                        b, n = at2((l, "f1", m), i)
                        pool.wait_ge(drained[b], n + 1)
                        pool.nop()
                        r = act2[:, bass.ds(8 * i + m, 1), :]
                        pool.tensor_tensor(r, r, r, ALU.mult).then_inc(acted2, 1)

        def stack2_vector(vec):
            def wait_full(name, i=0):
                b, n = at2(name, i)
                vec.wait_ge(full[b], n + 1)
                return bank(b), drained[b]

            step = Steps(vec, vec_step, L * VEC_STEPS + 4)

            def modulated_norm(l, norm):
                now = parts(l, norm == 0)
                b, n = at2((l, "ms", norm))
                vec.wait_ge(drained[b], n + 1)
                c0 = 0 if len(now) == 2 else NB
                step.done(vec.reciprocal(small[:, c0:4], small[:, c0:4]))
                for d in range(c0, 4):
                    vec.tensor_scalar(diag[:, d * P:(d + 1) * P], ident, small[:, d:d + 1], None,
                                      ALU.mult).then_inc(diags, 1)
                o, sig = wait_full((l, "bc", norm))
                for t in range(KT):
                    for c in now:
                        e = vec.scalar_tensor_tensor(H2[:, c, t, :], X2[:, c, t, :], gain(l, norm, t, c),
                                                     o[:, c * S:(c + 1) * S], ALU.mult, ALU.mult)
                        e.then_inc(sig if (t, c) == (KT - 1, now[-1]) else modded, 1)

            for l in range(L):
                for norm in range(2):
                    c = (2 * l + norm) * 16
                    m0 = l * 2 * MT + (3 * norm + 1) * KT * 2
                    sc = mod[:, m0:m0 + 16].rearrange("p (t c) -> p t c", c=2)
                    g = uv[l][:, norm * KT:(norm + 1) * KT].unsqueeze(2).to_broadcast([P, KT, 2])
                    step.done(vec.scalar_tensor_tensor(gains2[:, c:c + 16].rearrange("p (t c) -> p t c", c=2), sc, 1.0,
                                                       g, ALU.add, ALU.mult))
            for l in range(L):
                w = 2 * S if l == 0 else S
                now = slice(0, 2) if l == 0 else slice(1, 2)
                modulated_norm(l, 0)
                o, sig = wait_full((l, "v"))
                vec.tensor_copy(arena[:, 2560:3072], o).then_inc(sig, 1)
                for m in range(5):
                    b, n = at2((l, "hm", m))
                    vec.wait_ge(drained[b], n + 1)
                    dst = k2 if m == 0 else q2[:, m - 1, 2 * S - w:2 * S]
                    r = root2[m][:, 0:2 * S if m == 0 else w]
                    step.done(vec.reciprocal(r, r))
                    g = uv[l][:, 17:18] if m == 0 else uv[l][:, 16:17]
                    vec.scalar_tensor_tensor(dst, dst, g, r, ALU.mult, ALU.mult).then_inc(headed, 1)
                for m in range(3):
                    vec.wait_ge(headed, 5 * l + (1, 3, 5)[m])
                    o, sig = wait_full((l, "rot", m))
                    if m == 0:
                        n, dst, ps = 1, k2[:, S:2 * S].unsqueeze(1), o[:, 0:S].unsqueeze(1)
                    else:
                        n, dst, ps = 2, q2[:, 2 * m - 2:2 * m, S:2 * S], o.rearrange("p (n w) -> p n w", w=S)
                    vec.wait_ge(roped, START + 4 * L + 3 * l + m)
                    t = tmp2[0][:, 0:n * S].rearrange("p (n w) -> p n w", w=S)
                    vec.tensor_tensor(t, ps, sin2.unsqueeze(1).to_broadcast([P, n, S]), ALU.mult).then_inc(sig, 1)
                    step.done(vec.tensor_tensor(dst, dst, cos2.unsqueeze(1).to_broadcast([P, n, S]), ALU.mult))
                    b, n = at2((l, "rot", m))
                    vec.wait_ge(drained[b], n + 1)
                    vec.tensor_tensor(dst, dst, t, ALU.add).then_inc(roped, 1)
                blocks = [c * NB + tb for c in parts(l) for tb in range(NB)]
                for d in blocks:
                    b, n = at2((l, "vg", d))
                    vec.wait_ge(drained[b], n + 1)
                    for g in range(4):
                        j = 4 * d + g
                        e = vec.bn_stats(stats[:, 6 * j:6 * j + 6], vg2[:, d, g * P:(g + 1) * P])
                        if g == 3:
                            step.done(e)
                    for g in range(4):
                        j = 4 * d + g
                        e = vec.bn_aggr(aggr[:, 2 * j:2 * j + 2], stats[:, 6 * j:6 * j + 6])
                        if (d, g) == (blocks[-1], 3):
                            e.then_inc(levelled_stats, 1)
                vec.wait_ge(spread_v, l + 1)
                g0 = 4 * blocks[0]
                var = aggr[:, :].rearrange("p (g two) -> p g two", two=2)[:, g0:16, 1]
                step.done(vec.reciprocal(var, var))
                for d in blocks:
                    for g in range(4):
                        j = 4 * d + g
                        v = vg2[:, d, g * P:(g + 1) * P]
                        e = vec.tensor_scalar(v, v, aggr[:, 2 * j:2 * j + 1], aggr[:, 2 * j + 1:2 * j + 2],
                                              ALU.subtract, ALU.mult)
                    e.then_inc(levelled, 1)

                units = UNITS2[l]
                base = L * NU1 + (len(UNITS2[0]) if l else 0)
                for i in range(len(units) + 1):
                    if i < len(units):
                        kind, t, s, qb = units[i]
                        c = 16 + 8 * (i % 4)
                        o, sig = wait_full((l, "S", i))
                        n = NB if kind == "ctx" else 1
                        step.done(vec.tensor_reduce(small[:, c + 6:c + 6 + n], o.rearrange("p (n w) -> p n w", n=n),
                                                    axis=AX.X, op=ALU.max))
                        if i >= 4:
                            b, m = at2((l, "T", i - 4))
                            vec.wait_ge(full[b], m + 1)
                        vec.tensor_scalar(small[:, c:c + n], small[:, c + 6:c + 6 + n], -HD_SCALE, None,
                                          ALU.mult).then_inc(negmax, 1)
                    if i >= 1:
                        u = i - 1
                        kind, t, s, qb = units[u]
                        c = 16 + 8 * (u % 4)
                        n = NB if kind == "ctx" else 1
                        b, m = at2((l, "S", u))
                        vec.wait_ge(drained[b], m + 1)
                        step.done(vec.reciprocal(small[:, c + 2:c + 2 + n], small[:, c + 2:c + 2 + n]))
                        for m in range(n):
                            qs = slice(m * S, (m + 1) * S) if n == 2 else slice(0, 2 * S)
                            e = vec.tensor_scalar(prob2[u % 4][:, qs], prob2[u % 4][:, qs],
                                                  small[:, c + 2 + m:c + 3 + m], None, ALU.mult)
                        e.then_inc(prob, 1)
                    if 4 <= i < 8:
                        g = i - 4
                        o, sig = wait_full((l, "sp", g))
                        vec.wait_ge(ws_in, 16 * (l + 1))
                        lo = 2 * S - w
                        n = w // P
                        t = tmp2[g % 2][:, lo:2 * S].rearrange("p (n w) -> p n w", w=P)
                        vec.scalar_tensor_tensor(t, o[:, lo:2 * S].rearrange("p (n w) -> p n w", w=P),
                                                 uv[l][:, 18 + g:19 + g], bs2[:, g:g + 1, :].to_broadcast([P, n, P]),
                                                 ALU.mult, ALU.add).then_inc(sig, 1)
                        b, m = at2((l, "sp", g))
                        vec.wait_ge(drained[b], m + 1)
                        vec.tensor_tensor(H2[:, now, 4 + g, :], tmp2[g % 2][:, lo:2 * S].rearrange("p (n w) -> p n w", w=S),
                                          u2[:, g, lo:2 * S].rearrange("p (n w) -> p n w", w=S),
                                          ALU.mult).then_inc(gated2, 1)
                for m in range(KT):
                    o, sig = wait_full((l, "out", m))
                    for c in parts(l):
                        ps = o[:, c * S:(c + 1) * S] if l == 0 else o[:, 0:S]
                        e = vec.scalar_tensor_tensor(X2[:, c, m, :], ps, modulation(l, 2, m, c), X2[:, c, m, :],
                                                     ALU.mult, ALU.add)
                    e.then_inc(sig, 1)
                modulated_norm(l, 1)
                with vec.Fori(0, 4) as i:
                    for j in range(2):
                        o, sig = wait_full((l, "f2", j), i)
                        for c in parts(l):
                            ps = o[:, c * S:(c + 1) * S] if l == 0 else o[:, 0:S]
                            x1 = X2[:, c, bass.ds(2 * i + j, 1), :]
                            m0 = l * 2 * MT + 5 * KT * 2 + c + 2 * j
                            e = vec.scalar_tensor_tensor(x1, ps.unsqueeze(1), mod[:, bass.ds(4 * i + m0, 1)], x1,
                                                         ALU.mult, ALU.add)
                        e.then_inc(sig, 1)

        block = ctx.enter_context(nc.Block())

        @block.sync
        def _(sp):
            def wait_full(l, name, times=1):
                b, n = FILL1[name]
                sp.wait_ge(full[b], START + l * BANK1[b] + n + times)

            def load(l, name, src, n=4096):
                s, used = SLAB1[name]
                sp.dma_start(slot(s, n), src).then_inc(loaded[s], 16)

            def load_mod(l, i):
                b, n = FILL1["mod"]
                sp.wait_ge(full[b], START + l * BANK1[b] + n + i)
                load(l, "mod", a["w_mod"][l, i])

            sp.dma_start(con[:, :], a["const"]).then_inc(const_in, 16)
            sp.dma_start(X[:, KT * S:2 * KT * S], a["xT"]).then_inc(x_in, 16)
            sp.dma_start(csil[:, 0:2 * KT], a["condT"]).then_inc(cond_in, 16)
            sp.dma_start(mod[:, :], a["b_mod"]).then_inc(mod_in, 16)
            sp.dma_start(uvec[:, :], a["uvec"]).then_inc(fg_in, 16)
            with sp.Fori(0, L) as l:
                sp.wait_ge(drained[4], START + l * BANK1[4])
                sp.dma_start(vA[:, :], a["vecA"][l]).then_inc(va_in, 16)
                for i, name in enumerate(("w_cq", "w_ckv", "w_q", "w_k", "w_v")):
                    b = FREED_AT_END1[SLAB1[name][0]]
                    sp.wait_ge(full[b], START + l * BANK1[b])
                    load(l, name, a["w_proj"][l, i])
                sp.wait_ge(drained[7], START + l * BANK1[7])
                sp.dma_start(vB[:, :], a["vecB"][l]).then_inc(vb_in, 16)
                wait_full(l, LAST1["w_cq"])
                load(l, "w_gq", a["w_proj"][l, 5])
                wait_full(l, LAST1["w_ckv"])
                load(l, "w_uq", a["w_uq"][l], QT * 768)
                wait_full(l, LAST1["w_q"])
                load(l, "w_ukv", a["w_ukv"][l], KVT * 1024)
                with sp.Fori(0, 3) as i:
                    for j in range(2):
                        wait_full(l, LAST1[("w_k", "w_v")[j]])
                        b, n = FILL1[("gate", 2 * j + 1)]
                        sp.wait_ge(full[b], START + l * BANK1[b] + n + i)
                        load(l, ("gate", j), a["w_gate"][l, 2 * i + j])
                for br, before in enumerate(("w_gq", "w_uq", "w_ukv")):
                    wait_full(l, LAST1[before])
                    load(l, ("br", br), a["w_br"][l, br])
                for j in range(2):
                    wait_full(l, ("gate", 2 * j + 1), 3)
                    load(l, ("out", j), a["w_out"][l, j])
                with sp.Fori(0, FT // 2) as i:
                    for j in range(2):
                        wait_full(l, LAST1[("br", j)])
                        b, n = FILL1[("up", j)]
                        sp.wait_ge(full[b], START + l * BANK1[b] + n + i)
                        load(l, ("up", j), a["w_up"][l, 2 * i + j], KT * 2 * P)
                        if j == 0:
                            load_mod(l, i)
                load_mod(l, FT // 2)
                with sp.Fori(0, KT // 2) as i:
                    for j in range(2):
                        wait_full(l, LAST1[(("br", 2), ("out", 0))[j]])
                        b, n = FILL1[("down", j)]
                        sp.wait_ge(full[b], START + l * BANK1[b] + n + i)
                        load(l, ("down", j), a["w_down"][l, 2 * i + j], FT * P)
            stack2_sync(sp)

        @block.tensor
        def _(pe):
            def claim(l, name, i=0):
                b, n = at1(l, name, i)
                pe.wait_ge(drained[b], n)
                return bank(b), full[b]

            def taken(l, *names):
                last = {}
                for name in names:
                    b, n = FILL1[name]
                    last[b] = max(last.get(b, 0), n + 1)
                for b, n in last.items():
                    pe.wait_ge(drained[b], START + l * BANK1[b] + n)

            def slab(l, name, width, i=0, n=None):
                s, used = SLAB1[name]
                pe.wait_ge(loaded[s], 16 * (l * SLOT1[s] + used + i + 1))
                return slot(s, (n or KT) * width).rearrange("p (k c) -> p k c", c=width)

            def group(o, lhs, rhs, nk):
                for k in range(nk):
                    mm = pe.matmul(o, lhs(k), rhs(k), start=(k == 0), stop=(k == nk - 1))
                return mm

            def channels(l, name, w, c0, n, x, nk=KT, width=S):
                o, sig = claim(l, name)
                for m in range(n):
                    mm = group(o[:, m * width:(m + 1) * width], lambda k: w[:, k, c0 + m * P:c0 + (m + 1) * P],
                               lambda k: x[:, k, :], nk)
                mm.then_inc(sig, 1)

            def mean_squares(l, name, s, nt, col):
                o, sig = claim(l, name)
                for tb in range(NB):
                    mm = group(o[:, tb:tb + 1], lambda t: s[:, t, tb * P:(tb + 1) * P], lambda t: col, nt)
                mm.then_inc(sig, 1)

            def spread(l, name, d0):
                o, sig = claim(l, name)
                for tb in range(NB):
                    mm = pe.matmul(o[:, tb * P:(tb + 1) * P], ones, diag[:, (d0 + tb) * P:(d0 + tb + 1) * P],
                                   start=True, stop=True)
                mm.then_inc(sig, 1)

            def rotate(l, name, src):
                o, sig = claim(l, name)
                pe.matmul(o, rot1, src, start=True, stop=True).then_inc(sig, 1)

            def modulate(l, i):
                w = slab(l, "mod", 512, i)
                o, sig = claim(l, "mod", i)
                for half in range(2):
                    for t in range(4):
                        k = 4 * half + t
                        mm = pe.matmul(o[32 * t:32 * t + 32, :], csil_wide[:, k, :], w[:, k, :],
                                       start=(half == 0), stop=(half == 1))
                mm.then_inc(sig, 1)

            def pick_rows(l, i):
                b, n = at1(l, "mod", i)
                pe.wait_ge(drained[b], n + 1)
                o, sig = claim(l, "pick", i)
                for m in range(4):
                    mm = pe.matmul(o[:, 2 * m:2 * m + 2], mod_parts[:, m * P:(m + 1) * P], pick, start=True, stop=True)
                mm.then_inc(sig, 1)

            pe.wait_ge(const_in, 16)
            pe.wait_ge(summed, KT - 1)
            mean_squares(0, "ms1", sq, 1, inv_d)
            with pe.Fori(0, L) as l:
                pe.wait_ge(diags, l * 8 + 2)
                spread(l, "bc1", 0)
                w = slab(l, "w_cq", 512)
                o, sig = claim(l, "cq01")
                for m in range(2):
                    for k in range(KT):
                        if m == 0 and k < KT - 1:
                            pe.wait_ge(normed, l * 2 * (KT - 1) + k + 1)
                        if m == 0 and k == KT - 1:
                            taken(l, "bc1")
                        mm = pe.matmul(o[:, m * S:(m + 1) * S], w[:, k, m * P:(m + 1) * P], hl[:, k, :],
                                       start=(k == 0), stop=(k == KT - 1))
                mm.then_inc(sig, 1)
                channels(l, "cq2gk", w, 256, 2, hl)
                w = slab(l, "w_ckv", 512)
                channels(l, "ckv", w, 0, 2, hl)
                o, sig = claim(l, "gv")
                for tb in range(NB):
                    mm = group(o[:, tb * P:(tb + 1) * P], lambda k: hl[:, k, tb * P:(tb + 1) * P],
                               lambda k: w[:, k, 256:384], KT)
                mm.then_inc(sig, 1)
                channels(l, "kr", w, 384, 1, hl)
                w = slab(l, "w_q", 512)
                channels(l, "q0", w, 0, 2, hl)
                channels(l, "q1", w, 256, 2, hl)
                pe.wait_ge(lat_squared, 2 * l + 1)
                mean_squares(l, "ms_q", sq, QT, inv_q)
                pe.wait_ge(lat_squared, 2 * l + 2)
                mean_squares(l, "ms_kv", sq[:, QT:QT + KVT, :], KVT, inv_kv)
                w = slab(l, "w_k", 512)
                channels(l, "k0", w, 0, 2, hl)
                channels(l, "k1", w, 256, 2, hl)
                taken(l, "cq2gk", "kr")
                rotate(l, "Rgk", arena[:, 4096:4608])
                pe.wait_ge(diags, l * 8 + 4)
                spread(l, "bc_q", 0)
                pe.wait_ge(diags, l * 8 + 6)
                spread(l, "bc_kv", 2)
                w = slab(l, "w_v", 512)
                for tb in range(NB):
                    o, sig = claim(l, f"v{tb}")
                    group(o, lambda k: hl[:, k, tb * P:(tb + 1) * P], lambda k: w[:, k, :], KT).then_inc(sig, 1)
                w = slab(l, "w_gq", 512)
                channels(l, "gq0", w, 0, 2, hl)
                channels(l, "gq1", w, 256, 2, hl)
                taken(l, "bc_q")
                w = slab(l, "w_uq", 768, n=QT)
                channels(l, "mqn0", w, 0, 2, cq_s, QT)
                channels(l, "mqn1", w, 256, 2, cq_s, QT)
                channels(l, "mqr", w, 512, 2, cq_s, QT)
                for j in range(2):
                    taken(l, f"gq{j}")
                    rotate(l, f"Rgq{j}", arena[:, 3072 + 512 * j:3584 + 512 * j])
                taken(l, "bc_kv")
                w = slab(l, "w_ukv", 1024, n=KVT)
                channels(l, "mkn0", w, 0, 2, ckv_s, KVT)
                channels(l, "mkn1", w, 256, 2, ckv_s, KVT)
                taken(l, "mqr")
                rotate(l, "Rmqr", arena[:, 7168:7680])
                for tb in range(NB):
                    o, sig = claim(l, f"mv{tb}")
                    group(o, lambda k: ckv_s[:, k, tb * P:(tb + 1) * P], lambda k: w[:, k, 512:1024],
                          KVT).then_inc(sig, 1)

                for i in range(NU1 + 3):
                    if i == 0:
                        taken(l, "q0", "q1", "k0", "k1", "v0", "v1")
                    if i == NA_HEADS:
                        taken(l, "gv")
                        pe.wait_ge(roped, START + 4 * l + 3)
                    if i == NA_HEADS + 8:
                        taken(l, "mqn0", "mqn1", "mkn0", "mkn1", "mv0", "mv1")
                        pe.wait_ge(roped, START + 4 * l + 4)
                    if i < NU1:
                        kind, h = UNITS1[i]
                        o, sig = claim(l, ("S", i))
                        half = slice(64 * (h % 2), 64 * (h % 2) + 64)
                        for qb in range(NB):
                            qs = slice(qb * P, (qb + 1) * P)
                            to = o[:, qb * S:(qb + 1) * S]
                            if kind == "na":
                                mm = pe.matmul(to, q_s[half, h // 2, qs], k_s[half, h // 2, :], start=True, stop=True)
                            elif kind == "gqa":
                                mm = pe.matmul(to, gq_s[half, h // 2, qs], gkr_s[half, 0, :], start=True, stop=True)
                            else:
                                pe.matmul(to, mq_s[:, h, qs], mk_s[:, h, :], start=True, stop=False)
                                mm = pe.matmul(to, mqr_s[half, h // 2, qs], gkr_s[half, 1, :], start=False, stop=True)
                        mm.then_inc(sig, 1)
                    if 0 <= i - 2 < NU1:
                        u = i - 2
                        o, sig = claim(l, ("T", u))
                        pe.wait_ge(prob, l * NU1 + u + 1)
                        for kt in range(NB):
                            for qb in range(NB):
                                mm = pe.transpose(o[:, kt * S + qb * P:kt * S + (qb + 1) * P],
                                                  prob_s[u % 4][:, qb * S + kt * P:qb * S + (kt + 1) * P], ident)
                        mm.then_inc(sig, 1)
                    if 0 <= i - 3 < NU1:
                        u = i - 3
                        kind, h = UNITS1[u]
                        b, n = at1(l, ("Y", u // 2))
                        if u % 2 == 0:
                            pe.wait_ge(drained[b], n)
                        taken(l, ("T", u))
                        for kt in range(NB):
                            pt = pt_s[u % 2][:, kt * S:(kt + 1) * S]
                            half = slice(64 * (h % 2), 64 * (h % 2) + 64)
                            if kind == "mla":
                                to, v = bank(b)[:, (h % 2) * S:(h % 2 + 1) * S], mv_s[:, kt, h * P:(h + 1) * P]
                            elif kind == "na":
                                to, v = psum[half, b, 0:S], v_s[:, kt, h * HD:(h + 1) * HD]
                            else:
                                to, v = psum[half, b, 0:S], gv_s[:, kt, half]
                            mm = pe.matmul(to, v, pt, start=(kt == 0), stop=(kt == NB - 1))
                        if u % 2 == 1:
                            mm.then_inc(full[b], 1)

                with pe.Fori(0, 3) as i:
                    for j in range(2):
                        w = slab(l, ("gate", j), 512, i)
                        for f in range(2):
                            o, sig = claim(l, ("gate", 2 * j + f), i)
                            for m in range(2):
                                mm = group(o[:, m * S:(m + 1) * S],
                                           lambda k: w[:, k, f * 256 + m * P:f * 256 + (m + 1) * P],
                                           lambda k: hl[:, k, :], KT)
                            mm.then_inc(sig, 1)
                for br in range(3):
                    taken(l, *(("Y", j) for j in ((0, 1, 2, 3), (4, 5, 6, 7), (8, 9))[br]))
                    w = slab(l, ("br", br), 1024, n=4)
                    for f in range(4):
                        channels(l, ("br", br, f), w, 256 * f, 2, y_s[br], 4)
                pe.wait_ge(merged_in, 4 * l + 4)
                for j in range(2):
                    w = slab(l, ("out", j), 512)
                    for f in range(2):
                        channels(l, ("out", 2 * j + f), w, 256 * f, 2, merged)
                pe.wait_ge(summed, (2 * l + 2) * (KT - 1))
                mean_squares(l, "ms2", sq, 1, inv_d)
                pe.wait_ge(diags, l * 8 + 8)
                spread(l, "bc2", 0)
                with pe.Fori(0, FT // 2) as i:
                    pe.wait_ge(normed, (2 * l + 2) * (KT - 1))
                    taken(l, "bc2")
                    pe.wait_ge(cond, 1)
                    for j in range(2):
                        w = slab(l, ("up", j), 2 * P, i)
                        o, sig = claim(l, ("up", j), i)
                        for m in range(2):
                            mm = group(o[:, m * S:(m + 1) * S], lambda k: w[:, k, m * P:(m + 1) * P],
                                       lambda k: hl[:, k, :], KT)
                        mm.then_inc(sig, 1)
                        if j == 0:
                            modulate(l, i)
                    pick_rows(l, i)
                modulate(l, FT // 2)
                with pe.Fori(0, KT // 2) as i:
                    for j in range(2):
                        pe.wait_ge(acted[j], START + (l + 1) * (FT // 2))
                    for j in range(2):
                        w = slab(l, ("down", j), P, i, n=FT)
                        o, sig = claim(l, ("down", j), i)
                        group(o[:, 0:S], lambda k: w[:, k, :], lambda k: act_s[:, k, :], FT).then_inc(sig, 1)
                pick_rows(l, FT // 2)
                pe.wait_ge(summed, (2 * l + 3) * (KT - 1))
                mean_squares(l + 1, "ms1", sq, 1, inv_d)
            pe.wait_ge(diags, 8 * L + 2)
            spread(L, "bc1", 0)
            stack2_tensor(pe)

        @block.scalar
        def _(act):
            def wait_full(l, name, i=0):
                b, n = at1(l, name, i)
                act.wait_ge(full[b], n + 1)
                return bank(b), drained[b]

            def take(l, name, dst, n=2 * S, i=0):
                o, sig = wait_full(l, name, i)
                act.activation(dst, o[:, 0:n], ACT.Copy).then_inc(sig, 1)

            def take_root(l, name, c):
                o, sig = wait_full(l, name)
                act.activation(small[:, c:c + 2], o[:, 0:2], ACT.Sqrt, bias=eps_c).then_inc(sig, 1)

            act.wait_ge(x_in, 16)
            for t in range(KT):
                act.activation(sq[:, t, :], xl[:, t, :], ACT.Square).then_inc(squared, 1)
            act.wait_ge(cond_in, 16)
            act.activation(small[:, 96:112], csil[:, 0:16], ACT.Exp, scale=-1.0).then_inc(cond_exp, 1)
            act.wait_ge(const_in, 16)
            with act.Fori(0, L) as l:
                take_root(l, "ms1", 0)
                take(l, "cq01", arena[:, 4864:5376])
                take(l, "ckv", arena[:, 5632:6144])
                b, n = at1(l, "cq2gk")
                act.wait_ge(drained[b], n + 1)
                b, n = at1(l, "cq01")
                act.wait_ge(drained[b], n + 1)
                act.activation(X[:, 0:QT * S], arena[:, 4864:5632], ACT.Square).then_inc(lat_squared, 1)
                b, n = at1(l, "ckv")
                act.wait_ge(drained[b], n + 1)
                act.activation(X[:, QT * S:(QT + KVT) * S], arena[:, 5632:6144], ACT.Square).then_inc(lat_squared, 1)
                take(l, "kr", arena[:, 4352:4608], S)
                take(l, "q0", arena[:, 0:512])
                take_root(l, "ms_q", 2)
                take_root(l, "ms_kv", 4)
                take(l, "k0", arena[:, 1024:1536])
                take(l, "v0", arena[:, 2048:2560])
                take(l, "gq0", arena[:, 3072:3584])
                take(l, "mqn0", arena[:, 6144:6656])
                take(l, "mkn0", arena[:, 8192:8704])
                take(l, "mv0", arena[:, 9216:9728])
                for i in range(NU1 + 3):
                    if i < NU1:
                        kind, h = UNITS1[i]
                        c = 16 + 8 * (i % 4)
                        b, n = at1(l, ("S", i))
                        act.wait_ge(negmax, l * NU1 + i + 1)
                        if kind == "gqa":
                            act.activation(small[:, c + 4:c + 6], small[:, c:c + 2], ACT.Exp,
                                           bias=vA[:, V_SINK + h:V_SINK + h + 1])
                        for qb in range(NB):
                            qs = slice(qb * S, (qb + 1) * S)
                            src = bank(b)[:, qs] if kind == "mla" else prob_s[i % 4][:, qs]
                            e = act.activation(prob_s[i % 4][:, qs], src, ACT.Exp, bias=small[:, c + qb:c + qb + 1],
                                               scale=MLA_SCALE if kind == "mla" else 1.0,
                                               accum_out=small[:, c + 2 + qb:c + 3 + qb])
                        e.then_inc(drained[b] if kind == "mla" else exped, 1)
                    if 0 <= i - 2 < NU1:
                        take(l, ("T", i - 2), pt_s[i % 2])
                    if 0 <= i - 3 < NU1 and (i - 3) % 2 == 1:
                        j = (i - 3) // 2
                        t = j if j < 4 else (j - 4 if j < 8 else 2 * (j - 8))
                        br = min(j // 4, 2)
                        dst = arena[:, 10240 + 1024 * br + t * S:10240 + 1024 * br + t * S + (S if br < 2 else 2 * S)]
                        take(l, ("Y", j), dst, S if br < 2 else 2 * S)
                act.wait_ge(half_bias, l + 1)
                with act.Fori(0, 3) as i:
                    for f in range(4):
                        o, sig = wait_full(l, ("gate", f), i)
                        act.nop()
                        for m in range(2):
                            g = gate_s[:, bass.ds(8 * i + 2 * f + m, 1), :]
                            e = act.activation(g, o[:, m * S:(m + 1) * S].unsqueeze(1), ACT.Tanh, scale=0.5,
                                               bias=derived[:, bass.ds(8 * i + 2 * f + m, 1)])
                        e.then_inc(sig, 1)
                for f in range(4):
                    b, n = at1(l, ("out", f))
                    act.wait_ge(drained[b], n + 1)
                    act.activation(X[:, f * 512:(f + 1) * 512], X[:, KT * S + f * 512:KT * S + (f + 1) * 512],
                                   ACT.Square).then_inc(squared, 1)
                take_root(l, "ms2", 6)
                act.wait_ge(vb_in, 16 * (l + 1))
                with act.Fori(0, FT // 2) as i:
                    for j in range(2):
                        o, _s = wait_full(l, ("up", j), i)
                        act.wait_ge(acted[j], START + l * (FT // 2) + i)
                        act.nop()
                        for m in range(2):
                            ch = FT * m + 2 * i + j
                            e = act.activation(conv_s[j][:, m, :], o[:, m * S:(m + 1) * S], ACT.Identity,
                                               scale=vB[:, bass.ds(V_W0 + 2 * FT + ch, 1)],
                                               bias=vB[:, bass.ds(V_CB + ch, 1)])
                        e.then_inc(tapped, 1)
                        if j == 0:
                            take(l, "mod", mod_parts, i=i)
                    for j in range(2):
                        b, n = at1(l, ("up", j), i)
                        act.wait_ge(drained[b], n + 1)
                        act.activation(gelu_s[j], conv_s[j][:, 1, :], gelu_fn).then_inc(gelued, 1)
                take(l, "mod", mod_parts, i=FT // 2)
                with act.Fori(0, KT // 2) as i:
                    for j in range(2):
                        b, n = at1(l, ("down", j), i)
                        act.wait_ge(drained[b], n + 1)
                        act.nop()
                        act.activation(sq[:, bass.ds(2 * i + j, 1), :], xl[:, bass.ds(2 * i + j, 1), :],
                                       ACT.Square).then_inc(squared, 1)
            take_root(L, "ms1", 0)
            stack2_scalar(act)

        @block.gpsimd
        def _(pool):
            def add_squares(norm, s, arrived):
                for t in range(1, KT):
                    pool.wait_ge(squared, arrived(t))
                    if t > 1:
                        pool.wait_ge(summed, norm * (KT - 1) + t - 1)
                    pool.tensor_tensor(s(0), s(0), s(t), ALU.add).then_inc(summed, 1)

            add_squares(0, lambda t: sq[:, t, :], lambda t: t + 1)
            pool.wait_ge(const_in, 16)
            with pool.Fori(0, L) as l:
                pool.wait_ge(drained[0], START + l * BANK1[0])
                pool.dma_start(biasb[:, :], a["na_bias"][l]).then_inc(bias_in, 16)
                pool.wait_ge(bias_in, 16 * (l + 1))
                pool.nop()
                for h in range(NA_HEADS):
                    for qb in range(NB):
                        b_ = biasb[:, h * 512 + qb * S:h * 512 + (qb + 1) * S]
                        pool.tensor_tensor(b_, b_, namask, ALU.add).then_inc(biased, 1)
                add_squares(2 * l + 1, lambda t: sq[:, t, :], lambda t: 12 * l + 8 + t // 2 + 1)
                with pool.Fori(0, FT // 2) as i:
                    for j in range(2):
                        pool.wait_ge(gelued, l * FT + 2 * i + j + 1)
                        pool.nop()
                        pool.tensor_tensor(act_s[:, bass.ds(2 * i + j, 1), :], gelu_s[j].unsqueeze(1),
                                           conv_s[j][:, 0:1, :], ALU.mult).then_inc(acted[j], 1)
                add_squares(2 * l + 2, lambda t: sq[:, t, :], lambda t: 12 * l + 12 + t + 1)
            stack2_gpsimd(pool, add_squares)

        @block.vector
        def _(vec):
            def wait_full(l, name, i=0):
                b, n = at1(l, name, i)
                vec.wait_ge(full[b], n + 1)
                return bank(b), drained[b]

            def after_own(l, name, i=0):
                b, n = at1(l, name, i)
                vec.wait_ge(drained[b], n + 1)

            def take(l, name, dst, n=2 * S):
                o, sig = wait_full(l, name)
                vec.tensor_copy(dst, o[:, 0:n]).then_inc(sig, 1)

            def factors(l, name, c, d0, step):
                b, n = at1(l, name)
                vec.wait_ge(drained[b], n + 1)
                step.done(vec.reciprocal(small[:, c:c + 2], small[:, c:c + 2]))
                for tb in range(NB):
                    vec.tensor_scalar(diag[:, (d0 + tb) * P:(d0 + tb + 1) * P], ident, small[:, c + tb:c + tb + 1],
                                      None, ALU.mult).then_inc(diags, 1)

            def apply_norm(l, name, dst, src, gains, nt, each=None):
                o, sig = wait_full(l, name)
                for t in range(nt):
                    e = vec.scalar_tensor_tensor(dst[:, t, :], src[:, t, :], gains[:, t:t + 1], o[:, 0:S],
                                                 ALU.mult, ALU.mult)
                    if t == nt - 1:
                        e.then_inc(sig, 1)
                    elif each is not None:
                        e.then_inc(each, 1)

            def rope(l, name, dst, step, nth):
                vec.wait_ge(roped, START + 4 * l + nth)
                o, sig = wait_full(l, name)
                wide = o.rearrange("p (n w) -> p n w", w=S)
                t = tmp_s[0].rearrange("p (n w) -> p n w", w=S)
                vec.tensor_tensor(t, wide, sin1.unsqueeze(1).to_broadcast([P, 2, S]), ALU.mult).then_inc(sig, 1)
                step.done(vec.tensor_tensor(dst, dst, cos1.unsqueeze(1).to_broadcast([P, 2, S]), ALU.mult))
                after_own(l, name)
                vec.tensor_tensor(dst, dst, t, ALU.add).then_inc(roped, 1)

            def add_modulations(l, i):
                o, sig = wait_full(l, "pick", i)
                m = mod[:, bass.ds(l * 2 * MT + 8 * i, 8)]
                vec.tensor_tensor(m, o[:, 0:8], m, ALU.add).then_inc(sig, 1)

            for s in (*full, *drained, *acted, roped):
                vec.sem_inc(s, START)
            vec.wait_ge(const_in, 16)
            vec.wait_ge(x_in, 16)
            vec.wait_ge(mod_in, 16)
            first = Steps(vec, vec_step)
            vec.wait_ge(cond_exp, 1)
            first.done(vec.tensor_scalar(small[:, 96:112], small[:, 96:112], 1.0, None, ALU.add))
            first.done(vec.reciprocal(small[:, 96:112], small[:, 96:112]))
            first.done(vec.memset(arena[:, 15360:15360 + KT * 32], 0.0))
            vec.tensor_tensor(csil_wide[:, :, 0:2], *(t.rearrange("p (k v) -> p k v", v=2)
                                                      for t in (csil[:, 0:16], small[:, 96:112])),
                              ALU.mult).then_inc(cond, 1)
            with vec.Fori(0, L) as l:
                step = Steps(vec, vec_step, l * VEC_STEPS + first.n)
                factors(l, "ms1", 0, 0, step)
                vec.wait_ge(va_in, 16 * (l + 1))
                apply_norm(l, "bc1", hl, xl, vA[:, V_G1:V_G1 + KT], KT, normed)
                o, sig = wait_full(l, "cq2gk")
                step.done(vec.tensor_copy(arena[:, 5376:5632], o[:, 0:S]))
                vec.tensor_copy(arena[:, 4096:4352], o[:, S:2 * S]).then_inc(sig, 1)
                take(l, "gv", arena[:, 4608:4864], S)
                vec.tensor_scalar(derived[:, 0:3 * KT], vA[:, V_BG:V_BG + 3 * KT], 0.5, None,
                                  ALU.mult).then_inc(half_bias, 1)
                step.done(vec.tensor_scalar(derived[:, 32:40], vA[:, V_SINK:V_SINK + 8], -1.0, None, ALU.mult))
                take(l, "q1", arena[:, 512:1024])
                factors(l, "ms_q", 2, 0, step)
                factors(l, "ms_kv", 4, 2, step)
                take(l, "k1", arena[:, 1536:2048])
                b, n = at1(l, "kr")
                vec.wait_ge(drained[b], n + 1)
                rope(l, "Rgk", gkr_s, step, 0)
                apply_norm(l, "bc_q", cq_s, cq_s, vA[:, V_QA:V_QA + QT], QT)
                apply_norm(l, "bc_kv", ckv_s, ckv_s, vA[:, V_KVA:V_KVA + KVT], KVT)
                take(l, "v1", arena[:, 2560:3072])
                take(l, "gq1", arena[:, 3584:4096])
                take(l, "mqn1", arena[:, 6656:7168])
                take(l, "mqr", arena[:, 7168:7680])
                b, n = at1(l, "gq0")
                vec.wait_ge(drained[b], n + 1)
                rope(l, "Rgq0", gq_s[:, 0:2, :], step, 1)
                after_own(l, "gq1")
                rope(l, "Rgq1", gq_s[:, 2:4, :], step, 2)
                take(l, "mkn1", arena[:, 8704:9216])
                after_own(l, "mqr")
                rope(l, "Rmqr", mqr_s, step, 3)
                take(l, "mv1", arena[:, 9728:10240])

                for i in range(NU1 + 1):
                    if i < NU1:
                        kind, h = UNITS1[i]
                        c = 16 + 8 * (i % 4)
                        o, sig = wait_full(l, ("S", i))
                        if i >= 4:
                            b, n = at1(l, ("T", i - 4))
                            vec.wait_ge(full[b], n + 1)
                        src = prob_s[i % 4]
                        if kind == "mla":
                            src = o
                        else:
                            if kind == "na":
                                vec.wait_ge(biased, 2 * (l * NA_HEADS + h + 1))
                            add = bias_s[:, h, :] if kind == "na" else winmask
                            vec.scalar_tensor_tensor(src, o, HD_SCALE, add, ALU.mult, ALU.add).then_inc(sig, 1)
                            after_own(l, ("S", i))
                        step.done(vec.tensor_reduce(small[:, c + 6:c + 8], src.rearrange("p (n w) -> p n w", w=S),
                                                    axis=AX.X, op=ALU.max))
                        if kind == "gqa":
                            e = vec.tensor_scalar(small[:, c:c + 2], small[:, c + 6:c + 8], -1.0,
                                                  derived[:, 32 + h:33 + h], ALU.mult, ALU.min)
                        else:
                            e = vec.tensor_scalar(small[:, c:c + 2], small[:, c + 6:c + 8],
                                                  -1.0 if kind == "na" else -MLA_SCALE, None, ALU.mult)
                        e.then_inc(negmax, 1)
                    if i >= 1:
                        u = i - 1
                        kind, h = UNITS1[u]
                        c = 16 + 8 * (u % 4)
                        b, n = at1(l, ("S", u))
                        if kind == "mla":
                            vec.wait_ge(drained[b], n + 1)
                        else:
                            vec.wait_ge(exped, l * (NA_HEADS + 8) + u + 1)
                        if kind == "gqa":
                            step.done(vec.tensor_tensor(small[:, c + 2:c + 4], small[:, c + 2:c + 4],
                                                        small[:, c + 4:c + 6], ALU.add))
                        step.done(vec.reciprocal(small[:, c + 2:c + 4], small[:, c + 2:c + 4]))
                        for qb in range(NB):
                            qs = slice(qb * S, (qb + 1) * S)
                            e = vec.tensor_scalar(prob_s[u % 4][:, qs], prob_s[u % 4][:, qs],
                                                  small[:, c + 2 + qb:c + 3 + qb], None, ALU.mult)
                        e.then_inc(prob, 1)

                for br in range(3):
                    for f in range(4):
                        if br == 0:
                            b, n = at1(l, ("gate", f))
                            vec.wait_ge(drained[b], n + 3)
                        o, sig = wait_full(l, ("br", br, f))
                        g = arena[:, (KT * br + 2 * f) * S:(KT * br + 2 * f + 2) * S]
                        m = H[:, f * 512:(f + 1) * 512]
                        t = m if br == 0 else tmp_s[f % 2]
                        vec.scalar_tensor_tensor(t, g, 1.0, o, ALU.add, ALU.mult).then_inc(sig, 1)
                        after_own(l, ("br", br, f))
                        if br == 1:
                            step.done(vec.tensor_tensor(m, m, t, ALU.add))
                        elif br == 2:
                            vec.tensor_tensor(m, m, t, ALU.add).then_inc(merged_in, 1)
                for f in range(4):
                    o, sig = wait_full(l, ("out", f))
                    x2 = X[:, KT * S + f * 512:KT * S + (f + 1) * 512]
                    vec.scalar_tensor_tensor(x2, o, 0.5, x2, ALU.mult, ALU.add).then_inc(sig, 1)
                vec.wait_ge(vb_in, 16 * (l + 1))
                factors(l, "ms2", 6, 0, step)
                apply_norm(l, "bc2", hl, xl, vB[:, V_G2:V_G2 + KT], KT, normed)
                assert step.n == VEC_STEPS, step.n

                with vec.Fori(0, FT // 2) as i:
                    taps = Steps(vec, conv_step, (l * (FT // 2) + i) * 6)
                    for j in range(2):
                        o, sig = wait_full(l, ("up", j), i)
                        vec.wait_ge(tapped, l * FT + 2 * i + j + 1)
                        for m in range(2):
                            ch = FT * m + 2 * i + j
                            w0, w2 = (vB[:, bass.ds(V_W0 + 2 * FT * k + ch, 1)] for k in (0, 2))
                            c = conv_s[j][:, m, :]
                            ps = o[:, m * S:(m + 1) * S]
                            taps.done(vec.scalar_tensor_tensor(c[:, 1:S], ps[:, 0:S - 1], w0, c[:, 1:S],
                                                               ALU.mult, ALU.add))
                            e = vec.scalar_tensor_tensor(c[:, 0:S - 1], ps[:, 1:S], w2, c[:, 0:S - 1],
                                                         ALU.mult, ALU.add)
                            if m == 0:
                                taps.done(e)
                        e.then_inc(sig, 1)
                    add_modulations(l, i)
                with vec.Fori(0, KT // 2) as i:
                    for j in range(2):
                        o, sig = wait_full(l, ("down", j), i)
                        x1 = xl[:, bass.ds(2 * i + j, 1), :]
                        vec.tensor_tensor(x1, o[:, 0:S].unsqueeze(1), x1, ALU.add).then_inc(sig, 1)
                add_modulations(l, FT // 2)
            final = Steps(vec, vec_step, L * VEC_STEPS + first.n)
            factors(L, "ms1", 0, 0, final)
            b, n = at1(L, "bc1")
            vec.wait_ge(fg_in, 16)
            apply_norm(L, "bc1", xl, xl, uvec[:, 0:KT], KT)
            stack2_vector(vec)


def layouts(inputs):
    i = {k: np.asarray(v) for k, v in inputs.items()}

    def slab(w):
        *lead, k, n = w.shape
        w = w.reshape(*lead, k // P, P, n)
        return np.ascontiguousarray(np.swapaxes(w, -3, -2)).reshape(*lead, P, (k // P) * n)

    def slabs(w, width):
        return np.stack([slab(w[:, :, c:c + width]) for c in range(0, w.shape[2], width)], axis=1)

    def columns(v):
        return np.swapaxes(v.reshape(*v.shape[:-1], -1, P), -1, -2)

    a = {}
    w = i["w_in"]
    q, k, v, cq, ckv, kr, gq, gkv, gate = np.split(
        w, np.cumsum([512, 512, 512, Q_RANK, KV_RANK, ROPE, 512, 256]).tolist(), axis=2)
    perm = np.arange(8).reshape(2, 4).T.ravel()
    gq = gq.reshape(L, D, 8, HD)[:, :, perm].reshape(L, D, 512)
    a["w_proj"] = np.stack([slab(x) for x in (
        np.concatenate([cq, gkv[..., :P]], 2), np.concatenate([ckv, gkv[..., P:], kr, kr], 2), q, k, v, gq)], axis=1)
    a["w_gate"] = slabs(gate, 512)
    uq = i["mla_w_uq"].reshape(L, Q_RANK, MLA_HEADS, NOPE + ROPE)
    a["w_uq"] = slab(np.concatenate([uq[..., :NOPE].reshape(L, Q_RANK, -1), uq[..., NOPE:].reshape(L, Q_RANK, -1)], 2))
    ukv = i["mla_w_ukv"].reshape(L, KV_RANK, MLA_HEADS, NOPE + VD)
    a["w_ukv"] = slab(np.concatenate([ukv[..., :NOPE].reshape(L, KV_RANK, -1), ukv[..., NOPE:].reshape(L, KV_RANK, -1)], 2))
    brg = i["w_br_gqa"].reshape(L, 8, HD, D)[:, perm].reshape(L, 512, D)
    a["w_br"] = np.stack([slab(x) for x in (i["w_br_na"], brg, i["w_br_mla"])], axis=1)
    a["w_out"] = slabs(i["w_out"], 512)
    up = i["w_up"].reshape(L, D, 2, FT, P).transpose(0, 1, 3, 2, 4).reshape(L, D, 2 * FF)
    a["w_up"] = slabs(up, 2 * P)
    a["w_down"] = slabs(i["w_down"], P)
    a["w_mod"] = slabs(i["w_mod_2"], 512)
    bg = columns(i["b_gate"])
    bg = bg.reshape(L, P, 3, KT)[:, :, [0, 2, 1]].reshape(L, P, 3 * KT)
    a["w_gate"] = a["w_gate"].reshape(L, 3, 2, P, 4096)[:, [0, 2, 1]].reshape(L, 6, P, 4096)
    sink = np.broadcast_to(i["gqa_sink"][:, None, perm], (L, P, 8))
    a["vecA"] = np.concatenate([columns(i["norm1_g"]), bg, columns(i["mla_qa_g"]), columns(i["mla_kva_g"]), sink], 2)
    a["vecB"] = np.concatenate([columns(i["norm2_g"])] + [columns(i["conv_w"][:, t]) for t in range(3)]
                               + [columns(i["conv_b"])], 2)
    r, c = np.arange(S) // GRID, np.arange(S) % GRID
    rows = r[None, :] - r[:, None] + WIN_R - 1
    cols = np.clip(c[None, :] - c[:, None] + WIN_C - 1, 0, 2 * WIN_C - 2)
    bias = i["na_rpb"][:, :, rows, cols]
    a["na_bias"] = bias.reshape(L, NA_HEADS, NB, P, S).transpose(0, 3, 1, 2, 4).reshape(L, P, -1)
    a["xT"] = slab(i["x"][0].T)
    a["ctxT"] = slab(i["ctx_2"][0].T)
    a["condT"] = np.stack([columns(i["c_ctx_2"]), columns(i["c_2"][0])], -1).reshape(P, 2 * KT)
    bm = columns(i["b_mod_2"]).transpose(1, 0, 2)
    a["b_mod"] = np.stack([bm, bm], -1).reshape(P, -1)
    a["uvec"] = np.concatenate([columns(i["final_g"])] + [
        np.concatenate([columns(i["norm1_g_2"][l]), columns(i["norm2_g_2"][l]),
                        np.tile(i["q_norm_g_2"][l], 2)[:, None], np.tile(i["k_norm_g_2"][l], 2)[:, None],
                        columns(i["gmlp_norm_g_2"][l])], 1) for l in range(L)], 1)
    w = i["w_in_2"]
    q, k, v, u, vg = np.split(w, [512, 640, 768, 1280], axis=2)
    a["w2_q"] = slab(q.reshape(L, D, 8, HD)[:, :, perm].reshape(L, D, 512))
    a["w2_kv"], a["w2_u"], a["w2_vg"] = slab(np.concatenate([k, v], 2)), slab(u), slab(vg)
    wo = i["w_out_2"]
    wo = np.concatenate([wo[:, :512].reshape(L, 8, HD, D)[:, perm].reshape(L, 512, D), wo[:, 512:]], 1)
    a["w2_out"], a["w2_ff1"], a["w2_ff2"] = slabs(wo, 512), slabs(i["w_ff1_2"], 512), slabs(i["w_ff2_2"], P)
    ws = i["w_spatial_2"].transpose(0, 3, 1, 2).reshape(L, P, 4 * P)
    bs = np.broadcast_to(i["b_spatial_2"].reshape(L, 1, 4 * P), (L, P, 4 * P))
    a["spatial"] = np.concatenate([ws, bs], 2)
    a["const"] = constants()
    return {k: np.ascontiguousarray(v) for k, v in a.items()}


def constants():
    c = np.zeros((P, N_CONST), np.float32)
    p, s = np.arange(P), np.arange(S)
    c[:, C_ID:C_ID + P] = np.eye(P)
    c[:, C_ONE:C_ONE + P] = 1
    for at, h in ((C_ROT1, 32), (C_ROT2, 16)):
        for m in range(P):
            if m % (2 * h) < h:
                c[m + h, at + m] = -1
            else:
                c[m - h, at + m] = 1
    c[:, C_HEAD:C_HEAD + P] = (p[:, None] // HD == p[None, :] // HD) / HD
    f32 = np.float32
    inv = f32(1) / (f32(THETA) ** (np.arange(0, HD, 2, dtype=f32) / f32(HD)))
    ang = s.astype(f32)[None, :] * inv[p % 32][:, None]
    c[:, C_COS1:C_COS1 + S], c[:, C_SIN1:C_SIN1 + S] = np.cos(ang), np.sin(ang)
    n = HD // 4
    inv = f32(THETA) ** (-np.arange(n, dtype=f32) / f32(n))
    pos = np.where((p % HD < 32)[:, None], (s // GRID)[None, :], (s % GRID)[None, :]).astype(f32)
    ang = pos * inv[p % n][:, None]
    c[:, C_COS2:C_COS2 + S], c[:, C_SIN2:C_SIN2 + S] = np.cos(ang), np.sin(ang)
    for qb in range(NB):
        far = np.abs((qb * P + p)[:, None] - s[None, :]) > GQA_WINDOW
        c[:, C_WIN + qb * S:C_WIN + (qb + 1) * S] = np.where(far, NEG, 0)
    qc, kc = (p % GRID)[:, None], (s % GRID)[None, :]
    start = np.clip(qc - WIN_C // 2, 0, GRID - WIN_C)
    c[:, C_NA:C_NA + S] = np.where((kc >= start) & (kc < start + WIN_C), 0, NEG)
    c[:, C_INV], c[:, C_INV + 1], c[:, C_INV + 2], c[:, C_INV + 3] = 1 / D, 1 / Q_RANK, 1 / KV_RANK, EPS
    for v in range(2):
        c[v::32, C_PICK + v] = 1
    return c


def kernel(**inputs):
    import concourse.bacc as bacc
    from concourse.bass_utils import run_bass_kernel_spmd

    nc = bacc.Bacc("TRN2", target_bir_lowering=False, num_devices=1)
    arrays = layouts(inputs)
    aps = {k: nc.dram_tensor(f"in_{k}", v.shape, mybir.dt.float32, kind="ExternalInput").ap() for k, v in arrays.items()}
    out = nc.dram_tensor("out_xT", (P, KT * S), mybir.dt.float32, kind="ExternalOutput").ap()
    build(nc, aps, out)
    r = run_bass_kernel_spmd(nc, [{f"in_{k}": v for k, v in arrays.items()}], core_ids=[0])
    y = r.results[0]["out_xT"].reshape(P, KT, S)
    return np.ascontiguousarray(y.transpose(2, 1, 0).reshape(1, S, D))
```

```python
import math
from contextlib import ExitStack

import numpy as np

import concourse.bass as bass
from concourse import mybir

P = 128
D = 1024
S = 256
L = 2
KT = D // P
NB = S // P
EPS = 1e-6
NEG = -1e30
THETA = 10000.0
GRID = 64

NA_HEADS, HD = 8, 64
NA_ROWS = S // GRID
WIN_R, WIN_C = 8, 16
MLA_HEADS, Q_RANK, KV_RANK, NOPE, ROPE, VD = 4, 384, 256, 128, 64, 128
QT, KVT = Q_RANK // P, KV_RANK // P
MLA_SCALE = (NOPE + ROPE) ** -0.5
HD_SCALE = HD ** -0.5
GQA_WINDOW = 128
FF = 2816
FT = FF // P
FF2 = 4096
FT2 = FF2 // P
N_MOD = 6
MT = N_MOD * KT
NM = N_MOD * D // 512

SLAB, SLOTS = 2048, 4
SLAB_UQ, SLAB_DOWN = QT * 2 * P, FT // 2 * P
N_UQ = 12
N_UKV = N_UQ + 3
N_GATE = N_UKV + 1
N_BR = N_GATE + 12
N_OUT = N_BR + 6
N_UP = N_OUT + 4
N_DOWN = N_UP + FT
SLABS1 = N_DOWN + 2 * KT
assert SLABS1 % SLOTS == 0
M_Q, M_KV, M_VG, M_U, M_OUT, M_FF = 0, 2, 3, 5, 7, 11
SLABS2 = M_FF + 32
N_ALL = L * (SLABS1 + SLABS2)

C_ID, C_ONE, C_ROT1, C_ROT2, C_HEAD = 0, 128, 256, 384, 512
C_COS1, C_SIN1, C_COS2, C_SIN2 = 640, 896, 1152, 1408
C_WIN, C_NA, C_INV, C_PICK = 1664, 2176, 2432, 2436
N_CONST = C_PICK + 2
V_G1, V_BG, V_QA, V_KVA, V_SINK = 0, 8, 32, 35, 37
N_VA = 45
V_G2, V_W0, V_CB = 0, 8, 8 + 3 * 2 * FT
N_VB = V_CB + 2 * FT
U_G1, U_G2, U_QG, U_KG, U_GG = 0, 8, 16, 17, 18
N_U = 22


def number(order):
    count, out = {}, {}
    for name, place, times in order:
        out[name] = (place, count.get(place, 0))
        count[place] = count.get(place, 0) + times
    return out, count


UNITS1 = [("na", h) for h in range(NA_HEADS)] + [("gqa", j) for j in range(8)] + [("mla", h) for h in range(MLA_HEADS)]
NU1 = len(UNITS1)


def fills_1():
    names = ["cq0", "cq1", "cq2gk", "ckv", "gv", "kr", "q0", "q1", "ms_q", "ms_kv", "k0", "k1", "Rgk", "bc_q", "bc_kv",
             "v0", "v1", "gq0", "gq1", "mqn0", "mqn1", "mqr", "Rgq0", "Rgq1", "mkn0", "mkn1", "Rmqr", "mv0", "mv1"]
    order = [("ms1", 7, 1), ("bc1", 6, 1)]
    order += [(n, i % 8, 1) for i, n in enumerate(names)]
    for i in range(NU1):
        order += [(("S", i), (0, 1)[i % 2], 1), (("T", i), (3, 4)[i % 2], 1)]
        if i % 2 == 0:
            order += [(("Y", i // 2), (5, 6)[(i // 2) % 2], 1)]
    for f in range(NM):
        order += [(("mod", f), 7, 1)]
        order += [(("pick", f), 2, 1)] if f < NM - 1 else []
    order += [(("gate", b), b, 3) for b in range(4)] + [(("pick", NM - 1), 2, 1)]
    order += [(("br", b, f), 4 + f % 4, 1) for b in range(3) for f in range(4)]
    order += [(("out", f), f, 1) for f in range(4)]
    order += [("ms2", 4, 1), ("bc2", 5, 1)]
    order += [(("up", j), (6, 7, 0, 1)[j], len(range(j, FT, 4))) for j in range(4)]
    order += [(("down", j), 2 + j, KT // 2) for j in range(2)]
    return number(order)


START = 1
FILL1, BANK1 = fills_1()

VEC_STEPS = 4 + 4 + 2 + 2 * NU1 + 8 + 4

UNITS2 = [[("ctx", j // 2, j % 2, 0) for j in range(8)], []]
for _l in range(L):
    UNITS2[_l] = UNITS2[_l] + [("lat", j // 4, j % 2, (j % 4) // 2) for j in range(16)]
Y2 = [[(j // 2, j % 2 == 0, j % 2 == 1) for j in range(8)] + [(4 + j // 4, j % 4 == 0, j % 4 == 3) for j in range(16)],
      [(j // 4, j % 4 == 0, j % 4 == 3) for j in range(16)]]


def fills_2():
    order = [("ms_f", 7, 1), ("bc_f", 6, 1)]
    for l in range(L):
        names = [("ms", 0), ("bc", 0)] + [("q", m) for m in range(4)] + [("k",), ("v", 0), ("v", 1)]
        names += [("hm", m) for m in range(5)] + [("vg", j, c) for j in range(2) for c in ((0, 1) if l == 0 else (1,))]
        names += [("u", 0), ("u", 1)] + [("rot", m) for m in range(3)] + [("u", 2), ("u", 3)]
        order += [((l, *n), i % 8, 1) for i, n in enumerate(names)]
        for i in range(len(UNITS2[l])):
            order += [((l, "S", i), (0, 1, 2)[i % 3], 1), ((l, "T", i), (3, 4)[i % 2], 1)]
        order += [((l, "Y", y), (5, 6)[y % 2], 1) for y in range(Y2[l][-1][0] + 1)]
        order += [((l, "sp", g), 7, 1) for g in range(4)]
        order += [((l, "out", m), m, 1) for m in range(KT)]
        order += [((l, "ms", 1), 7, 1), ((l, "bc", 1), 6, 1)]
        for half in range(2):
            order += [((l, "f1", m, half), m, 2) for m in range(8)]
            order += [((l, "f2", j, half), j, 2) for j in range(4)]
    return number(order)


FILL2, _ = fills_2()
DIAGS2 = {(0, 0): 8 * L + 2, (0, 1): 8 * L + 6, (1, 0): 8 * L + 10, (1, 1): 8 * L + 14}
MODDED2 = {(0, 0): 0, (0, 1): 2 * KT - 1, (1, 0): 2 * (2 * KT - 1), (1, 1): 3 * (2 * KT - 1)}


class Steps:

    def __init__(self, eng, sem, base=0):
        self.eng, self.sem, self.base, self.n = eng, sem, base, 0

    def done(self, instruction):
        instruction.then_inc(self.sem, 1)
        self.n += 1
        self.eng.wait_ge(self.sem, self.base + self.n)


def build(nc, a, out):
    f32, f32r = mybir.dt.float32, mybir.dt.float32r
    ALU = mybir.AluOpType
    ACT = mybir.ActivationFunctionType
    AX = mybir.AxisListType

    with ExitStack() as ctx:
        def sb(name, n):
            return ctx.enter_context(nc.sbuf_tensor(name, [P, n], f32))

        def sb_both(name, n):
            with nc.sbuf_tensor(name + "_f32", [P, n], f32) as plain:
                pass
            return plain, ctx.enter_context(nc.sbuf_tensor(name, [P, n], f32r))

        def plain(rounded_part):
            return rounded_part.bitcast(f32)

        def sem(name):
            return ctx.enter_context(nc.semaphore(name))


        X = sb("X", 2 * KT * S)
        H, Hr = sb_both("H", 4 * KT * S)
        rests, rests_r = sb_both("rests", SLOTS * SLAB)
        highs_r = ctx.enter_context(nc.sbuf_tensor("highs", [P, SLOTS * SLAB], f32r))
        arena, arena_r = sb_both("arena", 16384)
        spare = sb("spare", 2 * SLAB)
        con = sb("con", N_CONST)
        vA = sb("vA", N_VA)
        vB = sb("vB", N_VB)
        derived = sb("derived", 40)
        small = sb("small", 128)
        diag = sb("diag", 4 * P)
        mod_parts = diag[:, :]
        mod = sb("mod", L * MT * 2)
        csil = sb("csil", 2 * KT)

        def tiles(t, at, n, w=S):
            return t[:, at:at + n * w].rearrange("p (n w) -> p n w", w=w)

        def part(t, c, rest):
            return tiles(t, (2 * c + rest) * KT * S, KT)

        xl = tiles(X, KT * S, KT)
        hl_raw, hl_low = part(H, 1, 1), part(Hr, 1, 1)
        hl = part(Hr, 1, 0), hl_low
        ident, ones = con[:, C_ID:C_ID + P], con[:, C_ONE:C_ONE + P]
        rot1, rot2, headones = con[:, C_ROT1:C_ROT1 + P], con[:, C_ROT2:C_ROT2 + P], con[:, C_HEAD:C_HEAD + P]
        cos1, sin1 = con[:, C_COS1:C_COS1 + S], con[:, C_SIN1:C_SIN1 + S]
        cos2, sin2 = con[:, C_COS2:C_COS2 + S], con[:, C_SIN2:C_SIN2 + S]
        winmask = con[:, C_WIN:C_WIN + 2 * S]
        namask = con[:, C_NA:C_NA + S]
        pick = con[:, C_PICK:C_PICK + 2]
        inv_d, inv_q, inv_kv, eps_c = (con[:, C_INV + i:C_INV + i + 1] for i in range(4))

        q_s, k_s = tiles(arena, 0, 4), tiles(arena, 1024, 4)
        v_s = tiles(arena, 2048, NB, 512)
        gq_s = tiles(arena, 3072, 4)
        gkr_s = tiles(arena, 4096, 2)
        gv_s = tiles(arena, 4608, NB, P)
        cq_s, ckv_s = tiles(arena, 4864, QT), tiles(arena, 5632, KVT)
        cq_p = tiles(arena_r, 9728, QT), tiles(arena_r, 4864, QT)
        ckv_p = tiles(arena_r, 9728 + QT * S, KVT), tiles(arena_r, 5632, KVT)
        mq_s, mqr_s, mk_s = tiles(arena, 6144, 4), tiles(arena, 7168, 2), tiles(arena, 7680, 4)
        mv_s = tiles(arena, 8704, NB, 512)
        pt_s = [arena[:, 4864 + 512 * i:5376 + 512 * i] for i in range(2)]
        y_at = [9728 + 2048 * b for b in range(3)]
        y_p = [(tiles(arena_r, at, 4), tiles(arena_r, at + 1024, 4)) for at in y_at]
        rope_tmp = arena[:, 15360:15872]
        csil_wide = tiles(arena, 15872, KT, 32)
        gate_s = tiles(arena, 0, 3 * KT)
        tmp_s = [arena[:, 6144 + 512 * i:6656 + 512 * i] for i in range(2)]
        MERGED, MERGED_HIGH = 7168, 0
        merged_p = tiles(arena_r, MERGED_HIGH, KT), tiles(arena_r, MERGED, KT)
        ACTED = FT * S
        act_p = tiles(arena_r, 0, FT), tiles(arena_r, ACTED, FT)
        act_raw = tiles(arena, ACTED, FT)
        conv_s = [tiles(arena, 11264 + 512 * j, 2) for j in range(2)]
        gelu_s = [arena[:, 12288 + 256 * j:12544 + 256 * j] for j in range(2)]
        sq = tiles(X, 0, KT)
        prob_s = [X[:, 512 * i:512 * i + 512] for i in range(4)]
        bias_s = tiles(H, 0, NA_HEADS, 512)
        mod_slab = [tiles(spare, 2048 * h, 4, 512) for h in range(2)]

        psum = ctx.enter_context(nc.psum_tensor("psum", [P, 8, 512], f32))

        full = [sem(f"full{b}") for b in range(8)]
        drained = [sem(f"drained{b}") for b in range(8)]
        loaded = [sem(f"loaded{s}") for s in range(SLOTS)]
        rounded = sem("rounded")
        split = sem("split")
        begun = sem("begun")
        mod_loaded = [sem(f"mod_loaded{h}") for h in range(2)]
        mod_half = sem("mod_half")
        const_in, x_in, va_in, vb_in, bias_in = sem("const_in"), sem("x_in"), sem("va_in"), sem("vb_in"), sem("bias_in")
        cond_in = sem("cond_in")
        squared = sem("squared")
        summed = sem("summed")
        diags = sem("diags")
        normed = sem("normed")
        h_rounded, h_split = sem("h_rounded"), sem("h_split")
        lat_rounded, lat_split = sem("lat_rounded"), sem("lat_split")
        y_rounded = sem("y_rounded")
        lat_squared = sem("lat_squared")
        roped = sem("roped")
        biased = sem("biased")
        negmax = sem("negmax")
        exped = sem("exped")
        prob = sem("prob")
        half_bias = sem("half_bias")
        merged_in = sem("merged_in")
        merged_rounded, merged_split = sem("merged_rounded"), sem("merged_split")
        tapped = sem("tapped")
        gelued = sem("gelued")
        pool_step = sem("pool_step")
        acted = sem("acted")
        cond_exp, cond = sem("cond_exp"), sem("cond")
        vec_step, conv_step = sem("vec_step"), sem("conv_step")
        stored = sem("stored")

        fg_in, mod_in = sem("fg_in"), sem("mod_in")
        uvec = sb("uvec", L * N_U + KT)

        def at1(l, name, i=0):
            b, n = FILL1[name]
            return b, START + l * BANK1[b] + n + i

        def bank(b):
            return psum[:, b, :]

        def slab_no(l, m, i=0):
            return SLABS1 * l + m + SLOTS * i

        def in_slot(t, m, n=SLAB):
            return t[:, (m % SLOTS) * SLAB:(m % SLOTS) * SLAB + n]

        def round_slab(act, l, m, i=0, n=SLAB):
            act.wait_ge(loaded[m % SLOTS], 16 * (SLABS1 // SLOTS * l + m // SLOTS + i + 1))
            act.activation(in_slot(highs_r, m, n), in_slot(rests, m, n), ACT.Copy).then_inc(rounded, 1)

        def split_slab(vec, l, m, i=0, n=SLAB):
            vec.wait_ge(rounded, slab_no(l, m, i) + 1)
            vec.tensor_tensor(in_slot(rests_r, m, n), in_slot(rests, m, n), plain(in_slot(highs_r, m, n)),
                              ALU.subtract).then_inc(split, 1)

        def y_place(j):
            if j < 8:
                return y_at[j // 4] + j % 4 * S, S
            return y_at[2] + (j - 8) * 2 * S, 2 * S

        def slab_size(m, i=0):
            m += SLOTS * i if isinstance(i, int) else 0
            if N_UQ <= m < N_UKV:
                return SLAB_UQ
            return SLAB_DOWN if N_DOWN <= m < SLABS1 else SLAB

        X2, sq2 = (t[:, :].rearrange("p (c t w) -> p c t w", c=2, w=S) for t in (X, spare))
        Hf, Hq = (t[:, :].rearrange("p (c r t w) -> p c r t w", c=2, r=2, w=S) for t in (H, Hr))
        h_raw = Hf[:, :, 1]
        h_p = Hq[:, :, 0], Hq[:, :, 1]
        q2, k2 = tiles(arena, 0, 4, 2 * S), arena[:, 2048:2560]
        v2 = tiles(arena, 2560, 2 * NB, P)
        u2 = tiles(arena, 3072, 4, 2 * S)
        vg2 = tiles(arena, 5120, 2 * NB, 512)
        root2 = [arena[:, 7168 + 512 * i:7680 + 512 * i] for i in range(5)]
        hsq2 = [arena[:, 9728 + 512 * i:10240 + 512 * i] for i in range(5)]
        prob2 = [arena[:, 7168 + 512 * i:7680 + 512 * i] for i in range(4)]
        pt2 = [arena[:, 9216 + 512 * i:9728 + 512 * i] for i in range(2)]
        tmp2 = [arena[:, 12288 + 512 * i:12800 + 512 * i] for i in range(2)]
        ws2, bs2 = tiles(arena, 13824, 4, P), tiles(arena, 14336, 4, P)
        stats = sb("stats", 16 * 6)
        aggr = sb("aggr", 16 * 2)

        ws_in, ctx_in = sem("ws_in"), sem("ctx_in")
        modded = sem("modded")
        headed = sem("headed")
        spread_v = sem("spread_v")
        levelled_stats = sem("levelled_stats")
        y2_rounded = sem("y2_rounded")
        ctx_shifted = sem("ctx_shifted")
        ctx_split = sem("ctx_split")
        lat_squares, lat_summed = sem("lat_squares"), sem("lat_summed")
        gated2 = sem("gated2")
        gated_rounded, gated_split = sem("gated_rounded"), sem("gated_split")
        levelled = sem("levelled")
        acted2 = sem("acted2")

        def parts(l, both=False):
            return (0, 1) if l == 0 or both else (1,)

        def at2(name, i=0):
            b, n = FILL2[name]
            return b, START + L * BANK1[b] + n + i

        def act_tile(t, l, i, m, rest):
            w = 2 * S if l == 0 else S
            return tiles(t, rest * FT2 // 2 * w, FT2 // 2, w)[:, bass.ds(8 * i + m, 1), :]

        def modulation(l, which, t, part):
            return mod[:, l * 2 * MT + (which * KT + t) * 2 + part:l * 2 * MT + (which * KT + t) * 2 + part + 1]

        def gain(l, norm, t, part):
            c = (2 * l + norm) * 16 + 2 * t + part
            return gains2[:, c:c + 1]

        gains2 = sb("gains2", 64)
        uv = [uvec[:, KT + N_U * l:KT + N_U * (l + 1)] for l in range(L)]

        def stack2_sync(sp, load):
            def load2(l, m, src, i=0):
                load(L, SLABS2 * l + m, src, i, SLAB)

            for l in range(L):
                if l == 0:
                    load2(l, 0, a["w2_in"][l, 0])
                    load2(l, 1, a["w2_in"][l, 1])
                    b, n = at2("ms_f")
                    sp.wait_ge(full[b], n + 1)
                    sp.dma_start(X[:, 0:KT * S], a["ctxT"]).then_inc(ctx_in, 16)
                else:
                    load2(l, 0, a["w2_in"][l, 0])
                    load2(l, 1, a["w2_in"][l, 1])
                    b, n = at2((0, "f2", 3, 1))
                    sp.wait_ge(full[b], n + 2)
                sp.dma_start(arena[:, 13824:14848], a["spatial"][l]).then_inc(ws_in, 16)
                for m in range(2, M_OUT):
                    load2(l, m, a["w2_in"][l, m])
                for m in range(4):
                    load2(l, M_OUT + m, a["w2_out"][l, m])
                for half in range(2):
                    for stage in range(2):
                        with sp.Fori(0, 2) as i:
                            for j in range(4):
                                load2(l, M_FF + 16 * half + 8 * stage + j, a["w2_ff"][l, half, stage, 4 * i + j], i)
            for j in range(4):
                b, n = at2((L - 1, "f2", j, 1))
                sp.wait_ge(drained[b], n + 2)
            sp.dma_start(out, X[:, KT * S:2 * KT * S]).then_inc(stored, 16)
            sp.wait_ge(stored, 16)

        def stack2_tensor(pe, slab, group, two_groups):
            def claim(name, i=0):
                b, n = at2(name, i)
                pe.wait_ge(drained[b], n)
                return bank(b), full[b]

            def taken(*names):
                last = {}
                for name in names:
                    b, n = at2(name)
                    last[b] = max(last.get(b, 0), n + 1)
                for b, n in last.items():
                    pe.wait_ge(drained[b], n)

            def slab2(l, m, width=2 * P, i=0, nk=KT):
                return slab(L, SLABS2 * l + m, width, i, nk)

            def of(w, c0, n=P):
                return [lambda k, t=t: t[:, k, c0:c0 + n] for t in w]

            def input_of(c, tb=None):
                if tb is None:
                    return [lambda k, t=t: t[:, c, k, :] for t in h_p]
                return [lambda k, t=t: t[:, c, k, tb * P:(tb + 1) * P] for t in h_p]

            def two_tiles(l, names, w, i=0, wait=None):
                now, width = cols(l)
                if wait:
                    (o0, sig0), (o1, sig1) = (claim((l, *name), i) for name in names)
                    mm0, mm1 = two_groups((o0[:, 0:width], o1[:, 0:width]), (of(w, 0), of(w, P)), input_of(now), KT, wait)
                    mm0.then_inc(sig0, 1)
                    mm1.then_inc(sig1, 1)
                    return
                for m in range(2):
                    o, sig = claim((l, *names[m]), i)
                    group(o[:, 0:width], of(w, m * P), input_of(now), KT, begins=(m == 0)).then_inc(sig, 1)

            def mean_squares(l, norm):
                o, sig = claim((l, "ms", norm))
                pe.wait_ge(summed, (2 * L + 2 * l + norm + 2) * (KT - 1))
                if (l, norm) == (0, 0):
                    pe.wait_ge(lat_summed, KT - 1)
                for c in parts(l, norm == 0):
                    for tb in range(NB):
                        mm = pe.matmul(o[:, c * NB + tb:c * NB + tb + 1], sq2[:, c, 0, tb * P:(tb + 1) * P], inv_d,
                                       start=True, stop=True)
                mm.then_inc(sig, 1)

            def spread_factors(l, norm):
                o, sig = claim((l, "bc", norm))
                pe.wait_ge(diags, DIAGS2[l, norm] + NB * len(parts(l, norm == 0)))
                for c in parts(l, norm == 0):
                    for tb in range(NB):
                        d = c * NB + tb
                        mm = pe.matmul(o[:, d * P:(d + 1) * P], ones, diag[:, d * P:(d + 1) * P], start=True, stop=True)
                mm.then_inc(sig, 1)

            def input_ready(l, norm, k):
                pe.wait_ge(h_split, 2 * L * KT + (2 * l + norm) * KT + k + 1)
                if norm == 0 or l == 0:
                    pe.wait_ge(ctx_split, (2 * l + norm) * KT + k + 1)

            def cols(l, both=False):
                return (slice(0, 2), 2 * S) if l == 0 or both else (slice(1, 2), S)

            for l in range(L):
                mean_squares(l, 0)
                spread_factors(l, 0)
                now, w = cols(l)
                two_tiles(l, [("q", 0), ("q", 1)], slab2(l, M_Q),
                          wait=lambda k: input_ready(l, 0, k))
                two_tiles(l, [("q", 2), ("q", 3)], slab2(l, M_Q + 1))
                sl = slab2(l, M_KV)
                o, sig = claim((l, "k"))
                group(o, of(sl, 0), input_of(slice(0, 2)), KT, begins=True).then_inc(sig, 1)
                for c in range(2):
                    o, sig = claim((l, "v", c))
                    for tb in range(NB):
                        mm = group(o[:, tb * S:(tb + 1) * S], input_of(c, tb), of(sl, 0, 2 * P), KT)
                    mm.then_inc(sig, 1)
                for m in range(5):
                    taken((l, "k") if m == 0 else (l, "q", m - 1))
                    o, sig = claim((l, "hm", m))
                    n = 2 * S if m == 0 else w
                    pe.matmul(o[:, 0:n], headones, hsq2[m][:, 0:n], start=True, stop=True).then_inc(sig, 1)
                for j in range(2):
                    sl = slab2(l, M_VG + j)
                    for c in parts(l):
                        o, sig = claim((l, "vg", j, c))
                        for tb in range(NB):
                            mm = group(o[:, tb * S:(tb + 1) * S], input_of(c, tb), of(sl, 0, 2 * P), KT,
                                       begins=((c, tb) == (parts(l)[0], 0)))
                        mm.then_inc(sig, 1)
                two_tiles(l, [("u", 0), ("u", 1)], slab2(l, M_U))
                for m in range(3):
                    o, sig = claim((l, "rot", m))
                    pe.wait_ge(headed, 5 * l + (1, 3, 5)[m])
                    if m == 0:
                        mm = pe.matmul(o[:, 0:S], rot2, k2[:, S:2 * S], start=True, stop=True)
                    else:
                        mm = pe.matmul(o, rot2, q2[:, 2 * m - 2:2 * m, S:2 * S], start=True, stop=True)
                    mm.then_inc(sig, 1)
                two_tiles(l, [("u", 2), ("u", 3)], slab2(l, M_U + 1))
                units = UNITS2[l]
                base = L * NU1 + (len(UNITS2[0]) if l else 0)
                for i in range(len(units) + 3):
                    if i == 0:
                        taken((l, "v", 0), (l, "v", 1))
                        pe.wait_ge(roped, START + 4 * L + 3 * (l + 1))
                    if i < len(units):
                        kind, t, s, qb = units[i]
                        half = slice(64 * s, 64 * s + 64)
                        o, sig = claim((l, "S", i))
                        if kind == "ctx":
                            for n in range(NB):
                                mm = pe.matmul(o[:, n * S:(n + 1) * S], q2[half, t, n * P:(n + 1) * P], k2[half, 0:S],
                                               start=True, stop=True)
                        else:
                            mm = pe.matmul(o, q2[half, t, S + qb * P:S + (qb + 1) * P], k2[half, :],
                                           start=True, stop=True)
                        mm.then_inc(sig, 1)
                    if 8 <= i < 12:
                        g = i - 8
                        pe.wait_ge(levelled, (l + 1) * 4 if l == 0 else 4 + 2)
                        pe.wait_ge(ws_in, 16 * (l + 1))
                        o, sig = claim((l, "sp", g))
                        for c in parts(l):
                            for tb in range(NB):
                                d = c * NB + tb
                                mm = pe.matmul(o[:, d * P:(d + 1) * P], vg2[:, d, g * P:(g + 1) * P], ws2[:, g, :],
                                               start=True, stop=True)
                        mm.then_inc(sig, 1)
                    if 0 <= i - 2 < len(units):
                        u = i - 2
                        kind, t, s, qb = units[u]
                        o, sig = claim((l, "T", u))
                        pe.wait_ge(prob, base + u + 1)
                        for kt in range(4):
                            if kind == "ctx":
                                src, dst = (kt % 2) * S + (kt // 2) * P, (kt // 2) * S + (kt % 2) * P
                            else:
                                src = dst = kt * P
                            mm = pe.transpose(o[:, dst:dst + P], prob2[u % 4][:, src:src + P], ident)
                        mm.then_inc(sig, 1)
                    if 0 <= i - 3 < len(units):
                        u = i - 3
                        kind, t, s, qb = units[u]
                        half = slice(64 * s, 64 * s + 64)
                        y, first, last = Y2[l][u]
                        b, n = at2((l, "Y", y))
                        if first:
                            pe.wait_ge(drained[b], n)
                        taken((l, "T", u))
                        if kind == "ctx":
                            for kt in range(NB):
                                mm = pe.matmul(psum[half, b, 0:S], v2[:, kt, half], pt2[u % 2][:, kt * S:(kt + 1) * S],
                                               start=(kt == 0), stop=(kt == NB - 1))
                        else:
                            for kt in range(2 * NB):
                                mm = pe.matmul(psum[half, b, qb * P:(qb + 1) * P], v2[:, kt, half],
                                               pt2[u % 2][:, kt * P:(kt + 1) * P], start=(kt == 0), stop=(kt == 3))
                        if last:
                            mm.then_inc(full[b], 1)
                taken(*((l, "Y", y) for y in range(Y2[l][-1][0] + 1)))
                pe.wait_ge(gated_split, 4 * (l + 1))
                for j in range(4):
                    two_tiles(l, [("out", 2 * j), ("out", 2 * j + 1)], slab2(l, M_OUT + j))
                mean_squares(l, 1)
                spread_factors(l, 1)
                for half in range(2):
                    m0 = M_FF + 16 * half
                    with pe.Fori(0, 2) as i:
                        for j in range(4):
                            two_tiles(l, [("f1", 2 * j, half), ("f1", 2 * j + 1, half)], slab2(l, m0 + j, 2 * P, i), i,
                                      wait=(lambda k: input_ready(l, 1, k))
                                      if j == half == 0 else None)
                    hidden = [tiles(arena_r, rest * FT2 // 2 * w, FT2 // 2, w) for rest in range(2)]
                    with pe.Fori(0, 2) as i:
                        for j in range(4):
                            sl = slab2(l, m0 + 8 + j, P, i, FT2 // 2)
                            o, sig = claim((l, "f2", j, half), i)
                            wait = lambda k: pe.wait_ge(acted2, FT2 * l + FT2 // 2 * half + k + 1)
                            group(o[:, 0:w], of(sl, 0), [lambda k, t=t: t[:, k, :] for t in hidden], FT2 // 2,
                                  begins=True, wait=wait if j == 0 else None).then_inc(sig, 1)

        def stack2_scalar(act, prepare):
            def wait_full(name, i=0):
                b, n = at2(name, i)
                act.wait_ge(full[b], n + 1)
                return bank(b), drained[b]

            def ahead(l, m, i=0):
                m2 = SLABS2 * l + m + 2
                if m2 + (SLOTS * i if isinstance(i, int) else 0) < L * SLABS2:
                    round_slab(act, L, m2, i)

            def round_shifted(l, norm):
                now = parts(l, norm == 0)
                for t in range(KT):
                    if t < KT - 1:
                        act.wait_ge(modded, MODDED2[l, norm] + len(now) * (t + 1))
                    else:
                        b, n = at2((l, "bc", norm))
                        act.wait_ge(drained[b], n + 1)
                    for c in now:
                        e = act.activation(h_p[0][:, c, t, :], h_raw[:, c, t, :], ACT.Identity,
                                           bias=modulation(l, 3 * norm, t, c))
                    e.then_inc(h_rounded, 1)

            def root_of(l, norm):
                o, sig = wait_full((l, "ms", norm))
                c0 = 0 if len(parts(l, norm == 0)) == 2 else NB
                act.activation(small[:, c0:4], o[:, c0:4], ACT.Sqrt, bias=eps_c).then_inc(sig, 1)

            for t in range(KT):
                if t < KT - 1:
                    act.wait_ge(normed, 2 * L * (KT - 1) + t + 1)
                else:
                    b, n = at2("bc_f")
                    act.wait_ge(drained[b], n + 1)
                act.activation(sq2[:, 1, t, :], X2[:, 1, t, :], ACT.Square).then_inc(lat_squares, 1)
            act.wait_ge(ctx_in, 16)
            for t in range(KT):
                act.activation(sq2[:, 0, t, :], X2[:, 0, t, :], ACT.Square).then_inc(squared, 1)
            for l in range(L):
                now = slice(0, 2) if l == 0 else slice(1, 2)
                w = 2 * S if l == 0 else S
                root_of(l, 0)
                round_shifted(l, 0)
                for m in range(4):
                    if m % 2 == 0:
                        ahead(l, M_Q + m // 2)
                    o, sig = wait_full((l, "q", m))
                    act.activation(q2[:, m, 2 * S - w:2 * S], o[:, 0:w], ACT.Copy)
                    act.activation(hsq2[m + 1][:, 0:w], o[:, 0:w], ACT.Square).then_inc(sig, 1)
                ahead(l, M_KV)
                o, sig = wait_full((l, "k"))
                act.activation(k2, o, ACT.Copy)
                act.activation(hsq2[0], o, ACT.Square).then_inc(sig, 1)
                for m in range(5):
                    o, sig = wait_full((l, "hm", m))
                    n = 2 * S if m == 0 else w
                    act.activation(root2[m][:, 0:n], o[:, 0:n], ACT.Sqrt, bias=eps_c).then_inc(sig, 1)
                for j in range(2):
                    ahead(l, M_VG + j)
                    for c in parts(l):
                        o, sig = wait_full((l, "vg", j, c))
                        act.activation(vg2[:, NB * c:NB * (c + 1), 256 * j:256 * (j + 1)],
                                       o.rearrange("p (b c) -> p b c", b=NB), ACT.Gelu_apprx_tanh).then_inc(sig, 1)
                for m in range(4):
                    if m % 2 == 0:
                        ahead(l, M_U + m // 2)
                    if m == 2:
                        act.wait_ge(levelled_stats, l + 1)
                        g0 = 4 * NB * (2 - len(parts(l)))
                        var = aggr[:, :].rearrange("p (g two) -> p g two", two=2)[:, g0:16, 1]
                        act.activation(var, var, ACT.Sqrt, bias=eps_c).then_inc(spread_v, 1)
                    o, sig = wait_full((l, "u", m))
                    act.activation(u2[:, m, 2 * S - w:2 * S], o[:, 0:w], ACT.Gelu_apprx_tanh).then_inc(sig, 1)
                units = UNITS2[l]
                base = L * NU1 + (len(UNITS2[0]) if l else 0)
                for i in range(len(units) + 3):
                    if i < len(units):
                        kind, t, s, qb = units[i]
                        b, n = at2((l, "S", i))
                        c = 16 + 8 * (i % 4)
                        act.wait_ge(negmax, base + i + 1)
                        for n in range(NB if kind == "ctx" else 1):
                            qs = slice(n * S, (n + 1) * S) if kind == "ctx" else slice(0, 2 * S)
                            e = act.activation(prob2[i % 4][:, qs], bank(b)[:, qs], ACT.Exp, scale=HD_SCALE,
                                               bias=small[:, c + n:c + n + 1], accum_out=small[:, c + 2 + n:c + 3 + n])
                        e.then_inc(drained[b], 1)
                    if 0 <= i - 2 < len(units):
                        o, sig = wait_full((l, "T", i - 2))
                        act.activation(pt2[i % 2], o, ACT.Copy).then_inc(sig, 1)
                    if 0 <= i - 3 < len(units) and Y2[l][i - 3][2]:
                        kind, t, s, qb = units[i - 3]
                        o, sig = wait_full((l, "Y", Y2[l][i - 3][0]))
                        act.activation(h_p[0][:, 0 if kind == "ctx" else 1, t, :], o[:, 0:S],
                                       ACT.Copy).then_inc(y2_rounded, 1)
                    if 10 <= i < 14:
                        g = i - 10
                        act.wait_ge(gated2, 4 * l + g + 1)
                        act.activation(h_p[0][:, now, 4 + g, :], h_raw[:, now, 4 + g, :],
                                       ACT.Copy).then_inc(gated_rounded, 1)
                for m in range(KT):
                    if m == 6:
                        prepare()
                    if m % 2 == 0:
                        ahead(l, M_OUT + m // 2)
                    b, n = at2((l, "out", m))
                    act.wait_ge(drained[b], n + 1)
                    act.activation(sq2[:, now, m, :], X2[:, now, m, :], ACT.Square).then_inc(squared, 1)
                root_of(l, 1)
                round_shifted(l, 1)

                def hidden(i, half, j):
                    ahead(l, M_FF + 16 * half + j, i)
                    for m in range(2):
                        o, sig = wait_full((l, "f1", 2 * j + m, half), i)
                        act.nop()
                        act.activation(act_tile(arena, l, i, 2 * j + m, 1), o[:, 0:w].unsqueeze(1),
                                       ACT.Relu).then_inc(sig, 1)

                def square_tile(i, half, j):
                    if (half, i, j) == (1, 1, 3) and l < L - 1:
                        prepare()
                    ahead(l, M_FF + 16 * half + 8 + j, i)
                    if half == 1 and l < L - 1:
                        b, n = at2((l, "f2", j, half), i)
                        act.wait_ge(drained[b], n + 1)
                        act.nop()
                        for c in range(2):
                            e = act.activation(sq2[:, c, bass.ds(4 * i + j, 1), :], X2[:, c, bass.ds(4 * i + j, 1), :],
                                               ACT.Square)
                        e.then_inc(squared, 1)

                for half in range(2):
                    with act.Fori(0, 2) as i:
                        for j in range(4):
                            hidden(i, half, j)
                    if half == 1:
                        for i in range(2):
                            for j in range(4):
                                square_tile(i, half, j)
                    else:
                        with act.Fori(0, 2) as i:
                            for j in range(4):
                                square_tile(i, half, j)

        def stack2_gpsimd(pool, add_squares, split_in_place):
            def split_context(l, norm):
                for t in range(KT):
                    pool.wait_ge(h_rounded, 2 * L * KT + (2 * l + norm) * KT + t + 1)
                    raw = h_raw[:, 0, t, :]
                    pool.tensor_tensor(raw, raw, modulation(l, 3 * norm, t, 0).to_broadcast([P, S]),
                                       ALU.add).then_inc(ctx_shifted, 1)
                    pool.wait_ge(ctx_shifted, (2 * l + norm) * KT + t + 1)
                    pool.tensor_tensor(h_p[1][:, 0, t, :], raw, plain(h_p[0][:, 0, t, :]),
                                       ALU.subtract).then_inc(ctx_split, 1)

            def add(l, norm):
                now = slice(0, 2) if norm == 0 or l == 0 else slice(1, 2)
                n = 2 * l + norm
                if n == 0:
                    now = slice(0, 1)
                add_squares(2 * L + n + 1, lambda t: sq2[:, now, t, :], lambda t: 12 * L + 8 + 8 * n + t + 1)

            for l in range(L):
                w = 2 * S if l == 0 else S
                add(l, 0)
                split_context(l, 0)
                add(l, 1)
                if l == 0:
                    split_context(l, 1)
                for half in range(2):
                    with pool.Fori(0, 2) as i:
                        for m in range(8):
                            no = L * FT + FT2 * l + FT2 // 2 * half + 8 * i + m
                            b, n = at2((l, "f1", m, half), i)
                            pool.wait_ge(drained[b], n + 1)
                            pool.nop()
                            raw = act_tile(arena, l, i, m, 1)
                            pool.tensor_tensor(raw, raw, raw, ALU.mult).then_inc(pool_step, 1)
                            split_in_place(no, lambda: act_tile(arena_r, l, i, m, 0),
                                           lambda: act_tile(arena, l, i, m, 1),
                                           lambda: act_tile(arena_r, l, i, m, 1),
                                           lambda: arena_r[:, bass.ds(8 * w * i + w * m, w)].unsqueeze(1)
                                           ).then_inc(acted2, 1)

        def stack2_vector(vec):
            def wait_full(name, i=0):
                b, n = at2(name, i)
                vec.wait_ge(full[b], n + 1)
                return bank(b), drained[b]

            step = Steps(vec, vec_step, L * VEC_STEPS + 3 + 1)

            def ahead(l, m, i=0):
                m2 = SLABS2 * l + m + 2
                if m2 + (SLOTS * i if isinstance(i, int) else 0) < L * SLABS2:
                    split_slab(vec, L, m2, i)

            def modulated_norm(l, norm):
                now = parts(l, norm == 0)
                b, n = at2((l, "ms", norm))
                vec.wait_ge(drained[b], n + 1)
                c0 = 0 if len(now) == 2 else NB
                step.done(vec.reciprocal(small[:, c0:4], small[:, c0:4]))
                for d in range(c0, 4):
                    vec.tensor_scalar(diag[:, d * P:(d + 1) * P], ident, small[:, d:d + 1], None,
                                      ALU.mult).then_inc(diags, 1)
                o, sig = wait_full((l, "bc", norm))
                for t in range(KT + 1):
                    for c in now:
                        if t < KT:
                            e = vec.scalar_tensor_tensor(h_raw[:, c, t, :], X2[:, c, t, :], gain(l, norm, t, c),
                                                         o[:, c * S:(c + 1) * S], ALU.mult, ALU.mult)
                            e.then_inc(sig if (t, c) == (KT - 1, now[-1]) else modded, 1)
                    if t >= 1:
                        vec.wait_ge(h_rounded, 2 * L * KT + (2 * l + norm) * KT + t)
                        for c in now[-1:]:
                            e = vec.scalar_tensor_tensor(h_p[1][:, c, t - 1, :], h_raw[:, c, t - 1, :],
                                                         modulation(l, 3 * norm, t - 1, c), plain(h_p[0][:, c, t - 1, :]),
                                                         ALU.add, ALU.subtract)
                        e.then_inc(h_split, 1)

            for l in range(L):
                for norm in range(2):
                    c = (2 * l + norm) * 16
                    m0 = l * 2 * MT + (3 * norm + 1) * KT * 2
                    sc = mod[:, m0:m0 + 16].rearrange("p (t c) -> p t c", c=2)
                    g = uv[l][:, norm * KT:(norm + 1) * KT].unsqueeze(2).to_broadcast([P, KT, 2])
                    step.done(vec.scalar_tensor_tensor(gains2[:, c:c + 16].rearrange("p (t c) -> p t c", c=2), sc, 1.0,
                                                       g, ALU.add, ALU.mult))
            for t in range(1, KT):
                vec.wait_ge(lat_squares, t + 1)
                if t > 1:
                    vec.wait_ge(lat_summed, t - 1)
                vec.tensor_tensor(sq2[:, 1, 0, :], sq2[:, 1, 0, :], sq2[:, 1, t, :], ALU.add).then_inc(lat_summed, 1)
            for l in range(L):
                w = 2 * S if l == 0 else S
                now = slice(0, 2) if l == 0 else slice(1, 2)
                modulated_norm(l, 0)
                for m in range(M_KV + 1):
                    ahead(l, m)
                for c in range(2):
                    o, sig = wait_full((l, "v", c))
                    vec.tensor_copy(v2[:, NB * c:NB * (c + 1), :],
                                    o.rearrange("p (b c) -> p b c", b=NB)[:, :, P:2 * P]).then_inc(sig, 1)
                ahead(l, M_VG)
                for m in range(5):
                    b, n = at2((l, "hm", m))
                    vec.wait_ge(drained[b], n + 1)
                    dst = k2 if m == 0 else q2[:, m - 1, 2 * S - w:2 * S]
                    r = root2[m][:, 0:2 * S if m == 0 else w]
                    step.done(vec.reciprocal(r, r))
                    g = uv[l][:, 17:18] if m == 0 else uv[l][:, 16:17]
                    vec.scalar_tensor_tensor(dst, dst, g, r, ALU.mult, ALU.mult).then_inc(headed, 1)
                    if m == 1:
                        ahead(l, M_VG + 1)
                    if m == 3:
                        ahead(l, M_U)
                blocks = [c * NB + tb for c in parts(l) for tb in range(NB)]
                for d in blocks:
                    for j in range(2):
                        b, n = at2((l, "vg", j, d // NB))
                        vec.wait_ge(drained[b], n + 1)
                    for g in range(4):
                        j = 4 * d + g
                        e = vec.bn_stats(stats[:, 6 * j:6 * j + 6], vg2[:, d, g * P:(g + 1) * P])
                        if g == 3:
                            step.done(e)
                    for g in range(4):
                        j = 4 * d + g
                        e = vec.bn_aggr(aggr[:, 2 * j:2 * j + 2], stats[:, 6 * j:6 * j + 6])
                        if (d, g) == (blocks[-1], 3):
                            e.then_inc(levelled_stats, 1)
                for m in range(3):
                    vec.wait_ge(headed, 5 * l + (1, 3, 5)[m])
                    o, sig = wait_full((l, "rot", m))
                    if m == 0:
                        n, dst, ps = 1, k2[:, S:2 * S].unsqueeze(1), o[:, 0:S].unsqueeze(1)
                    else:
                        n, dst, ps = 2, q2[:, 2 * m - 2:2 * m, S:2 * S], o.rearrange("p (n w) -> p n w", w=S)
                    vec.wait_ge(roped, START + 4 * L + 3 * l + m)
                    t = tmp2[0][:, 0:n * S].rearrange("p (n w) -> p n w", w=S)
                    vec.tensor_tensor(t, ps, sin2.unsqueeze(1).to_broadcast([P, n, S]), ALU.mult).then_inc(sig, 1)
                    step.done(vec.tensor_tensor(dst, dst, cos2.unsqueeze(1).to_broadcast([P, n, S]), ALU.mult))
                    b, n = at2((l, "rot", m))
                    vec.wait_ge(drained[b], n + 1)
                    vec.tensor_tensor(dst, dst, t, ALU.add).then_inc(roped, 1)
                ahead(l, M_U + 1)

                def level_factors():
                    vec.wait_ge(spread_v, l + 1)
                    g0 = 4 * blocks[0]
                    var = aggr[:, :].rearrange("p (g two) -> p g two", two=2)[:, g0:16, 1]
                    step.done(vec.reciprocal(var, var))

                def level(d):
                    for g in range(4):
                        j = 4 * d + g
                        v = vg2[:, d, g * P:(g + 1) * P]
                        e = vec.tensor_scalar(v, v, aggr[:, 2 * j:2 * j + 1], aggr[:, 2 * j + 1:2 * j + 2],
                                              ALU.subtract, ALU.mult)
                    e.then_inc(levelled, 1)

                units = UNITS2[l]
                base = L * NU1 + (len(UNITS2[0]) if l else 0)
                for i in range(len(units) + 4):
                    if i < len(units):
                        kind, t, s, qb = units[i]
                        c = 16 + 8 * (i % 4)
                        o, sig = wait_full((l, "S", i))
                        n = NB if kind == "ctx" else 1
                        step.done(vec.tensor_reduce(small[:, c + 6:c + 6 + n], o.rearrange("p (n w) -> p n w", n=n),
                                                    axis=AX.X, op=ALU.max))
                        if i >= 4:
                            b, m = at2((l, "T", i - 4))
                            vec.wait_ge(full[b], m + 1)
                        vec.tensor_scalar(small[:, c:c + n], small[:, c + 6:c + 6 + n], -HD_SCALE, None,
                                          ALU.mult).then_inc(negmax, 1)
                    if 1 <= i <= len(units):
                        u = i - 1
                        kind, t, s, qb = units[u]
                        c = 16 + 8 * (u % 4)
                        n = NB if kind == "ctx" else 1
                        b, m = at2((l, "S", u))
                        vec.wait_ge(drained[b], m + 1)
                        step.done(vec.reciprocal(small[:, c + 2:c + 2 + n], small[:, c + 2:c + 2 + n]))
                        for m in range(n):
                            qs = slice(m * S, (m + 1) * S) if n == 2 else slice(0, 2 * S)
                            e = vec.tensor_scalar(prob2[u % 4][:, qs], prob2[u % 4][:, qs],
                                                  small[:, c + 2 + m:c + 3 + m], None, ALU.mult)
                        e.then_inc(prob, 1)
                    if i == 1:
                        level_factors()
                    if 2 <= i < 2 + len(blocks):
                        level(blocks[i - 2])
                    if 9 <= i < 13:
                        g = i - 9
                        o, sig = wait_full((l, "sp", g))
                        vec.wait_ge(ws_in, 16 * (l + 1))
                        lo = 2 * S - w
                        n = w // P
                        t = tmp2[g % 2][:, lo:2 * S].rearrange("p (n w) -> p n w", w=P)
                        vec.scalar_tensor_tensor(t, o[:, lo:2 * S].rearrange("p (n w) -> p n w", w=P),
                                                 uv[l][:, 18 + g:19 + g], bs2[:, g:g + 1, :].to_broadcast([P, n, P]),
                                                 ALU.mult, ALU.add).then_inc(sig, 1)
                        b, m = at2((l, "sp", g))
                        vec.wait_ge(drained[b], m + 1)
                        vec.tensor_tensor(h_raw[:, now, 4 + g, :], tmp2[g % 2][:, lo:2 * S].rearrange("p (n w) -> p n w", w=S),
                                          u2[:, g, lo:2 * S].rearrange("p (n w) -> p n w", w=S),
                                          ALU.mult).then_inc(gated2, 1)
                    if 11 <= i < 15:
                        g = i - 11
                        vec.wait_ge(gated_rounded, 4 * l + g + 1)
                        vec.tensor_tensor(h_p[1][:, now, 4 + g, :], h_raw[:, now, 4 + g, :], plain(h_p[0][:, now, 4 + g, :]),
                                          ALU.subtract).then_inc(gated_split, 1)
                    if i >= 4 and Y2[l][i - 4][2]:
                        kind, t, s, qb = units[i - 4]
                        y, c = Y2[l][i - 4][0], 0 if kind == "ctx" else 1
                        b, n = at2((l, "Y", y))
                        vec.wait_ge(y2_rounded, (Y2[0][-1][0] + 1) * l + y + 1)
                        vec.tensor_tensor(h_p[1][:, c, t, :], bank(b)[:, 0:S], plain(h_p[0][:, c, t, :]),
                                          ALU.subtract).then_inc(drained[b], 1)
                for m in range(KT):
                    if m % 2 == 0 and m < 6:
                        ahead(l, M_OUT + m // 2)
                    o, sig = wait_full((l, "out", m))
                    for c in parts(l):
                        ps = o[:, c * S:(c + 1) * S] if l == 0 else o[:, 0:S]
                        e = vec.scalar_tensor_tensor(X2[:, c, m, :], ps, modulation(l, 2, m, c), X2[:, c, m, :],
                                                     ALU.mult, ALU.add)
                    e.then_inc(sig, 1)
                ahead(l, M_FF - 1)
                modulated_norm(l, 1)

                def add_down(i, half, j):
                    if (half, i, j) != (1, 1, 3):
                        ahead(l, M_FF + 16 * half + 8 + j, i)
                    o, sig = wait_full((l, "f2", j, half), i)
                    for c in parts(l):
                        ps = o[:, c * S:(c + 1) * S] if l == 0 else o[:, 0:S]
                        x1 = X2[:, c, bass.ds(4 * i + j, 1), :]
                        m0 = l * 2 * MT + 5 * KT * 2 + c + 2 * j
                        e = vec.scalar_tensor_tensor(x1, ps.unsqueeze(1), mod[:, bass.ds(8 * i + m0, 1)], x1,
                                                     ALU.mult, ALU.add)
                    e.then_inc(sig, 1)

                for half in range(2):
                    with vec.Fori(0, 2) as i:
                        for j in range(4):
                            ahead(l, M_FF + 16 * half + j, i)
                    if half == 1:
                        for i in range(2):
                            for j in range(4):
                                add_down(i, half, j)
                    else:
                        with vec.Fori(0, 2) as i:
                            for j in range(4):
                                add_down(i, half, j)
                ahead(l, SLABS2 - 1)
        block = ctx.enter_context(nc.Block())

        @block.sync
        def _(sp):
            def load(l, m, src, i=0, n=None):
                sp.wait_ge(begun, slab_no(l, m, i) + 1)
                n = n or slab_size(m)
                sp.dma_start(in_slot(rests, m, n), src).then_inc(loaded[m % SLOTS], 16)

            def load_mod(l, f, h):
                sp.dma_start(spare[:, SLAB * h:SLAB * h + SLAB], a["w_mod"][l, 2 * f + h]).then_inc(mod_loaded[h], 16)

            sp.dma_start(X[:, KT * S:2 * KT * S], a["xT"]).then_inc(x_in, 16)
            sp.dma_start(con[:, :], a["const"]).then_inc(const_in, 16)
            sp.dma_start(csil[:, 0:2 * KT], a["condT"]).then_inc(cond_in, 16)
            sp.dma_start(mod[:, :], a["b_mod"]).then_inc(mod_in, 16)
            sp.dma_start(uvec[:, :], a["uvec"]).then_inc(fg_in, 16)
            with sp.Fori(0, L) as l:
                sp.wait_ge(drained[4], START + l * BANK1[4])
                sp.dma_start(vA[:, :], a["vecA"][l]).then_inc(va_in, 16)
                for m in range(N_UQ):
                    load(l, m, a["w_proj"][l, m])
                    if m == 8:
                        load_mod(l, 0, 0)
                        load_mod(l, 0, 1)
                    if m == 3:
                        sp.wait_ge(drained[7], START + l * BANK1[7])
                        sp.dma_start(vB[:, :], a["vecB"][l]).then_inc(vb_in, 16)
                for m in range(3):
                    load(l, N_UQ + m, a["w_uq"][l, m])
                load(l, N_UKV, a["w_ukv"][l])
                for m in range(3):
                    load(l, N_GATE + m, a["w_gate"][l, m])
                for f in range(1, NM):
                    sp.wait_ge(mod_half, NM * l + f)
                    load_mod(l, f, 0)
                    b, n = FILL1[("mod", f - 1)]
                    sp.wait_ge(full[b], START + l * BANK1[b] + n + 1)
                    load_mod(l, f, 1)
                load(l, N_GATE + 3, a["w_gate"][l, 3])
                with sp.Fori(0, 2) as i:
                    for j in range(4):
                        load(l, N_GATE + 4 + j, a["w_gate"][l, 4 * i + 4 + j], i)
                for m in range(6):
                    load(l, N_BR + m, a["w_br"][l, m])
                for m in range(4):
                    load(l, N_OUT + m, a["w_out"][l, m])
                with sp.Fori(0, FT // 4) as i:
                    for j in range(4):
                        load(l, N_UP + j, a["w_up"][l, 4 * i + j], i)
                for m in range(FT // 4 * 4, FT):
                    load(l, N_UP + m, a["w_up"][l, m])
                with sp.Fori(0, KT // 2) as i:
                    for j in range(4):
                        load(l, N_DOWN + j, a["w_down"][l, 4 * i + j], i)
            stack2_sync(sp, load)

        @block.tensor
        def _(pe):
            def claim(l, name, i=0):
                b, n = at1(l, name, i)
                pe.wait_ge(drained[b], n)
                return bank(b), full[b]

            def taken(l, *names):
                last = {}
                for name in names:
                    b, n = FILL1[name]
                    last[b] = max(last.get(b, 0), n + 1)
                for b, n in last.items():
                    pe.wait_ge(drained[b], START + l * BANK1[b] + n)

            def slab(l, m, width, i=0, nk=KT):
                pe.wait_ge(split, slab_no(l, m, i) + 1)
                return [in_slot(t, m, nk * width).rearrange("p (k c) -> p k c", c=width) for t in (highs_r, rests_r)]

            def group(o, a, b, nk, start=True, stop=True, begins=False, wait=None):
                for k in range(nk):
                    if wait:
                        wait(k)
                    ak, bk = [f(k) for f in a], [f(k) for f in b]
                    mm = pe.matmul(o, ak[0], bk[0], start=(start and k == 0), stop=False)
                    if begins and k == 0:
                        mm.then_inc(begun, 1)
                    pe.matmul(o, ak[0], bk[1], start=False, stop=False)
                    mm = pe.matmul(o, ak[1], bk[0], start=False, stop=(stop and k == nk - 1))
                return mm

            def two_groups(outs, a, b, nk, wait):
                last = []
                for k in range(nk):
                    wait(k)
                    bk = [f(k) for f in b]
                    for n, o in enumerate(outs):
                        ak = [f(k) for f in a[n]]
                        mm = pe.matmul(o, ak[0], bk[0], start=(k == 0), stop=False)
                        if k == 0 and n == 0:
                            mm.then_inc(begun, 1)
                        pe.matmul(o, ak[0], bk[1], start=False, stop=False)
                        mm = pe.matmul(o, ak[1], bk[0], start=False, stop=(k == nk - 1))
                        if k == nk - 1:
                            last.append(mm)
                return last

            def cols(w, c0, n=P):
                return [lambda k, t=t: t[:, k, c0:c0 + n] for t in w]

            def tokens(x, tb=None):
                c = slice(0, S) if tb is None else slice(tb * P, (tb + 1) * P)
                return [lambda k, t=t: t[:, k, c] for t in x]

            def channels(l, name, w, c0, n, x, nk=KT, begins=True, i=0, wait=None):
                o, sig = claim(l, name, i)
                for m in range(n):
                    mm = group(o[:, m * S:(m + 1) * S], cols(w, c0 + m * P), tokens(x), nk,
                               begins=(begins and m == 0), wait=wait if m == 0 else None)
                mm.then_inc(sig, 1)

            def by_token(l, name, w, c0, x, nk=KT, begins=True, n=2 * P):
                o, sig = claim(l, name)
                for tb in range(NB):
                    mm = group(o[:, tb * n:(tb + 1) * n], tokens(x, tb), cols(w, c0, n), nk, begins=(begins and tb == 0))
                mm.then_inc(sig, 1)

            def mean_squares(l, name, s, nt, col):
                o, sig = claim(l, name)
                for tb in range(NB):
                    for t in range(nt):
                        mm = pe.matmul(o[:, tb:tb + 1], s[:, t, tb * P:(tb + 1) * P], col,
                                       start=(t == 0), stop=(t == nt - 1))
                mm.then_inc(sig, 1)

            def spread(l, name, d0):
                o, sig = claim(l, name)
                for tb in range(NB):
                    mm = pe.matmul(o[:, tb * P:(tb + 1) * P], ones, diag[:, (d0 + tb) * P:(d0 + tb + 1) * P],
                                   start=True, stop=True)
                mm.then_inc(sig, 1)

            def rotate(l, name, src):
                o, sig = claim(l, name)
                pe.matmul(o, rot1, src, start=True, stop=True).then_inc(sig, 1)

            def modulate(l, f, half):
                pe.wait_ge(mod_loaded[half], 16 * (NM * l + f + 1))
                if half == 0:
                    o, sig = claim(l, ("mod", f))
                else:
                    o, sig = bank(FILL1[("mod", f)][0]), full[FILL1[("mod", f)][0]]
                for t in range(4):
                    mm = pe.matmul(o[32 * t:32 * t + 32, :], csil_wide[:, 4 * half + t, :], mod_slab[half][:, t, :],
                                   start=(half == 0), stop=(half == 1))
                mm.then_inc(sig if half == 1 else mod_half, 1)

            def pick_rows(l, f):
                taken(l, ("mod", f))
                o, sig = claim(l, ("pick", f))
                for m in range(4):
                    mm = pe.matmul(o[:, 2 * m:2 * m + 2], mod_parts[:, m * P:(m + 1) * P], pick, start=True, stop=True)
                mm.then_inc(sig, 1)

            pe.wait_ge(const_in, 16)
            pe.wait_ge(summed, KT - 1)
            mean_squares(0, "ms1", sq, 1, inv_d)
            with pe.Fori(0, L) as l:
                pe.wait_ge(diags, l * 8 + 2)
                spread(l, "bc1", 0)
                w = slab(l, 0, 2 * P)
                (o0, sig0), (o1, sig1) = claim(l, "cq0"), claim(l, "cq1")
                mm0, mm1 = two_groups((o0[:, 0:S], o1[:, 0:S]), (cols(w, 0), cols(w, P)), tokens(hl), KT,
                                      lambda k: pe.wait_ge(h_split, l * 2 * KT + k + 1))
                mm0.then_inc(sig0, 1)
                mm1.then_inc(sig1, 1)
                channels(l, "cq2gk", slab(l, 1, 2 * P), 0, 2, hl)
                channels(l, "ckv", slab(l, 2, 2 * P), 0, 2, hl)
                w = slab(l, 3, 2 * P)
                by_token(l, "gv", w, 0, hl)
                channels(l, "kr", w, P, 1, hl, begins=False)
                channels(l, "q0", slab(l, 4, 2 * P), 0, 2, hl)
                channels(l, "q1", slab(l, 5, 2 * P), 0, 2, hl)
                pe.wait_ge(lat_squared, 2 * l + 1)
                mean_squares(l, "ms_q", sq, QT, inv_q)
                pe.wait_ge(lat_squared, 2 * l + 2)
                mean_squares(l, "ms_kv", sq[:, QT:QT + KVT, :], KVT, inv_kv)
                channels(l, "k0", slab(l, 6, 2 * P), 0, 2, hl)
                channels(l, "k1", slab(l, 7, 2 * P), 0, 2, hl)
                taken(l, "cq2gk", "kr")
                rotate(l, "Rgk", arena[:, 4096:4608])
                pe.wait_ge(diags, l * 8 + 4)
                spread(l, "bc_q", 0)
                pe.wait_ge(diags, l * 8 + 6)
                spread(l, "bc_kv", 2)
                by_token(l, "v0", slab(l, 8, 2 * P), 0, hl)
                by_token(l, "v1", slab(l, 9, 2 * P), 0, hl)
                channels(l, "gq0", slab(l, 10, 2 * P), 0, 2, hl)
                channels(l, "gq1", slab(l, 11, 2 * P), 0, 2, hl)
                pe.wait_ge(lat_split, 2 * l + 1)
                for m, name in enumerate(("mqn0", "mqn1", "mqr")):
                    channels(l, name, slab(l, N_UQ + m, 2 * P, nk=QT), 0, 2, cq_p, QT)
                for j in range(2):
                    taken(l, f"gq{j}")
                    rotate(l, f"Rgq{j}", arena[:, 3072 + 512 * j:3584 + 512 * j])
                pe.wait_ge(lat_split, 2 * l + 2)
                w = slab(l, N_UKV, 1024, nk=KVT)
                channels(l, "mkn0", w, 0, 2, ckv_p, KVT)
                channels(l, "mkn1", w, 256, 2, ckv_p, KVT, begins=False)
                taken(l, "mqr")
                rotate(l, "Rmqr", arena[:, 7168:7680])
                for tb in range(NB):
                    o, sig = claim(l, f"mv{tb}")
                    group(o, tokens(ckv_p, tb), cols(w, 512, 512), KVT).then_inc(sig, 1)

                for i in range(NU1 + 3):
                    if i == 0:
                        taken(l, "q0", "q1", "k0", "k1", "v0", "v1")
                    if i == NA_HEADS:
                        taken(l, "gv")
                        pe.wait_ge(roped, START + 4 * l + 3)
                    if i == NA_HEADS + 8:
                        taken(l, "mqn0", "mqn1", "mkn0", "mkn1", "mv0", "mv1")
                        pe.wait_ge(roped, START + 4 * l + 4)
                    if i < NU1:
                        kind, h = UNITS1[i]
                        o, sig = claim(l, ("S", i))
                        half = slice(64 * (h % 2), 64 * (h % 2) + 64)
                        for qb in range(NB):
                            qs = slice(qb * P, (qb + 1) * P)
                            to = o[:, qb * S:(qb + 1) * S]
                            if kind == "na":
                                mm = pe.matmul(to, q_s[half, h // 2, qs], k_s[half, h // 2, :], start=True, stop=True)
                            elif kind == "gqa":
                                mm = pe.matmul(to, gq_s[half, h // 2, qs], gkr_s[half, 0, :], start=True, stop=True)
                            else:
                                pe.matmul(to, mq_s[:, h, qs], mk_s[:, h, :], start=True, stop=False)
                                mm = pe.matmul(to, mqr_s[half, h // 2, qs], gkr_s[half, 1, :], start=False, stop=True)
                        mm.then_inc(sig, 1)
                    if 0 <= i - 2 < NU1:
                        u = i - 2
                        o, sig = claim(l, ("T", u))
                        pe.wait_ge(prob, l * NU1 + u + 1)
                        for kt in range(NB):
                            for qb in range(NB):
                                mm = pe.transpose(o[:, kt * S + qb * P:kt * S + (qb + 1) * P],
                                                  prob_s[u % 4][:, qb * S + kt * P:qb * S + (kt + 1) * P], ident)
                        mm.then_inc(sig, 1)
                    if 0 <= i - 3 < NU1:
                        u = i - 3
                        kind, h = UNITS1[u]
                        b, n = at1(l, ("Y", u // 2))
                        if u % 2 == 0:
                            pe.wait_ge(drained[b], n)
                        taken(l, ("T", u))
                        for kt in range(NB):
                            pt = pt_s[u % 2][:, kt * S:(kt + 1) * S]
                            half = slice(64 * (h % 2), 64 * (h % 2) + 64)
                            if kind == "mla":
                                to, v = bank(b)[:, (h % 2) * S:(h % 2 + 1) * S], mv_s[:, kt, h * P:(h + 1) * P]
                            elif kind == "na":
                                to, v = psum[half, b, 0:S], v_s[:, kt, h * HD:(h + 1) * HD]
                            else:
                                to, v = psum[half, b, 0:S], gv_s[:, kt, half]
                            mm = pe.matmul(to, v, pt, start=(kt == 0), stop=(kt == NB - 1))
                        if u % 2 == 1:
                            mm.then_inc(full[b], 1)
                    if i == 0:
                        pe.wait_ge(cond, 1)
                    if i % 2 == 0 and i > 0:
                        pick_rows(l, i // 2 - 1)
                    modulate(l, i // 2, i % 2)
                modulate(l, NM - 1, 1)

                with pe.Fori(0, 3) as i:
                    for j in range(4):
                        channels(l, ("gate", j), slab(l, N_GATE + j, 2 * P, i), 0, 2, hl, i=i)
                pick_rows(l, NM - 1)
                for br in range(3):
                    taken(l, *(("Y", j) for j in ((0, 1, 2, 3), (4, 5, 6, 7), (8, 9))[br]))
                    for h in range(2):
                        w = slab(l, N_BR + 2 * br + h, 512, nk=4)
                        for f in range(2):
                            channels(l, ("br", br, 2 * h + f), w, 256 * f, 2, y_p[br], 4, begins=(f == 0))
                for f in range(4):
                    channels(l, ("out", f), slab(l, N_OUT + f, 2 * P), 0, 2, merged_p,
                             wait=(lambda k: pe.wait_ge(merged_split, 4 * l + k // 2 + 1)) if f == 0 else None)
                pe.wait_ge(summed, (2 * l + 2) * (KT - 1))
                mean_squares(l, "ms2", sq, 1, inv_d)
                pe.wait_ge(diags, l * 8 + 8)
                spread(l, "bc2", 0)

                def up(i, j):
                    wait = (lambda k: pe.wait_ge(h_split, (2 * l + 1) * KT + k + 1)) if j == 0 else None
                    channels(l, ("up", j), slab(l, N_UP + j, 2 * P, i), 0, 2, hl, i=i, wait=wait)

                with pe.Fori(0, FT // 4) as i:
                    for j in range(4):
                        up(i, j)
                for j in range(FT % 4):
                    up(FT // 4, j)
                with pe.Fori(0, KT // 2) as i:
                    for j in range(2):
                        o, sig = claim(l, ("down", j), i)
                        for h in range(2):
                            w = slab(l, N_DOWN + 2 * j + h, P, i, FT // 2)
                            x = [lambda k, t=t, h=h: t[:, h * (FT // 2) + k, :] for t in act_p]
                            wait = lambda k: pe.wait_ge(acted, 2 + l * FT + h * (FT // 2) + k + 1)
                            mm = group(o[:, 0:S], cols(w, 0), x, FT // 2, start=(h == 0), stop=(h == 1), begins=True,
                                       wait=wait if j == 0 else None)
                        mm.then_inc(sig, 1)
                pe.wait_ge(summed, (2 * l + 3) * (KT - 1))
                mean_squares(l + 1, "ms1", sq, 1, inv_d)
            pe.wait_ge(diags, 8 * L + 2)
            spread(L, "bc1", 0)
            stack2_tensor(pe, slab, group, two_groups)

        @block.scalar
        def _(act):
            def wait_full(l, name, i=0):
                b, n = at1(l, name, i)
                act.wait_ge(full[b], n + 1)
                return bank(b), drained[b]

            def take(l, name, dst, n=2 * S):
                o, sig = wait_full(l, name)
                act.activation(dst, o[:, 0:n], ACT.Copy).then_inc(sig, 1)

            def take_root(l, name, c):
                o, sig = wait_full(l, name)
                act.activation(small[:, c:c + 2], o[:, 0:2], ACT.Sqrt, bias=eps_c).then_inc(sig, 1)

            def prepare(function=ACT.Sqrt):
                act.activation(small[:, 112:113], eps_c, function)

            def round_ahead(l, m, i=0):
                round_slab(act, l, m + 2, i, slab_size(m + 2, i))

            def round_input(l, which, bc):
                for t in range(KT):
                    if t < KT - 1:
                        act.wait_ge(normed, (2 * l + which) * (KT - 1) + t + 1)
                    else:
                        b, n = at1(l, bc)
                        act.wait_ge(drained[b], n + 1)
                    act.activation(hl[0][:, t, :], hl_raw[:, t, :], ACT.Copy).then_inc(h_rounded, 1)

            act.wait_ge(x_in, 16)
            for t in range(KT):
                act.activation(sq[:, t, :], xl[:, t, :], ACT.Square).then_inc(squared, 1)
            act.wait_ge(cond_in, 16)
            act.activation(small[:, 96:112], csil[:, 0:16], ACT.Exp, scale=-1.0).then_inc(cond_exp, 1)
            act.wait_ge(const_in, 16)
            prepare()
            for m in range(2):
                round_slab(act, 0, m)
            with act.Fori(0, L) as l:
                take_root(l, "ms1", 0)
                round_input(l, 0, "bc1")
                round_ahead(l, 0)
                take(l, "cq0", arena[:, 4864:5120], S)
                take(l, "cq1", arena[:, 5120:5376], S)
                round_ahead(l, 1)
                round_ahead(l, 2)
                take(l, "ckv", arena[:, 5632:6144])
                for name in ("cq2gk", "cq0", "cq1"):
                    b, n = at1(l, name)
                    act.wait_ge(drained[b], n + 1)
                act.activation(X[:, 0:QT * S], arena[:, 4864:5632], ACT.Square).then_inc(lat_squared, 1)
                b, n = at1(l, "ckv")
                act.wait_ge(drained[b], n + 1)
                act.activation(X[:, QT * S:(QT + KVT) * S], arena[:, 5632:6144], ACT.Square).then_inc(lat_squared, 1)
                round_ahead(l, 3)
                take(l, "kr", arena[:, 4352:4608], S)
                round_ahead(l, 4)
                take(l, "q0", arena[:, 0:512])
                round_ahead(l, 5)
                take_root(l, "ms_q", 2)
                take_root(l, "ms_kv", 4)
                round_ahead(l, 6)
                take(l, "k0", arena[:, 1024:1536])
                round_ahead(l, 7)
                for name, (high, _low), raw in (("bc_q", cq_p, cq_s), ("bc_kv", ckv_p, ckv_s)):
                    b, n = at1(l, name)
                    act.wait_ge(drained[b], n + 1)
                    act.activation(high, raw, ACT.Copy).then_inc(lat_rounded, 1)
                round_ahead(l, 8)
                o, sig = wait_full(l, "v0")
                act.activation(v_s[:, :, 0:256], o.rearrange("p (b c) -> p b c", b=NB), ACT.Copy).then_inc(sig, 1)
                round_ahead(l, 9)
                round_ahead(l, 10)
                take(l, "gq0", arena[:, 3072:3584])
                round_ahead(l, 11)
                round_ahead(l, 12)
                take(l, "mqn0", arena[:, 6144:6656])
                round_ahead(l, 13)
                take(l, "mqn1", arena[:, 6656:7168])
                round_ahead(l, 14)
                take(l, "mqr", arena[:, 7168:7680])
                round_ahead(l, 15)
                prepare(ACT.Exp)
                take(l, "mkn0", arena[:, 7680:8192])
                take(l, "mkn1", arena[:, 8192:8704])
                take(l, "mv0", arena[:, 8704:9216])
                take(l, "mv1", arena[:, 9216:9728])
                for i in range(NU1 + 3):
                    if i % 2 == 0 and i > 0:
                        take(l, ("mod", i // 2 - 1), mod_parts)
                    if i < NU1:
                        kind, h = UNITS1[i]
                        c = 16 + 8 * (i % 4)
                        b, n = at1(l, ("S", i))
                        act.wait_ge(negmax, l * NU1 + i + 1)
                        if kind == "gqa":
                            act.activation(small[:, c + 4:c + 6], small[:, c:c + 2], ACT.Exp,
                                           bias=vA[:, V_SINK + h:V_SINK + h + 1])
                        for qb in range(NB):
                            qs = slice(qb * S, (qb + 1) * S)
                            src = bank(b)[:, qs] if kind == "mla" else prob_s[i % 4][:, qs]
                            e = act.activation(prob_s[i % 4][:, qs], src, ACT.Exp, bias=small[:, c + qb:c + qb + 1],
                                               scale=MLA_SCALE if kind == "mla" else 1.0,
                                               accum_out=small[:, c + 2 + qb:c + 3 + qb])
                        e.then_inc(drained[b] if kind == "mla" else exped, 1)
                    if 0 <= i - 2 < NU1:
                        take(l, ("T", i - 2), pt_s[i % 2])
                    if 0 <= i - 3 < NU1 and (i - 3) % 2 == 1:
                        at, w = y_place((i - 3) // 2)
                        o, _sig = wait_full(l, ("Y", (i - 3) // 2))
                        act.activation(arena_r[:, at:at + w], o[:, 0:w], ACT.Copy).then_inc(y_rounded, 1)
                take(l, ("mod", NM - 1), mod_parts)
                act.wait_ge(half_bias, l + 1)
                with act.Fori(0, 3) as i:
                    for f in range(4):
                        round_ahead(l, N_GATE + f, i)
                        o, sig = wait_full(l, ("gate", f), i)
                        act.nop()
                        for m in range(2):
                            g = gate_s[:, bass.ds(8 * i + 2 * f + m, 1), :]
                            e = act.activation(g, o[:, m * S:(m + 1) * S].unsqueeze(1), ACT.Tanh, scale=0.5,
                                               bias=derived[:, bass.ds(8 * i + 2 * f + m, 1)])
                        e.then_inc(sig, 1)
                for m in range(6):
                    round_ahead(l, N_BR + m)
                    for f in (2 * m - 8, 2 * m - 7):
                        if f >= 0:
                            act.wait_ge(merged_in, 4 * l + f + 1)
                            act.activation(arena_r[:, MERGED_HIGH + 512 * f:MERGED_HIGH + 512 * (f + 1)],
                                           arena[:, MERGED + 512 * f:MERGED + 512 * (f + 1)],
                                           ACT.Copy).then_inc(merged_rounded, 1)
                for f in range(4):
                    if f == 3:
                        prepare()
                    round_ahead(l, N_OUT + f)
                    b, n = at1(l, ("out", f))
                    act.wait_ge(drained[b], n + 1)
                    act.activation(X[:, f * 512:(f + 1) * 512], X[:, KT * S + f * 512:KT * S + (f + 1) * 512],
                                   ACT.Square).then_inc(squared, 1)
                take_root(l, "ms2", 6)
                round_input(l, 1, "bc2")
                act.wait_ge(vb_in, 16 * (l + 1))

                def middle_tap(i, j, last=False):
                    act.wait_ge(acted, l * FT + 4 * i + j + 1)
                    o, _s = wait_full(l, ("up", j), i)
                    act.nop()
                    for m in range(2):
                        ch = FT * m + 4 * i + j
                        e = act.activation(conv_s[j % 2][:, m, :], o[:, m * S:(m + 1) * S], ACT.Identity,
                                           scale=vB[:, bass.ds(V_W0 + 2 * FT + ch, 1)],
                                           bias=vB[:, bass.ds(V_CB + ch, 1)])
                    e.then_inc(tapped, 1)
                    if not last:
                        round_ahead(l, N_UP + j + 1, i)
                    b, n = at1(l, ("up", j), i)
                    act.wait_ge(drained[b], n + 1)
                    act.activation(gelu_s[j % 2], conv_s[j % 2][:, 1, :], ACT.Gelu_apprx_tanh).then_inc(gelued, 1)

                round_ahead(l, N_UP)
                with act.Fori(0, FT // 4 - 1) as i:
                    for j in range(4):
                        middle_tap(i, j)
                for t in range(FT // 4 * 4 - 4, FT):
                    middle_tap(t // 4, t % 4, last=(t == FT - 1))

                def square_tile(i, j):
                    b, n = at1(l, ("down", j), i)
                    act.wait_ge(drained[b], n + 1)
                    act.nop()
                    act.activation(sq[:, bass.ds(2 * i + j, 1), :], xl[:, bass.ds(2 * i + j, 1), :],
                                   ACT.Square).then_inc(squared, 1)

                with act.Fori(0, KT // 2 - 1) as i:
                    for j in range(4):
                        round_ahead(l, N_DOWN + j, i)
                        if j % 2 == 1:
                            square_tile(i, j // 2)
                for j in range(4):
                    if j == 3:
                        prepare()
                    round_ahead(l, SLABS1 - 4 + j)
                    if j % 2 == 1:
                        square_tile(KT // 2 - 1, j // 2)
            take_root(L, "ms1", 0)
            stack2_scalar(act, prepare)

        @block.gpsimd
        def _(pool):
            def add_squares(norm, s, arrived):
                for t in range(1, KT):
                    pool.wait_ge(squared, arrived(t))
                    if t > 1:
                        pool.wait_ge(summed, norm * (KT - 1) + t - 1)
                    pool.tensor_tensor(s(0), s(0), s(t), ALU.add).then_inc(summed, 1)

            def split_in_place(no, high, raw, low, high_again):
                pool.wait_ge(pool_step, 2 * no + 1)
                pool.nop()
                pool.tensor_copy(high(), raw()).then_inc(pool_step, 1)
                pool.wait_ge(pool_step, 2 * no + 2)
                pool.nop()
                return pool.tensor_tensor(low(), raw(), plain(high_again()), ALU.subtract)

            add_squares(0, lambda t: sq[:, t, :], lambda t: t + 1)
            pool.wait_ge(const_in, 16)
            with pool.Fori(0, L) as l:
                pool.wait_ge(drained[0], START + l * BANK1[0])
                pool.dma_start(H[:, 0:NA_HEADS * 512], a["na_bias"][l]).then_inc(bias_in, 16)
                pool.wait_ge(bias_in, 16 * (l + 1))
                pool.nop()
                for h in range(NA_HEADS):
                    for qb in range(NB):
                        b_ = H[:, h * 512 + qb * S:h * 512 + (qb + 1) * S]
                        pool.tensor_tensor(b_, b_, namask, ALU.add).then_inc(biased, 1)
                add_squares(2 * l + 1, lambda t: sq[:, t, :], lambda t: 12 * l + 8 + t // 2 + 1)

                with pool.Fori(0, FT // 2) as i:
                    for j in range(2):
                        no = l * FT + 2 * i + j
                        pool.wait_ge(gelued, no + 1)
                        pool.nop()
                        pool.tensor_tensor(act_raw[:, bass.ds(2 * i + j, 1), :], gelu_s[j].unsqueeze(1),
                                           conv_s[j][:, 0:1, :], ALU.mult).then_inc(pool_step, 1)
                        split_in_place(no, *(lambda t=t: t[:, bass.ds(2 * i + j, 1), :]
                                             for t in (act_p[0], act_raw, act_p[1])),
                                       lambda: arena_r[:, bass.ds(2 * S * i + S * j, S)].unsqueeze(1)).then_inc(acted, 1)
                add_squares(2 * l + 2, lambda t: sq[:, t, :], lambda t: 12 * l + 12 + t + 1)
            stack2_gpsimd(pool, add_squares, split_in_place)

        @block.vector
        def _(vec):
            def wait_full(l, name, i=0):
                b, n = at1(l, name, i)
                vec.wait_ge(full[b], n + 1)
                return bank(b), drained[b]

            def after_own(l, name, i=0):
                b, n = at1(l, name, i)
                vec.wait_ge(drained[b], n + 1)

            def take(l, name, dst, n=2 * S):
                o, sig = wait_full(l, name)
                vec.tensor_copy(dst, o[:, 0:n]).then_inc(sig, 1)

            def split_ahead(l, m, i=0):
                split_slab(vec, l, m + 2, i, slab_size(m + 2, i))

            def factors(l, name, c, d0, step):
                b, n = at1(l, name)
                vec.wait_ge(drained[b], n + 1)
                step.done(vec.reciprocal(small[:, c:c + 2], small[:, c:c + 2]))
                for tb in range(NB):
                    vec.tensor_scalar(diag[:, (d0 + tb) * P:(d0 + tb + 1) * P], ident, small[:, c + tb:c + tb + 1],
                                      None, ALU.mult).then_inc(diags, 1)

            def apply_norm(l, name, dst, src, gains, nt, each=None):
                o, sig = wait_full(l, name)
                for t in range(nt):
                    e = vec.scalar_tensor_tensor(dst[:, t, :], src[:, t, :], gains[:, t:t + 1], o[:, 0:S],
                                                 ALU.mult, ALU.mult)
                    if t < nt - 1 and each is not None:
                        e.then_inc(each, 1)
                e.then_inc(sig, 1)

            def normalised_input(l, which, name, gains):
                o, sig = wait_full(l, name)
                for t in range(KT + 1):
                    if t < KT:
                        vec.scalar_tensor_tensor(hl_raw[:, t, :], xl[:, t, :], gains[:, t:t + 1], o[:, 0:S],
                                                 ALU.mult, ALU.mult).then_inc(normed if t < KT - 1 else sig, 1)
                    if t >= 1:
                        vec.wait_ge(h_rounded, (2 * l + which) * KT + t)
                        vec.tensor_tensor(hl_low[:, t - 1, :], hl_raw[:, t - 1, :], plain(hl[0][:, t - 1, :]),
                                          ALU.subtract).then_inc(h_split, 1)

            def split_merged(l, f):
                vec.wait_ge(merged_rounded, 4 * l + f + 1)
                at, high = MERGED + f * 512, MERGED_HIGH + f * 512
                vec.tensor_tensor(arena_r[:, at:at + 512], arena[:, at:at + 512], plain(arena_r[:, high:high + 512]),
                                  ALU.subtract).then_inc(merged_split, 1)

            def rope(l, name, dst, step, nth):
                vec.wait_ge(roped, START + 4 * l + nth)
                o, sig = wait_full(l, name)
                wide = o.rearrange("p (n w) -> p n w", w=S)
                t = rope_tmp.rearrange("p (n w) -> p n w", w=S)
                vec.tensor_tensor(t, wide, sin1.unsqueeze(1).to_broadcast([P, 2, S]), ALU.mult).then_inc(sig, 1)
                step.done(vec.tensor_tensor(dst, dst, cos1.unsqueeze(1).to_broadcast([P, 2, S]), ALU.mult))
                after_own(l, name)
                vec.tensor_tensor(dst, dst, t, ALU.add).then_inc(roped, 1)

            def add_modulations(l, f):
                o, sig = wait_full(l, ("pick", f))
                m = mod[:, bass.ds(l * 2 * MT + 8 * f, 8)]
                vec.tensor_tensor(m, o[:, 0:8], m, ALU.add).then_inc(sig, 1)

            for s in (*full, *drained, roped):
                vec.sem_inc(s, START)
            vec.sem_inc(begun, SLOTS - 1)
            vec.sem_inc(acted, 2)
            vec.wait_ge(const_in, 16)
            vec.wait_ge(x_in, 16)
            vec.wait_ge(mod_in, 16)
            first = Steps(vec, vec_step)
            vec.wait_ge(cond_exp, 1)
            first.done(vec.tensor_scalar(small[:, 96:112], small[:, 96:112], 1.0, None, ALU.add))
            first.done(vec.reciprocal(small[:, 96:112], small[:, 96:112]))
            first.done(vec.memset(arena[:, 15872:15872 + KT * 32], 0.0))
            vec.tensor_tensor(csil_wide[:, :, 0:2], *(t.rearrange("p (k v) -> p k v", v=2)
                                                      for t in (csil[:, 0:16], small[:, 96:112])),
                              ALU.mult).then_inc(cond, 1)
            for m in range(2):
                split_slab(vec, 0, m)
            with vec.Fori(0, L) as l:
                step = Steps(vec, vec_step, l * VEC_STEPS + first.n)
                factors(l, "ms1", 0, 0, step)
                vec.wait_ge(va_in, 16 * (l + 1))
                normalised_input(l, 0, "bc1", vA[:, V_G1:V_G1 + KT])
                split_ahead(l, 0)
                split_ahead(l, 1)
                o, sig = wait_full(l, "cq2gk")
                step.done(vec.tensor_copy(arena[:, 5376:5632], o[:, 0:S]))
                vec.tensor_copy(arena[:, 4096:4352], o[:, S:2 * S]).then_inc(sig, 1)
                split_ahead(l, 2)
                split_ahead(l, 3)
                o, sig = wait_full(l, "gv")
                vec.tensor_copy(gv_s, o.rearrange("p (b c) -> p b c", b=NB)[:, :, 0:P]).then_inc(sig, 1)
                vec.tensor_scalar(derived[:, 0:3 * KT], vA[:, V_BG:V_BG + 3 * KT], 0.5, None,
                                  ALU.mult).then_inc(half_bias, 1)
                step.done(vec.tensor_scalar(derived[:, 32:40], vA[:, V_SINK:V_SINK + 8], -1.0, None, ALU.mult))
                split_ahead(l, 4)
                split_ahead(l, 5)
                take(l, "q1", arena[:, 512:1024])
                factors(l, "ms_q", 2, 0, step)
                factors(l, "ms_kv", 4, 2, step)
                split_ahead(l, 6)
                split_ahead(l, 7)
                take(l, "k1", arena[:, 1536:2048])
                b, n = at1(l, "kr")
                vec.wait_ge(drained[b], n + 1)
                rope(l, "Rgk", gkr_s, step, 0)
                apply_norm(l, "bc_q", cq_s, cq_s, vA[:, V_QA:V_QA + QT], QT)
                apply_norm(l, "bc_kv", ckv_s, ckv_s, vA[:, V_KVA:V_KVA + KVT], KVT)
                for nth, (at, n, high) in enumerate(((4864, QT * S, 9728), (5632, KVT * S, 9728 + QT * S))):
                    vec.wait_ge(lat_rounded, 2 * l + nth + 1)
                    vec.tensor_tensor(arena_r[:, at:at + n], arena[:, at:at + n], plain(arena_r[:, high:high + n]),
                                      ALU.subtract).then_inc(lat_split, 1)
                split_ahead(l, 8)
                split_ahead(l, 9)
                o, sig = wait_full(l, "v1")
                vec.tensor_copy(v_s[:, :, 256:512], o.rearrange("p (b c) -> p b c", b=NB)).then_inc(sig, 1)
                split_ahead(l, 10)
                split_ahead(l, 11)
                take(l, "gq1", arena[:, 3584:4096])
                split_ahead(l, 12)
                split_ahead(l, 13)
                split_ahead(l, 14)
                split_ahead(l, 15)
                b, n = at1(l, "gq0")
                vec.wait_ge(drained[b], n + 1)
                rope(l, "Rgq0", gq_s[:, 0:2, :], step, 1)
                after_own(l, "gq1")
                rope(l, "Rgq1", gq_s[:, 2:4, :], step, 2)

                for i in range(NU1 + 4):
                    if i % 2 == 1 and i > 1:
                        add_modulations(l, i // 2 - 1)
                    if i < NU1:
                        kind, h = UNITS1[i]
                        c = 16 + 8 * (i % 4)
                        o, sig = wait_full(l, ("S", i))
                        if i >= 4:
                            b, n = at1(l, ("T", i - 4))
                            vec.wait_ge(full[b], n + 1)
                        src = prob_s[i % 4]
                        if kind == "mla":
                            src = o
                        else:
                            if kind == "na":
                                vec.wait_ge(biased, 2 * (l * NA_HEADS + h + 1))
                            add = bias_s[:, h, :] if kind == "na" else winmask
                            vec.scalar_tensor_tensor(src, o, HD_SCALE, add, ALU.mult, ALU.add).then_inc(sig, 1)
                            after_own(l, ("S", i))
                        step.done(vec.tensor_reduce(small[:, c + 6:c + 8], src.rearrange("p (n w) -> p n w", w=S),
                                                    axis=AX.X, op=ALU.max))
                        if kind == "gqa":
                            e = vec.tensor_scalar(small[:, c:c + 2], small[:, c + 6:c + 8], -1.0,
                                                  derived[:, 32 + h:33 + h], ALU.mult, ALU.min)
                        else:
                            e = vec.tensor_scalar(small[:, c:c + 2], small[:, c + 6:c + 8],
                                                  -1.0 if kind == "na" else -MLA_SCALE, None, ALU.mult)
                        e.then_inc(negmax, 1)
                    if i == 1:
                        after_own(l, "mqr")
                        rope(l, "Rmqr", mqr_s, step, 3)
                    if 1 <= i <= NU1:
                        u = i - 1
                        kind, h = UNITS1[u]
                        c = 16 + 8 * (u % 4)
                        b, n = at1(l, ("S", u))
                        if kind == "mla":
                            vec.wait_ge(drained[b], n + 1)
                        else:
                            vec.wait_ge(exped, l * (NA_HEADS + 8) + u + 1)
                        if kind == "gqa":
                            step.done(vec.tensor_tensor(small[:, c + 2:c + 4], small[:, c + 2:c + 4],
                                                        small[:, c + 4:c + 6], ALU.add))
                        step.done(vec.reciprocal(small[:, c + 2:c + 4], small[:, c + 2:c + 4]))
                        for qb in range(NB):
                            qs = slice(qb * S, (qb + 1) * S)
                            e = vec.tensor_scalar(prob_s[u % 4][:, qs], prob_s[u % 4][:, qs],
                                                  small[:, c + 2 + qb:c + 3 + qb], None, ALU.mult)
                        e.then_inc(prob, 1)
                    if i >= 5 and i % 2 == 1:
                        j = (i - 5) // 2
                        at, w = y_place(j)
                        vec.wait_ge(y_rounded, l * (NU1 // 2) + j + 1)
                        b, n = FILL1[("Y", j)]
                        vec.tensor_tensor(arena_r[:, at + 1024:at + 1024 + w], bank(b)[:, 0:w], plain(arena_r[:, at:at + w]),
                                          ALU.subtract).then_inc(drained[b], 1)

                with vec.Fori(0, 3) as i:
                    for j in range(4):
                        split_ahead(l, N_GATE + j, i)
                add_modulations(l, NM - 1)
                b, n = at1(l, ("gate", 3))
                vec.wait_ge(drained[b], n + 3)
                for br in range(3):
                    for f in range(4):
                        if f % 2 == 0 and (br, f) != (2, 2):
                            split_ahead(l, N_BR + 2 * br + f // 2)
                        o, sig = wait_full(l, ("br", br, f))
                        g = arena[:, (KT * br + 2 * f) * S:(KT * br + 2 * f + 2) * S]
                        m = arena[:, MERGED + f * 512:MERGED + (f + 1) * 512]
                        t = m if br == 0 else tmp_s[f % 2]
                        vec.scalar_tensor_tensor(t, g, 1.0, o, ALU.add, ALU.mult).then_inc(sig, 1)
                        after_own(l, ("br", br, f))
                        if br == 1:
                            step.done(vec.tensor_tensor(m, m, t, ALU.add))
                        elif br == 2:
                            vec.tensor_tensor(m, m, t, ALU.add).then_inc(merged_in, 1)
                        if br == 2 and f > 0:
                            split_merged(l, f - 1)
                split_merged(l, 3)
                split_ahead(l, N_OUT - 1)
                for f in range(4):
                    if f < 3:
                        split_ahead(l, N_OUT + f)
                    o, sig = wait_full(l, ("out", f))
                    x2 = X[:, KT * S + f * 512:KT * S + (f + 1) * 512]
                    vec.scalar_tensor_tensor(x2, o, 0.5, x2, ALU.mult, ALU.add).then_inc(sig, 1)
                split_ahead(l, N_OUT + 3)
                vec.wait_ge(vb_in, 16 * (l + 1))
                factors(l, "ms2", 6, 0, step)
                normalised_input(l, 1, "bc2", vB[:, V_G2:V_G2 + KT])
                assert step.n == VEC_STEPS, step.n

                def outer_taps(i, j):
                    split_ahead(l, N_UP + j, i)
                    taps = Steps(vec, conv_step, (l * FT + 4 * i + j) * 3)
                    o, sig = wait_full(l, ("up", j), i)
                    vec.wait_ge(tapped, l * FT + 4 * i + j + 1)
                    for m in range(2):
                        ch = FT * m + 4 * i + j
                        w0, w2 = (vB[:, bass.ds(V_W0 + 2 * FT * k + ch, 1)] for k in (0, 2))
                        c = conv_s[j % 2][:, m, :]
                        ps = o[:, m * S:(m + 1) * S]
                        taps.done(vec.scalar_tensor_tensor(c[:, 1:S], ps[:, 0:S - 1], w0, c[:, 1:S],
                                                           ALU.mult, ALU.add))
                        e = vec.scalar_tensor_tensor(c[:, 0:S - 1], ps[:, 1:S], w2, c[:, 0:S - 1],
                                                     ALU.mult, ALU.add)
                        if m == 0:
                            taps.done(e)
                    e.then_inc(sig, 1)

                with vec.Fori(0, FT // 4) as i:
                    for j in range(4):
                        outer_taps(i, j)
                for j in range(FT % 4):
                    outer_taps(FT // 4, j)

                def add_down(i, j):
                    o, sig = wait_full(l, ("down", j), i)
                    x1 = xl[:, bass.ds(2 * i + j, 1), :]
                    vec.tensor_tensor(x1, o[:, 0:S].unsqueeze(1), x1, ALU.add).then_inc(sig, 1)

                with vec.Fori(0, KT // 2 - 1) as i:
                    for j in range(4):
                        split_ahead(l, N_DOWN + j, i)
                        if j % 2 == 1:
                            add_down(i, j // 2)
                for j in range(4):
                    if j < 3:
                        split_ahead(l, SLABS1 - 4 + j)
                    if j % 2 == 1:
                        add_down(KT // 2 - 1, j // 2)
                split_ahead(l, SLABS1 - 1)
            final = Steps(vec, vec_step, L * VEC_STEPS + first.n)
            factors(L, "ms1", 0, 0, final)
            vec.wait_ge(fg_in, 16)
            apply_norm(L, "bc1", xl, xl, uvec[:, 0:KT], KT, normed)
            stack2_vector(vec)


def layouts(inputs):
    i = {k: np.asarray(v) for k, v in inputs.items()}

    def slab(w):
        *lead, k, n = w.shape
        w = w.reshape(*lead, k // P, P, n)
        return np.ascontiguousarray(np.swapaxes(w, -3, -2)).reshape(*lead, P, (k // P) * n)

    def slabs(w, width):
        return np.stack([slab(w[:, :, c:c + width]) for c in range(0, w.shape[2], width)], axis=1)

    def columns(v):
        return np.swapaxes(v.reshape(*v.shape[:-1], -1, P), -1, -2)

    a = {}
    w = i["w_in"]
    q, k, v, cq, ckv, kr, gq, gkv, gate = np.split(
        w, np.cumsum([512, 512, 512, Q_RANK, KV_RANK, ROPE, 512, 256]).tolist(), axis=2)
    perm = np.arange(8).reshape(2, 4).T.ravel()
    gq = gq.reshape(L, D, 8, HD)[:, :, perm].reshape(L, D, 512)
    a["w_proj"] = slabs(np.concatenate([cq, gkv[..., :P], ckv, gkv[..., P:], kr, kr, q, k, v, gq], 2), 2 * P)
    a["w_gate"] = slabs(gate, 2 * P).reshape(L, 3, 4, P, SLAB)[:, [0, 2, 1]].reshape(L, 12, P, SLAB)
    uq = i["mla_w_uq"].reshape(L, Q_RANK, MLA_HEADS, NOPE + ROPE)
    a["w_uq"] = slabs(np.concatenate([uq[..., :NOPE].reshape(L, Q_RANK, -1),
                                      uq[..., NOPE:].reshape(L, Q_RANK, -1)], 2), 2 * P)
    ukv = i["mla_w_ukv"].reshape(L, KV_RANK, MLA_HEADS, NOPE + VD)
    a["w_ukv"] = slab(np.concatenate([ukv[..., :NOPE].reshape(L, KV_RANK, -1), ukv[..., NOPE:].reshape(L, KV_RANK, -1)], 2))
    brg = i["w_br_gqa"].reshape(L, 8, HD, D)[:, perm].reshape(L, 512, D)
    a["w_br"] = np.concatenate([slabs(x, 512) for x in (i["w_br_na"], brg, i["w_br_mla"])], axis=1)
    a["w_out"] = slabs(i["w_out"], 2 * P)
    up = i["w_up"].reshape(L, D, 2, FT, P).transpose(0, 1, 3, 2, 4).reshape(L, D, 2 * FF)
    a["w_up"] = slabs(up, 2 * P)
    a["w_down"] = np.swapaxes(slabs(i["w_down"], P).reshape(L, KT, P, 2, SLAB_DOWN), 2, 3).reshape(L, -1, P, SLAB_DOWN)
    a["w_mod"] = np.swapaxes(slabs(i["w_mod_2"], 512).reshape(L, NM, P, 2, SLAB), 2, 3).reshape(L, -1, P, SLAB)
    bg = columns(i["b_gate"])
    bg = bg.reshape(L, P, 3, KT)[:, :, [0, 2, 1]].reshape(L, P, 3 * KT)
    sink = np.broadcast_to(i["gqa_sink"][:, None, perm], (L, P, 8))
    a["vecA"] = np.concatenate([columns(i["norm1_g"]), bg, columns(i["mla_qa_g"]), columns(i["mla_kva_g"]), sink], 2)
    a["vecB"] = np.concatenate([columns(i["norm2_g"])] + [columns(i["conv_w"][:, t]) for t in range(3)]
                               + [columns(i["conv_b"])], 2)
    r, c = np.arange(S) // GRID, np.arange(S) % GRID
    rows = r[None, :] - r[:, None] + WIN_R - 1
    cols = np.clip(c[None, :] - c[:, None] + WIN_C - 1, 0, 2 * WIN_C - 2)
    bias = i["na_rpb"][:, :, rows, cols]
    a["na_bias"] = bias.reshape(L, NA_HEADS, NB, P, S).transpose(0, 3, 1, 2, 4).reshape(L, P, -1)
    a["xT"] = slab(i["x"][0].T)
    a["ctxT"] = slab(i["ctx_2"][0].T)
    a["condT"] = np.stack([columns(i["c_ctx_2"]), columns(i["c_2"][0])], -1).reshape(P, 2 * KT)
    bm = columns(i["b_mod_2"]).transpose(1, 0, 2)
    a["b_mod"] = np.stack([bm, bm], -1).reshape(P, -1)
    a["uvec"] = np.concatenate([columns(i["final_g"])] + [
        np.concatenate([columns(i["norm1_g_2"][l]), columns(i["norm2_g_2"][l]),
                        np.tile(i["q_norm_g_2"][l], 2)[:, None], np.tile(i["k_norm_g_2"][l], 2)[:, None],
                        columns(i["gmlp_norm_g_2"][l])], 1) for l in range(L)], 1)
    w = i["w_in_2"]
    q, k, v, u, vg = np.split(w, [512, 640, 768, 1280], axis=2)
    q = q.reshape(L, D, 8, HD)[:, :, perm].reshape(L, D, 512)
    a["w2_in"] = slabs(np.concatenate([q, k, v, vg, u], 2), 2 * P)
    wo = i["w_out_2"]
    wo = np.concatenate([wo[:, :512].reshape(L, 8, HD, D)[:, perm].reshape(L, 512, D), wo[:, 512:]], 1)
    a["w2_out"] = slabs(wo, 2 * P)
    ff1 = slabs(i["w_ff1_2"], 2 * P).reshape(L, 2, KT, P, SLAB)
    ff2 = slabs(i["w_ff2_2"], P).reshape(L, KT, P, 2, SLAB).transpose(0, 3, 1, 2, 4)
    a["w2_ff"] = np.stack([ff1, ff2], 2)
    ws = i["w_spatial_2"].transpose(0, 3, 1, 2).reshape(L, P, 4 * P)
    bs = np.broadcast_to(i["b_spatial_2"].reshape(L, 1, 4 * P), (L, P, 4 * P))
    a["spatial"] = np.concatenate([ws, bs], 2)
    a["const"] = constants()
    return {k: np.ascontiguousarray(v) for k, v in a.items()}


def constants():
    c = np.zeros((P, N_CONST), np.float32)
    p, s = np.arange(P), np.arange(S)
    c[:, C_ID:C_ID + P] = np.eye(P)
    c[:, C_ONE:C_ONE + P] = 1
    for at, h in ((C_ROT1, 32), (C_ROT2, 16)):
        for m in range(P):
            if m % (2 * h) < h:
                c[m + h, at + m] = -1
            else:
                c[m - h, at + m] = 1
    c[:, C_HEAD:C_HEAD + P] = (p[:, None] // HD == p[None, :] // HD) / HD
    f32 = np.float32
    inv = f32(1) / (f32(THETA) ** (np.arange(0, HD, 2, dtype=f32) / f32(HD)))
    ang = s.astype(f32)[None, :] * inv[p % 32][:, None]
    c[:, C_COS1:C_COS1 + S], c[:, C_SIN1:C_SIN1 + S] = np.cos(ang), np.sin(ang)
    n = HD // 4
    inv = f32(THETA) ** (-np.arange(n, dtype=f32) / f32(n))
    pos = np.where((p % HD < 32)[:, None], (s // GRID)[None, :], (s % GRID)[None, :]).astype(f32)
    ang = pos * inv[p % n][:, None]
    c[:, C_COS2:C_COS2 + S], c[:, C_SIN2:C_SIN2 + S] = np.cos(ang), np.sin(ang)
    for qb in range(NB):
        far = np.abs((qb * P + p)[:, None] - s[None, :]) > GQA_WINDOW
        c[:, C_WIN + qb * S:C_WIN + (qb + 1) * S] = np.where(far, NEG, 0)
    qc, kc = (p % GRID)[:, None], (s % GRID)[None, :]
    start = np.clip(qc - WIN_C // 2, 0, GRID - WIN_C)
    c[:, C_NA:C_NA + S] = np.where((kc >= start) & (kc < start + WIN_C), 0, NEG)
    c[:, C_INV], c[:, C_INV + 1], c[:, C_INV + 2], c[:, C_INV + 3] = 1 / D, 1 / Q_RANK, 1 / KV_RANK, EPS
    for v in range(2):
        c[v::32, C_PICK + v] = 1
    return c


def kernel(**inputs):
    import concourse.bacc as bacc
    from concourse.bass_utils import run_bass_kernel_spmd

    nc = bacc.Bacc("TRN2", target_bir_lowering=False, num_devices=1)
    arrays = layouts(inputs)
    aps = {k: nc.dram_tensor(f"in_{k}", v.shape, mybir.dt.float32, kind="ExternalInput").ap() for k, v in arrays.items()}
    out = nc.dram_tensor("out_xT", (P, KT * S), mybir.dt.float32, kind="ExternalOutput").ap()
    build(nc, aps, out)
    r = run_bass_kernel_spmd(nc, [{f"in_{k}": v for k, v in arrays.items()}], core_ids=[0])
    y = r.results[0]["out_xT"].reshape(P, KT, S)
    return np.ascontiguousarray(y.transpose(2, 1, 0).reshape(1, S, D))
```
